# Optimizing a Trainium2 kernel written in Bass

```python
import jax, jax.numpy as jnp
from jax import lax
import numpy as np

D_MODEL = 1024
BATCH = 1
SEQ = 512
DEPTH = 2
DEC_BATCH = 8
DEC_SEQ = 4
PAST_LEN = 512
PAGE_SIZE = 128

N_EVEN = (DEPTH + 1) // 2
N_ODD = DEPTH // 2

SSM_HEADS = 16
SSM_HEAD_DIM = 64
D_SSM = SSM_HEADS * SSM_HEAD_DIM
SSM_GROUPS = 2
D_STATE = 128
SSD_CONV = 4
SSD_CHUNK = 128
CONV_DIM = D_SSM + 2 * SSM_GROUPS * D_STATE
ATT_HEADS = 16
ATT_HEAD_DIM = 64
D_ATT = ATT_HEADS * ATT_HEAD_DIM
Q_BLOCK = 128
SB_SCALE = ATT_HEAD_DIM ** -0.5
SB_BIAS_INIT = -6.0
_S0 = D_SSM
_S1 = _S0 + CONV_DIM
_S2 = _S1 + SSM_HEADS
_S3 = _S2 + D_ATT
_S4 = _S3 + D_ATT
SPLIT_EVEN = (_S0, _S1, _S2, _S3, _S4)
IN_EVEN = _S4 + D_ATT
D_SC = D_MODEL
SC_WIDTH = 3
N_EXPERT_GROUPS = 4
EXPERTS_PER_GROUP = 8
N_EXPERTS = N_EXPERT_GROUPS * EXPERTS_PER_GROUP
TOP_K = 2
D_EXPERT = 256
RMS_EPS = 1e-6

kernel_name = "hybrid_ssd_stickbreak_shortconv_hmoe_step"

def rmsnorm(x, g):
    xf = x.astype(jnp.float32)
    y = xf * lax.rsqrt(jnp.mean(xf * xf, axis=-1, keepdims=True) + RMS_EPS)
    return (y * g.astype(jnp.float32)).astype(x.dtype)

def group_rmsnorm(y, g):
    shp = y.shape
    yg = y.reshape(shp[:-1] + (SSM_GROUPS, D_SSM // SSM_GROUPS))
    yg = yg * lax.rsqrt(jnp.mean(yg * yg, axis=-1, keepdims=True) + RMS_EPS)
    return yg.reshape(shp) * g.astype(jnp.float32)

def ada_modulation(c, w, b):
    mod = jax.nn.silu(c) @ w + b
    return jnp.split(mod[:, None, :], 6, axis=-1)

def modulate(h, shift, scale):
    return h * (1.0 + scale) + shift

def causal_dwconv(u, buf, w):
    width, length = w.shape[0], u.shape[1]
    up = jnp.concatenate([buf.astype(u.dtype), u], axis=1)
    out = up[:, :length] * w[0]
    for j in range(1, width):
        out = out + up[:, j:j + length] * w[j]
    return out, up[:, -(width - 1):]

def ssd_scan(x, dt, a, bmat, cmat, h0, chunk):
    f32 = jnp.float32
    bsz, length, nh, hp = x.shape
    ng, ns = bmat.shape[-2:]
    rep = nh // ng
    nc = length // chunk
    xr = x.astype(f32).reshape(bsz, nc, chunk, ng, rep, hp)
    dtr = dt.reshape(bsz, nc, chunk, ng, rep)
    br = bmat.astype(f32).reshape(bsz, nc, chunk, ng, ns)
    cr = cmat.astype(f32).reshape(bsz, nc, chunk, ng, ns)
    a_cum = jnp.cumsum(dtr * a.reshape(ng, rep), axis=2)
    xdt = xr * dtr[..., None]
    seg = a_cum[:, :, :, None] - a_cum[:, :, None, :]
    tri = jnp.tril(jnp.ones((chunk, chunk), bool))[:, :, None, None]
    decay = jnp.exp(jnp.where(tri, seg, -jnp.inf))
    cb = jnp.einsum('bclgn,bcsgn->bclsg', cr, br)
    y_diag = jnp.einsum('bclsgr,bcsgrp->bclgrp', cb[..., None] * decay, xdt)
    to_end = jnp.exp(a_cum[:, :, -1:] - a_cum)
    states = jnp.einsum('bclgn,bclgrp->bcgrpn', br, xdt * to_end[..., None])
    chunk_decay = jnp.exp(a_cum[:, :, -1])

    def step(h, inp):
        s_c, d_c = inp
        return h * d_c[..., None, None] + s_c, h

    h_final, h_prev = lax.scan(step, h0.astype(f32).reshape(bsz, ng, rep, hp, ns),
                               (jnp.moveaxis(states, 1, 0), jnp.moveaxis(chunk_decay, 1, 0)))
    h_prev = jnp.moveaxis(h_prev, 0, 1)
    y_off = jnp.einsum('bclgn,bcgrpn->bclgrp', cr, h_prev) * jnp.exp(a_cum)[..., None]
    y = (y_diag + y_off).reshape(bsz, length, nh, hp)
    return y, h_final.reshape(bsz, nh, hp, ns)

def _sb_block(q, k, v, q_pos, k_pos, bias):
    z = jnp.einsum('bqhd,bkhd->bhqk', q, k).astype(jnp.float32) * SB_SCALE \
        + bias.astype(jnp.float32)[None, :, None, None]
    causal = k_pos[None, :] < q_pos[:, None]
    log_beta = jax.nn.log_sigmoid(z)
    log_rest = jnp.where(causal, log_beta - z, 0.0)
    between = lax.cumsum(log_rest, axis=3, reverse=True) - log_rest
    w = jnp.where(causal, jnp.exp(log_beta + between), 0.0)
    return jnp.einsum('bhqk,bkhd->bqhd', w.astype(v.dtype), v)

def sb_attention(q, k, v, past, bias):
    bsz, length, nh, hd = q.shape
    qb = Q_BLOCK if length % Q_BLOCK == 0 else length
    nb = length // qb
    k_pos = jnp.arange(k.shape[1])
    q_blocks = jnp.moveaxis(q.reshape(bsz, nb, qb, nh, hd), 1, 0)
    q_pos = (past + jnp.arange(length)).reshape(nb, qb)
    out = lax.map(lambda a: _sb_block(a[0], k, v, a[1], k_pos, bias), (q_blocks, q_pos))
    return jnp.moveaxis(out, 0, 1).reshape(bsz, length, nh, hd)

def even_mixer(h, w_in, w_out, conv_w, conv_b, dt_bias, a_log, d_skip, norm_g, sb_bias, h0, conv_buf, k_past, v_past):
    f32 = jnp.float32
    bsz, length, _ = h.shape
    z, xbc, dt_raw, q, k, v = jnp.split(h @ w_in, SPLIT_EVEN, axis=-1)
    xbc, conv_new = causal_dwconv(xbc, conv_buf, conv_w)
    xbc = jax.nn.silu(xbc + conv_b)
    xs, bmat, cmat = jnp.split(xbc, (D_SSM, D_SSM + SSM_GROUPS * D_STATE), axis=-1)
    xs = xs.reshape(bsz, length, SSM_HEADS, SSM_HEAD_DIM)
    bmat = bmat.reshape(bsz, length, SSM_GROUPS, D_STATE)
    cmat = cmat.reshape(bsz, length, SSM_GROUPS, D_STATE)
    dt = jax.nn.softplus(dt_raw.astype(f32) + dt_bias.astype(f32))
    a = -jnp.exp(a_log.astype(f32))
    chunk = SSD_CHUNK if length % SSD_CHUNK == 0 else length
    y, h_new = ssd_scan(xs, dt, a, bmat, cmat, h0, chunk)
    y = y + xs.astype(f32) * d_skip.astype(f32)[:, None]
    y = y.reshape(bsz, length, D_SSM) * jax.nn.silu(z.astype(f32))
    y = group_rmsnorm(y, norm_g).astype(h.dtype)
    q = q.reshape(bsz, length, ATT_HEADS, ATT_HEAD_DIM)
    k = k.reshape(bsz, length, ATT_HEADS, ATT_HEAD_DIM)
    v = v.reshape(bsz, length, ATT_HEADS, ATT_HEAD_DIM)
    k_all = jnp.concatenate([k_past.astype(k.dtype), k], axis=1)
    v_all = jnp.concatenate([v_past.astype(v.dtype), v], axis=1)
    attn = sb_attention(q, k_all, v_all, k_past.shape[1], sb_bias)
    out = jnp.concatenate([y, attn.reshape(bsz, length, D_ATT)], axis=-1) @ w_out
    return out, h_new, conv_new, k, v

def odd_mixer(h, w_in, conv_w, w_out, conv_buf):
    b_gate, c_gate, u = jnp.split(h @ w_in, 3, axis=-1)
    conv, buf_new = causal_dwconv(c_gate * u, conv_buf, conv_w)
    return (b_gate * conv) @ w_out, buf_new

def hier_moe(h, w_group, b_group, w_router, b_router, w_gate, w_up, w_down):
    f32 = jnp.float32
    shp = h.shape
    t = h.reshape(-1, shp[-1])
    g_prob = jax.nn.softmax((t @ w_group + b_group).astype(f32), axis=-1)
    g_idx = jnp.argmax(g_prob, axis=-1)
    g_top = jnp.max(g_prob, axis=-1)
    e_logits = (t @ w_router + b_router).astype(f32).reshape(-1, N_EXPERT_GROUPS, EXPERTS_PER_GROUP)
    e_sel = jnp.einsum('tge,tg->te', e_logits, jax.nn.one_hot(g_idx, N_EXPERT_GROUPS, dtype=f32))
    top_p, top_i = lax.top_k(jax.nn.softmax(e_sel, axis=-1), TOP_K)
    wts = top_p / jnp.sum(top_p, axis=-1, keepdims=True) * g_top[:, None]
    expert_id = g_idx[:, None] * EXPERTS_PER_GROUP + top_i
    gates = jnp.einsum('tk,tke->te', wts, jax.nn.one_hot(expert_id, N_EXPERTS, dtype=f32))
    hg = jnp.einsum('td,edf->tef', t, w_gate)
    hu = jnp.einsum('td,edf->tef', t, w_up)
    hid = jax.nn.silu(hg) * hu * gates[:, :, None].astype(hg.dtype)
    out = jnp.einsum('tef,efd->td', hid, w_down)
    return out.astype(h.dtype).reshape(shp)

def setup_inputs(seed: int = 0) -> dict:
    key = jax.random.key(seed)
    ks = iter(jax.random.split(key, 40))
    f32 = jnp.float32

    def nrm(shape, scale=1.0):
        return jax.random.normal(next(ks), shape, f32) * scale

    def gain(shape):
        return 1.0 + nrm(shape, 0.02)

    n_pages = PAST_LEN // PAGE_SIZE
    n_used = DEC_BATCH * n_pages
    n_pool = n_used + n_used // 4
    d = D_MODEL
    x_prompt = nrm((BATCH, SEQ, d))
    x_sample = nrm((DEC_BATCH, DEC_SEQ, d))
    c_prompt = nrm((BATCH, d))
    c_sample = nrm((DEC_BATCH, d))
    state_ssm = nrm((N_EVEN, DEC_BATCH, SSM_HEADS, SSM_HEAD_DIM, D_STATE), 0.5)
    state_ssd_conv = nrm((N_EVEN, DEC_BATCH, SSD_CONV - 1, CONV_DIM))
    cache_k = nrm((N_EVEN, n_pool, PAGE_SIZE, ATT_HEADS, ATT_HEAD_DIM))
    cache_v = nrm((N_EVEN, n_pool, PAGE_SIZE, ATT_HEADS, ATT_HEAD_DIM))
    page_table = jax.random.permutation(next(ks), n_pool)[:n_used].reshape(DEC_BATCH, n_pages).astype(jnp.int32)
    state_short_conv = nrm((N_ODD, DEC_BATCH, SC_WIDTH - 1, D_SC))
    ada_w = nrm((DEPTH, d, 6 * d), 0.5 * d ** -0.5)
    ada_b = nrm((DEPTH, 6 * d), 0.02)
    ln_mix_g = gain((DEPTH, d))
    ln_ffn_g = gain((DEPTH, d))
    mix_w_in = nrm((N_EVEN, d, IN_EVEN), d ** -0.5)
    mix_w_out = nrm((N_EVEN, D_SSM + D_ATT, d), (D_SSM + D_ATT) ** -0.5)
    ssd_conv_w = nrm((N_EVEN, SSD_CONV, CONV_DIM), SSD_CONV ** -0.5)
    ssd_conv_b = nrm((N_EVEN, CONV_DIM), 0.02)
    dt0 = jnp.exp(jax.random.uniform(next(ks), (N_EVEN, SSM_HEADS), f32, np.log(1e-3), np.log(1e-1)))
    ssd_dt_bias = dt0 + jnp.log(-jnp.expm1(-dt0))
    ssd_a_log = jnp.log(jax.random.uniform(next(ks), (N_EVEN, SSM_HEADS), f32, 1.0, 16.0))
    ssd_d = 1.0 + nrm((N_EVEN, SSM_HEADS), 0.1)
    ssd_norm_g = gain((N_EVEN, D_SSM))
    sb_bias = SB_BIAS_INIT + nrm((N_EVEN, ATT_HEADS), 0.5)
    sc_w_in = nrm((N_ODD, d, 3 * D_SC), d ** -0.5)
    sc_conv_w = nrm((N_ODD, SC_WIDTH, D_SC), SC_WIDTH ** -0.5)
    sc_w_out = nrm((N_ODD, D_SC, d), D_SC ** -0.5)
    moe_w_group = nrm((DEPTH, d, N_EXPERT_GROUPS), d ** -0.5)
    moe_b_group = nrm((DEPTH, N_EXPERT_GROUPS), 0.01)
    moe_w_router = nrm((DEPTH, d, N_EXPERTS), d ** -0.5)
    moe_b_router = nrm((DEPTH, N_EXPERTS), 0.01)
    moe_w_gate = nrm((DEPTH, N_EXPERTS, d, D_EXPERT), d ** -0.5)
    moe_w_up = nrm((DEPTH, N_EXPERTS, d, D_EXPERT), d ** -0.5)
    moe_w_down = nrm((DEPTH, N_EXPERTS, D_EXPERT, d), D_EXPERT ** -0.5)
    final_g = gain((d,))
    return {"x_prompt": x_prompt, "x_sample": x_sample, "c_prompt": c_prompt, "c_sample": c_sample,
            "state_ssm": state_ssm, "state_ssd_conv": state_ssd_conv, "cache_k": cache_k, "cache_v": cache_v,
            "page_table": page_table, "state_short_conv": state_short_conv,
            "ada_w": ada_w, "ada_b": ada_b, "ln_mix_g": ln_mix_g, "ln_ffn_g": ln_ffn_g,
            "mix_w_in": mix_w_in, "mix_w_out": mix_w_out, "ssd_conv_w": ssd_conv_w, "ssd_conv_b": ssd_conv_b,
            "ssd_dt_bias": ssd_dt_bias, "ssd_a_log": ssd_a_log, "ssd_d": ssd_d, "ssd_norm_g": ssd_norm_g,
            "sb_bias": sb_bias,
            "sc_w_in": sc_w_in, "sc_conv_w": sc_conv_w, "sc_w_out": sc_w_out,
            "moe_w_group": moe_w_group, "moe_b_group": moe_b_group, "moe_w_router": moe_w_router,
            "moe_b_router": moe_b_router, "moe_w_gate": moe_w_gate, "moe_w_up": moe_w_up,
            "moe_w_down": moe_w_down, "final_g": final_g}

def reference(x_prompt, x_sample, c_prompt, c_sample, state_ssm, state_ssd_conv, cache_k, cache_v, page_table,
              state_short_conv, ada_w, ada_b, ln_mix_g, ln_ffn_g, mix_w_in, mix_w_out, ssd_conv_w, ssd_conv_b,
              ssd_dt_bias, ssd_a_log, ssd_d, ssd_norm_g, sb_bias, sc_w_in, sc_conv_w, sc_w_out, moe_w_group,
              moe_b_group, moe_w_router, moe_b_router, moe_w_gate, moe_w_up, moe_w_down, final_g):
    xp, xs = x_prompt, x_sample
    bp, bs = xp.shape[0], xs.shape[0]
    past_len = page_table.shape[1] * cache_k.shape[2]
    ssm_p, ssm_s, cv_p, cv_s, kp, ksm, vp, vsm, sc_p, sc_s = [], [], [], [], [], [], [], [], [], []
    for layer in range(DEPTH):
        mp = ada_modulation(c_prompt, ada_w[layer], ada_b[layer])
        ms = ada_modulation(c_sample, ada_w[layer], ada_b[layer])
        hp = modulate(rmsnorm(xp, ln_mix_g[layer]), mp[0], mp[1])
        hs = modulate(rmsnorm(xs, ln_mix_g[layer]), ms[0], ms[1])
        if layer % 2 == 0:
            i = layer // 2
            prm = (mix_w_in[i], mix_w_out[i], ssd_conv_w[i], ssd_conv_b[i], ssd_dt_bias[i], ssd_a_log[i],
                   ssd_d[i], ssd_norm_g[i], sb_bias[i])
            zero_h = jnp.zeros((bp, SSM_HEADS, SSM_HEAD_DIM, D_STATE), jnp.float32)
            zero_buf = jnp.zeros((bp, SSD_CONV - 1, CONV_DIM), xp.dtype)
            no_kv = jnp.zeros((bp, 0, ATT_HEADS, ATT_HEAD_DIM), xp.dtype)
            op, h_p, b_p, k_p, v_p = even_mixer(hp, *prm, zero_h, zero_buf, no_kv, no_kv)
            k_past = jnp.take(cache_k[i], page_table, axis=0).reshape(bs, past_len, ATT_HEADS, ATT_HEAD_DIM)
            v_past = jnp.take(cache_v[i], page_table, axis=0).reshape(bs, past_len, ATT_HEADS, ATT_HEAD_DIM)
            osm, h_s, b_s, k_s, v_s = even_mixer(hs, *prm, state_ssm[i], state_ssd_conv[i], k_past, v_past)
            ssm_p.append(h_p); ssm_s.append(h_s); cv_p.append(b_p); cv_s.append(b_s)
            kp.append(k_p); ksm.append(k_s); vp.append(v_p); vsm.append(v_s)
        else:
            i = layer // 2
            zero_buf = jnp.zeros((bp, SC_WIDTH - 1, D_SC), xp.dtype)
            op, b_p = odd_mixer(hp, sc_w_in[i], sc_conv_w[i], sc_w_out[i], zero_buf)
            osm, b_s = odd_mixer(hs, sc_w_in[i], sc_conv_w[i], sc_w_out[i], state_short_conv[i])
            sc_p.append(b_p); sc_s.append(b_s)
        xp = xp + mp[2] * op.astype(xp.dtype)
        xs = xs + ms[2] * osm.astype(xs.dtype)
        moe_prm = (moe_w_group[layer], moe_b_group[layer], moe_w_router[layer], moe_b_router[layer],
                   moe_w_gate[layer], moe_w_up[layer], moe_w_down[layer])
        xp = xp + mp[5] * hier_moe(modulate(rmsnorm(xp, ln_ffn_g[layer]), mp[3], mp[4]), *moe_prm)
        xs = xs + ms[5] * hier_moe(modulate(rmsnorm(xs, ln_ffn_g[layer]), ms[3], ms[4]), *moe_prm)
    y_prompt = rmsnorm(xp, final_g)
    y_sample = rmsnorm(xs, final_g)
    return (y_prompt, y_sample, jnp.stack(ssm_p), jnp.stack(ssm_s), jnp.stack(cv_p), jnp.stack(cv_s),
            jnp.stack(kp), jnp.stack(ksm), jnp.stack(vp), jnp.stack(vsm), jnp.stack(sc_p), jnp.stack(sc_s))


_drawn_inputs = setup_inputs


def setup_inputs(seed=0):
    import zlib

    import numpy as np

    out = dict(_drawn_inputs(seed))
    spreads = {}
    factors = {'cache_k': 2.859,
     'ln_ffn_g': 3.224,
     'ssd_norm_g': 5.715,
     'moe_b_group': 8.0,
     'final_g': 7.892,
     'moe_b_router': 2.839}
    for name, (base, spread) in spreads.items():
        noise = np.random.default_rng([zlib.crc32(name.encode()), seed]).standard_normal(out[name].shape)
        drawn = base * np.exp(spread * noise) if base else spread * noise
        out[name] = __import__('jax').numpy.asarray(drawn.astype(out[name].dtype))
    for name, factor in factors.items():
        out[name] = (out[name] * factor).astype(out[name].dtype)
    return out
```

```python
from contextlib import ExitStack

import concourse.bass as bass
from concourse import mybir

F32 = mybir.dt.float32
I32 = mybir.dt.int32
ALU = mybir.AluOpType
ACT = mybir.ActivationFunctionType
AX_X = mybir.AxisListType.X

P = 128
D = 1024
KT = D // P
TP = 512
NB, NQ = 8, 4
TS = NB * NQ
T = TP + TS
HALF = T // 2
TT = 5
TOK = [(i * P, P) for i in range(4)] + [(TP, TS)]
NC9 = 1 + NB
H, HD = 16, 64
NS = 128
XT = 12
PAGES, PAGE = 4, 128
POOL_PAGES = 40
NE, DE = 32, 256
CAP = 64
OVB = -(-((2 * T - 1) // CAP) // 4) * 4
NBLK = NE + OVB
MAXQ = (T - 1) // CAP
EPS = 1e-6
BIG = 1.0e6
NO_DECAY = -1.0e4

COLS = {}
_at = 0
for _name, _n in (("ada_b", 96), ("ln_mix", 16), ("ln_ffn", 16), ("final_g", 8), ("conv_w", 48), ("conv_b", 12),
                  ("d_skip", 8), ("norm_g", 8), ("sc_w", 24), ("dt_bias", 16), ("a_log", 16), ("sb_bias", 16),
                  ("router_b", 72)):
    COLS[_name] = (_at, _at + _n)
    _at += _n
N_SMALL = _at


class Chain:

    def __init__(self, eng, sem):
        self.eng, self.sem, self.n = eng, sem, 0

    def did(self, ins):
        ins.then_inc(self.sem, 1)
        self.n += 1
        return ins

    def settle(self):
        if self.n:
            self.eng.wait_ge(self.sem, self.n)

    def step(self, ins):
        self.did(ins)
        self.settle()


class Trunk:

    def __init__(self, nc, ctx, io):
        self.nc, self.ctx, self.io = nc, ctx, io
        self.phase_sems = []
        sb = self.sb
        self.xT = sb("xT", [P, KT, T])
        self.hT = sb("hT", [P, KT, T])
        self.mod = sb("mod", [P, 96, NC9])
        self.small = sb("small", [P, N_SMALL])
        self.ident = sb("ident", [P, P])
        self.ones = sb("ones", [P, P])
        self.neg_ones = sb("neg_ones", [P, P])
        self.neg_tri = sb("neg_tri", [P, P])
        self.tri_le = sb("tri_le", [P, P])
        self.tri_lt = sb("tri_lt", [P, P])
        self.same = sb("same", [TS, TS])
        self.tri_same = sb("tri_same", [TS, TS])
        self.member = sb("member", [TS, NB])
        self.w_ready = [self.sem(f"w_ready{b}") for b in range(2)]
        self.mm_done = [[self.sem(f"mm_done{b}{t}") for t in range(2)] for b in range(2)]
        self.ps_free = [[self.sem(f"ps_free{b}{t}") for t in range(2)] for b in range(2)]
        self.phase_sems = []
        self.rounds = 0

    def sb(self, name, shape, dt=F32, ctx=None):
        return (ctx or self.ctx).enter_context(self.nc.sbuf_tensor(name, shape, dt))

    def ps(self, name, shape, ctx):
        return ctx.enter_context(self.nc.psum_tensor(name, shape, F32))

    def sem(self, name):
        one = self.nc.alloc_semaphore(name=name)
        self.phase_sems.append(one)
        return one

    def recycle(self):
        self.nc.clear_and_free_semaphores(self.phase_sems)
        self.nc.all_engine_barrier()
        self.phase_sems = []

    def col(self, name, i, n=1):
        a = COLS[name][0] + i
        return self.small[:, a:a + n]

    def mod_tiles(self, layer, chunk):
        a = layer * 48 + chunk * KT
        return self.mod[:, a:a + KT, :]


def phase_constants(k):
    nc, io = k.nc, k.io
    cT = k.cT
    loaded, made, cond_ready = k.sem("loaded"), k.sem("made"), k.sem("cond_ready")
    zeroed, cleared = k.sem("zeroed"), k.sem("cleared")
    zero_rows = k.hT[:, :, :].rearrange("p k t -> p (k t)")[:, 0:D]
    with nc.Block() as block:
        @block.sync
        def _(sp):
            sp.dma_start(cT[:, :, :], io["cT"].rearrange("(k p) c -> p k c", p=P)).then_inc(loaded, 16)
            sp.dma_start(k.small[:, :], io["small"]).then_inc(loaded, 16)
            sp.dma_start(k.xT[:, :, :], io["xT"].rearrange("(k p) t -> p k t", p=P)).then_inc(loaded, 16)
            sp.wait_ge(loaded, 48)
            sp.wait_ge(zeroed, 1)
            for i in range(NE * CAP, NBLK * CAP, P):
                sp.dma_start(k.y_rows[i:i + P, :], zero_rows).then_inc(cleared, 16)
            sp.wait_ge(cleared, 16 * (OVB * CAP // P))

        @block.scalar
        def _(act):
            act.wait_ge(loaded, 48)
            nc.scalar.activation(cT[:, :, :], cT[:, :, :], ACT.Silu).then_inc(cond_ready, 1)
            act.wait_ge(cond_ready, 1)

        @block.vector
        def _(dve):
            nc.vector.memset(zero_rows, 0.0).then_inc(zeroed, 1)
            for b in range(2):
                for t in range(2):
                    dve.sem_inc(k.ps_free[b][t], 1)

        @block.gpsimd
        def _(pool):
            own = Chain(pool, made)
            own.did(nc.gpsimd.memset(k.ident[:, :], 0.0))
            own.did(nc.gpsimd.memset(k.ones[:, :], 1.0))
            own.did(nc.gpsimd.memset(k.neg_ones[:, :], -1.0))
            own.did(nc.gpsimd.memset(k.neg_tri[:, :], -1.0))
            own.did(nc.gpsimd.memset(k.tri_le[:, :], 1.0))
            own.did(nc.gpsimd.memset(k.tri_lt[:, :], 1.0))
            own.did(nc.gpsimd.memset(k.same[:, :], 1.0))
            own.did(nc.gpsimd.memset(k.member[:, :], 1.0))
            own.settle()

            def keep(m, pattern, base, mult, op, fill):
                own.did(nc.gpsimd.affine_select(out=m, in_=m, pattern=pattern, base=base, channel_multiplier=mult,
                                                compare_op=op, fill=fill))

            keep(k.ident[:, :], [[-1, P]], 0, 1, ALU.not_equal, 1.0)
            keep(k.neg_tri[:, :], [[-1, P]], 0, 1, ALU.is_ge, 0.0)
            keep(k.tri_le[:, :], [[1, P]], 0, -1, ALU.is_ge, 0.0)
            keep(k.tri_lt[:, :], [[1, P]], 0, -1, ALU.is_gt, 0.0)
            same = k.same[:, :].rearrange("j (b q) -> j b q", q=NQ)
            keep(same, [[-NQ, NB], [0, NQ]], 0, 1, ALU.is_ge, 0.0)
            keep(k.member[:, :], [[-NQ, NB]], 0, 1, ALU.is_ge, 0.0)
            own.settle()
            keep(same, [[NQ, NB], [0, NQ]], NQ - 1, -1, ALU.is_ge, 0.0)
            keep(k.member[:, :], [[NQ, NB]], NQ - 1, -1, ALU.is_ge, 0.0)
            own.settle()
            own.step(nc.gpsimd.tensor_tensor(k.tri_same[:, :], k.same[:, :], k.tri_le[0:TS, 0:TS], ALU.mult))


def phase_project(k, name, w, kt, steps, rhs, width, take_vector, take_scalar, vector_sem, scalar_sem):
    nc = k.nc
    halves = 1 if width <= 512 and width != T else 2
    cols = width // halves
    rounds = steps // 2
    base = k.rounds
    with ExitStack() as ctx:
        slots = [k.sb(f"{name}_w{b}", [P, kt, 256], ctx=ctx) for b in range(2)]
        ps = [[k.ps(f"{name}_ps{b}{t}", [P, 2, 512], ctx) for t in range(2)] for b in range(2)]
        w_view = w.rearrange("(k p) n -> p k n", p=P)

        with nc.Block() as block:
            @block.sync
            def _(sp):
                for b in range(2):
                    sp.dma_start(slots[b][:, :, :], w_view[:, :, b * 256:(b + 1) * 256]).then_inc(k.w_ready[b], 16)
                if rounds > 1:
                    with sp.Fori(0, rounds - 1) as i:
                        for b in range(2):
                            sp.wait_ge(k.mm_done[b][1], i + (base + 1))
                            sp.dma_start(slots[b][:, :, :], w_view[:, :, bass.ds(i * 512 + (512 + b * 256), 256)])\
                              .then_inc(k.w_ready[b], 16)

            @block.tensor
            def _(pe):
                with pe.Fori(0, rounds) as i:
                    for b in range(2):
                        pe.wait_ge(k.w_ready[b], i * 16 + 16 * (base + 1))
                        for t in range(2):
                            pe.wait_ge(k.ps_free[b][t], i + (base + 1))
                            for h in range(halves):
                                for j in range(kt):
                                    last = nc.tensor.matmul(ps[b][t][:, h, 0:cols], slots[b][:, j, t * P:(t + 1) * P],
                                                            rhs(j, h), start=(j == 0), stop=(j == kt - 1))
                            last.then_inc(k.mm_done[b][t], 1)

            @block.vector
            def _(dve):
                with dve.Fori(0, rounds) as i:
                    for b in range(2):
                        dve.wait_ge(k.mm_done[b][0], i + (base + 1))
                        take_vector(dve, i * 4 + 2 * b, ps[b][0][:, 0:halves, 0:cols], i * 2 + (b + 1))\
                            .then_inc(k.ps_free[b][0], 1)

            @block.scalar
            def _(act):
                with act.Fori(0, rounds) as i:
                    for b in range(2):
                        act.wait_ge(k.mm_done[b][1], i + (base + 1))
                        take_scalar(act, i * 4 + (2 * b + 1), ps[b][1][:, 0:halves, 0:cols], i * 2 + (b + 1))\
                            .then_inc(k.ps_free[b][1], 1)
    k.rounds += rounds


def by_half(dst):
    return dst.rearrange("p (h t) -> p h t", h=2)


def phase_ada(k, layer):
    nc = k.nc
    bias0 = COLS["ada_b"][0] + layer * 48

    def take_vector(dve, tile, ps, _):
        return nc.vector.tensor_scalar(k.mod[:, bass.ds(tile + layer * 48, 1), :], ps, k.small[:, bass.ds(tile + bias0, 1)],
                                       None, ALU.add)

    def take_scalar(act, tile, ps, _):
        return nc.scalar.activation(k.mod[:, bass.ds(tile + layer * 48, 1), :], ps, ACT.Identity,
                                    bias=k.small[:, bass.ds(tile + bias0, 1)])

    phase_project(k, f"ada{layer}", k.io["ada_w"][layer], KT, 24, lambda j, h: k.cT[:, j, :], NC9,
                  take_vector, take_scalar, None, None)
    folded = k.sem(f"folded{layer}")
    with nc.Block() as block:
        @block.vector
        def _(dve):
            for chunk, gain in ((1, "ln_mix"), (4, "ln_ffn")):
                s = k.mod_tiles(layer, chunk)
                g = k.col(gain, layer * KT, KT).unsqueeze(2).to_broadcast([P, KT, NC9])
                nc.vector.scalar_tensor_tensor(out=s, in0=s, scalar=1.0, in1=g, op0=ALU.add, op1=ALU.mult)\
                  .then_inc(folded, 1)
            dve.wait_ge(folded, 2)


def phase_norm(k, name, layer, chunk):
    nc = k.nc
    squared, summed, root, scaled = (k.sem(f"{name}_{s}") for s in ("squared", "summed", "root", "scaled"))
    root_in, own_d, own_a = (k.sem(f"{name}_{s}") for s in ("root_in", "own_d", "own_a"))
    with ExitStack() as ctx:
        sq = k.sb(f"{name}_sq", [P, 2, T], ctx=ctx)
        rstd = k.sb(f"{name}_rstd", [P, T], ctx=ctx)
        ps = k.ps(f"{name}_ps", [P, 2, 512], ctx)
        with nc.Block() as block:
            @block.scalar
            def _(act):
                for j in range(KT):
                    if j >= 2:
                        act.wait_ge(summed, j - 1)
                    nc.scalar.activation(sq[:, j % 2, :], k.xT[:, j, :], ACT.Square).then_inc(squared, 1)
                act.wait_ge(root_in, 1)
                nc.scalar.activation(rstd[:, :], rstd[:, :], ACT.Sqrt).then_inc(root, 1)
                for j in range(KT):
                    act.wait_ge(scaled, j + 1)
                    if layer is not None:
                        nc.scalar.activation(k.hT[:, j, 0:TP], k.hT[:, j, 0:TP], ACT.Identity,
                                             bias=k.mod[:, layer * 48 + chunk * KT + j, 0:1],
                                             scale=k.mod[:, layer * 48 + (chunk + 1) * KT + j, 0:1]).then_inc(own_a, 1)
                if layer is not None:
                    act.wait_ge(own_a, KT)

            @block.tensor
            def _(pe):
                for j in range(KT):
                    pe.wait_ge(squared, j + 1)
                    for h in range(2):
                        last = nc.tensor.matmul(ps[:, h, 0:HALF], k.ones[:, :], sq[:, j % 2, h * HALF:(h + 1) * HALF],
                                                start=(j == 0), stop=(j == KT - 1))
                    last.then_inc(summed, 1)

            @block.vector
            def _(dve):
                own = Chain(dve, own_d)
                dve.wait_ge(summed, KT)
                nc.vector.tensor_scalar(by_half(rstd[:, :]), ps[:, :, 0:HALF], 1.0 / D, EPS, ALU.mult, ALU.add)\
                  .then_inc(root_in, 1)
                dve.wait_ge(root, 1)
                own.step(nc.vector.reciprocal(rstd[:, :], rstd[:, :]))
                for j in range(KT):
                    if layer is None:
                        nc.vector.scalar_tensor_tensor(out=k.hT[:, j, :], in0=k.xT[:, j, :],
                                                       scalar=k.col("final_g", j), in1=rstd[:, :],
                                                       op0=ALU.mult, op1=ALU.mult).then_inc(scaled, 1)
                    else:
                        nc.vector.tensor_tensor(k.hT[:, j, :], k.xT[:, j, :], rstd[:, :], ALU.mult).then_inc(scaled, 1)
                dve.wait_ge(scaled, KT)
                if layer is not None:
                    hs = k.hT[:, :, TP:T].rearrange("p k (b q) -> p k b q", q=NQ)
                    a = k.mod_tiles(layer, chunk + 1)[:, :, 1:NC9].unsqueeze(3).to_broadcast([P, KT, NB, NQ])
                    s = k.mod_tiles(layer, chunk)[:, :, 1:NC9].unsqueeze(3).to_broadcast([P, KT, NB, NQ])
                    own.step(nc.vector.tensor_tensor(hs, hs, a, ALU.mult))
                    own.step(nc.vector.tensor_tensor(hs, hs, s, ALU.add))

            if layer is None:
                stored = k.sem("y_stored")

                @block.sync
                def _(sp):
                    y = k.io["yT"].rearrange("(k p) t -> p k t", p=P)
                    for j in range(KT):
                        sp.wait_ge(scaled, j + 1)
                        sp.dma_start(y[:, j, :], k.hT[:, j, :]).then_inc(stored, 16)
                    sp.wait_ge(stored, 16 * KT)


def phase_value(k, vtok):
    nc = k.nc
    ready, done, free, stored = k.sem("wv_ready"), k.sem("v_done"), k.sem("v_free"), k.sem("kv_stored")
    with ExitStack() as ctx:
        wv = k.sb("wv", [P, 2, KT, 512], ctx=ctx)
        ps = k.ps("v_ps", [P, 2, 512], ctx)
        w = k.io["mix_w_in"][:, 4624:5648].rearrange("(k p) n -> p k n", p=P)
        with nc.Block() as block:
            @block.sync
            def _(sp):
                for n in range(2):
                    sp.dma_start(wv[:, n, :, :], w[:, :, n * 512:(n + 1) * 512]).then_inc(ready, 16)
                    sp.wait_ge(ready, 16 * (n + 1))
                sp.dma_start(k.io["kT"], k.kT[:, :, :]).then_inc(stored, 16)
                for i, (a, m) in enumerate(TOK):
                    sp.wait_ge(free, 2 * (i + 1))
                    sp.dma_start(k.io["v"][a:a + m, :], vtok[0:m, i, :]).then_inc(stored, 16)
                sp.wait_ge(stored, 16 * (1 + TT))

            @block.tensor
            def _(pe):
                pe.wait_ge(ready, 32)
                for i, (a, m) in enumerate(TOK):
                    for n in range(2):
                        u = 2 * i + n
                        if u >= 2:
                            pe.wait_ge(free, u - 1)
                        for j in range(KT):
                            last = nc.tensor.matmul(ps[0:m, u % 2, :], k.hT[:, j, a:a + m], wv[:, n, j, :],
                                                    start=(j == 0), stop=(j == KT - 1))
                        last.then_inc(done, 1)

            @block.vector
            def _(dve):
                for i, (a, m) in enumerate(TOK):
                    for n in range(2):
                        u = 2 * i + n
                        dve.wait_ge(done, u + 1)
                        nc.vector.tensor_copy(vtok[0:m, i, n * 512:(n + 1) * 512], ps[0:m, u % 2, :]).then_inc(free, 1)


def phase_attention_prompt(k, vtok, mixT):
    nc = k.nc
    units = [(h, j) for h in range(H) for j in (3, 2, 1, 0)]
    NZ, NSP, NW, LAG = 6, 8, 4, 3
    names = ("z_done", "zb_done", "e_done", "l_done", "sp_done", "spm_done", "cum_done", "w_done", "wm_done",
             "pv_done", "o_done")
    s = {n: k.sem("ap_" + n) for n in names}
    with ExitStack() as ctx:
        zb = k.sb("ap_zb", [P, 3, 512], ctx=ctx)
        sp_t = k.sb("ap_sp", [P, NSP, 512], ctx=ctx)
        w_t = k.sb("ap_w", [P, NW, 512], ctx=ctx)
        z_ps = [k.ps(f"ap_z{i}", [P, 512], ctx) for i in range(NZ)]
        o_ps = [k.ps(f"ap_o{i}", [P, 512], ctx) for i in range(2)]
        n_units = len(units)

        with nc.Block() as block:
            @block.tensor
            def _(pe):
                def scores(u):
                    h, j = units[u]
                    r = slice(64 * (h % 2), 64 * (h % 2) + 64)
                    if u >= NZ:
                        pe.wait_ge(s["w_done"], u - NZ + 1)
                    nc.tensor.matmul(z_ps[u % NZ][:, j * P:512], k.kT[r, h // 2, j * P:(j + 1) * P],
                                     k.qT[r, h // 2, j * P:TP], start=True, stop=False, skip_group_check=True)\
                      .then_inc(s["z_done"], 1)

                def cumulate(u):
                    h, j = units[u]
                    pe.wait_ge(s["spm_done"], u + 1)
                    z = z_ps[u % NZ]
                    last = nc.tensor.matmul(z[:, j * P:512], k.neg_tri[:, :], sp_t[:, u % NSP, j * P:512],
                                            start=False, stop=(j == 3), skip_group_check=True)
                    for back in range(1, 4 - j):
                        jj = j + back
                        last = nc.tensor.matmul(z[:, jj * P:512], k.neg_ones[:, :],
                                                sp_t[:, (u - back) % NSP, jj * P:512],
                                                start=False, stop=(jj == 3), skip_group_check=True)
                    last.then_inc(s["cum_done"], 1)

                def values(u):
                    h, j = units[u]
                    r = slice(64 * (h % 2), 64 * (h % 2) + 64)
                    pe.wait_ge(s["wm_done"], u + 1)
                    if j == 3 and h % 2 == 0 and h >= 4:
                        pe.wait_ge(s["o_done"], h // 2 - 1)
                    nc.tensor.matmul(o_ps[(h // 2) % 2][r, j * P:512], vtok[:, j, h * HD:(h + 1) * HD],
                                     w_t[:, u % NW, j * P:512], start=(j == 3), stop=(j == 0), skip_group_check=True)\
                      .then_inc(s["pv_done"], 1)

                for u in range(n_units + LAG + 2):
                    if u < n_units:
                        scores(u)
                    if LAG <= u < n_units + LAG:
                        cumulate(u - LAG)
                    if u >= LAG + 2:
                        values(u - LAG - 2)

            @block.vector
            def _(dve):
                def bounded(u):
                    h, j = units[u]
                    dve.wait_ge(s["z_done"], u + 1)
                    if u >= 3:
                        dve.wait_ge(s["e_done"], u - 2)
                    nc.vector.tensor_scalar(zb[:, u % 3, j * P:512], z_ps[u % NZ][:, j * P:512],
                                            k.col("sb_bias", h), 40.0, ALU.add, ALU.min).then_inc(s["zb_done"], 1)

                def softplus(u):
                    h, j = units[u]
                    dve.wait_ge(s["l_done"], u + 1)
                    nc.vector.scalar_tensor_tensor(out=sp_t[:, u % NSP, j * P:512], in0=z_ps[u % NZ][:, j * P:512],
                                                   scalar=k.col("sb_bias", h), in1=sp_t[:, u % NSP, j * P:512],
                                                   op0=ALU.add, op1=ALU.max).then_inc(s["sp_done"], 1)

                def output(pair):
                    dve.wait_ge(s["pv_done"], 8 * (pair + 1))
                    nc.vector.tensor_copy(mixT[:, KT + pair, 0:TP], o_ps[pair % 2][:, :]).then_inc(s["o_done"], 1)

                for u in range(n_units + 1):
                    if u < n_units:
                        bounded(u)
                    if u >= 1:
                        softplus(u - 1)
                    if u >= 14 and (u - 14) % 8 == 0:
                        output((u - 14) // 8)
                for pair in range((n_units - 14) // 8 + 1, H // 2):
                    output(pair)
                dve.wait_ge(s["o_done"], H // 2)

            @block.scalar
            def _(act):
                def exponential(u):
                    h, j = units[u]
                    act.wait_ge(s["zb_done"], u + 1)
                    if u >= NSP:
                        act.wait_ge(s["cum_done"], (u - NSP) // 4 * 4 + 4)
                    nc.scalar.activation(sp_t[:, u % NSP, j * P:512], zb[:, u % 3, j * P:512], ACT.Exp)\
                      .then_inc(s["e_done"], 1)
                    act.wait_ge(s["e_done"], u + 1)
                    nc.scalar.activation(sp_t[:, u % NSP, j * P:512], sp_t[:, u % NSP, j * P:512], ACT.Ln, bias=1.0)\
                      .then_inc(s["l_done"], 1)

                def weights(u):
                    h, j = units[u]
                    act.wait_ge(s["cum_done"], u + 1)
                    if u >= NW:
                        act.wait_ge(s["pv_done"], u - NW + 1)
                    nc.scalar.activation(w_t[:, u % NW, j * P:512], z_ps[u % NZ][:, j * P:512], ACT.Exp,
                                         bias=k.col("sb_bias", h)).then_inc(s["w_done"], 1)

                for u in range(n_units + LAG):
                    if u < n_units:
                        exponential(u)
                    if u >= LAG:
                        weights(u - LAG)

            @block.gpsimd
            def _(pool):
                def mask(tile, buf, ready, done, u):
                    h, j = units[u]
                    pool.wait_ge(ready, u + 1)
                    d = tile[:, buf, j * P:(j + 1) * P]
                    nc.gpsimd.affine_select(out=d, in_=d, pattern=[[1, P]], base=0, channel_multiplier=-1,
                                            compare_op=ALU.is_gt, fill=0.0).then_inc(done, 1)

                for u in range(n_units + LAG):
                    if u < n_units:
                        mask(sp_t, u % NSP, s["sp_done"], s["spm_done"], u)
                    if u >= LAG:
                        mask(w_t, (u - LAG) % NW, s["w_done"], s["wm_done"], u - LAG)


def phase_attention_sample(k, mixT):
    nc = k.nc
    RING = 3
    names = ("page_ready", "q_made", "kz_done", "zb_done", "e_done", "l_done", "sp_done", "m_done", "cum_done",
             "wz_done", "w_done", "wm_done", "pv_done", "o_done", "pt_ready", "q_zero")
    s = {n: k.sem("as_" + n) for n in names if n != "page_ready"}
    arrived = [k.sem(f"as_page{r}") for r in range(RING)]
    C = NB * H * NQ
    with ExitStack() as ctx:
        pages = k.sb("as_pages", [P, RING, PAGES + 1, D], ctx=ctx)
        table = k.sb("as_table", [1, NB * PAGES], I32, ctx=ctx)
        qd = k.sb("as_qd", [P, KT, NB, 2, NQ], ctx=ctx)
        zb = k.sb("as_zb", [P, 2, C], ctx=ctx)
        sp_t = k.sb("as_sp", [P, PAGES, C], ctx=ctx)
        sp_n = k.sb("as_spn", [NQ, C], ctx=ctx)
        zb_n = k.sb("as_zbn", [NQ, C], ctx=ctx)
        z_ps = [k.ps(f"as_z{i}", [P, C], ctx) for i in range(PAGES)]
        zn_ps = k.ps("as_zn", [P, C], ctx)
        o_ps = k.ps("as_o", [P, KT, NB, 2, NQ], ctx)

        def bias(m):
            b = COLS["sb_bias"][0]
            return k.small[0:m, b:b + H].unsqueeze(1).unsqueeze(3).to_broadcast([m, NB, H, NQ])

        def all_of(n):
            return sum(16 * (PAGES + (m >= NB)) for m in range(n % RING, n + 1, RING))

        def grid(t):
            return t.rearrange("p (b h q) -> p b h q", b=NB, h=H)

        with nc.Block() as block:
            @block.sync
            def _(sp):
                sp.dma_start(table[:, :], k.io["page_table"]).then_inc(s["pt_ready"], 16)
                sp.wait_ge(s["pt_ready"], 16)
                for n in range(2 * NB):
                    b = n % NB
                    if n >= RING:
                        m = n - RING
                        if m < NB:
                            sp.wait_ge(s["kz_done"], m + 1)
                        else:
                            sp.wait_ge(s["pv_done"], m - NB + 1)
                    for p in range(PAGES):
                        page = sp.value_load(table[0:1, b * PAGES + p:b * PAGES + p + 1], min_val=0, max_val=POOL_PAGES - 1)
                        src = k.io["cache_kT"] if n < NB else k.io["cache_v"]
                        sp.dma_start(pages[:, n % RING, p, :], src[bass.ds(page, 1), :, :].rearrange("a p n -> p (a n)"))\
                          .then_inc(arrived[n % RING], 16)
                    if n >= NB:
                        sp.dma_start(pages[0:NQ, n % RING, PAGES, :], k.io["v"][TP + NQ * b:TP + NQ * (b + 1), :])\
                          .then_inc(arrived[n % RING], 16)

            @block.tensor
            def _(pe):
                pe.wait_ge(s["q_made"], 2)
                for b in range(NB):
                    pe.wait_ge(arrived[b % RING], all_of(b))
                    for p in range(PAGES):
                        for j in range(KT):
                            c = b * 64 + j * 8
                            last = nc.tensor.matmul(z_ps[p][:, c:c + 8], pages[:, b % RING, p, j * P:(j + 1) * P],
                                                    qd[:, j, b, :, :], start=(b == 0 and j == 0), stop=False,
                                                    skip_group_check=True)
                    last.then_inc(s["kz_done"], 1)
                for b in range(NB):
                    for j in range(KT):
                        c = b * 64 + j * 8
                        last = nc.tensor.matmul(zn_ps[0:NQ, c:c + 8], k.kT[:, j, TP + NQ * b:TP + NQ * (b + 1)],
                                                qd[:, j, b, :, :], start=(b == 0 and j == 0), stop=False,
                                                skip_group_check=True)
                last.then_inc(s["kz_done"], 1)
                pe.wait_ge(s["sp_done"], PAGES)
                pe.wait_ge(s["m_done"], 1)
                for p in range(PAGES):
                    nc.tensor.matmul(z_ps[p][:, :], k.neg_tri[:, :], sp_t[:, p, :], start=False, stop=False,
                                     skip_group_check=True)
                    for pp in range(p + 1, PAGES):
                        nc.tensor.matmul(z_ps[p][:, :], k.neg_ones[:, :], sp_t[:, pp, :], start=False, stop=False,
                                         skip_group_check=True)
                    nc.tensor.matmul(z_ps[p][:, :], k.neg_ones[0:NQ, :], sp_n[:, :], start=False, stop=True,
                                     skip_group_check=True).then_inc(s["cum_done"], 1)
                nc.tensor.matmul(zn_ps[0:NQ, :], k.neg_tri[0:NQ, 0:NQ], sp_n[:, :], start=False, stop=True,
                                 skip_group_check=True).then_inc(s["cum_done"], 1)
                pe.wait_ge(s["w_done"], PAGES + 1)
                pe.wait_ge(s["wm_done"], 1)
                for b in range(NB):
                    n = NB + b
                    pe.wait_ge(arrived[n % RING], all_of(n))
                    for j in range(KT):
                        c = b * 64 + j * 8
                        for p in range(PAGES):
                            nc.tensor.matmul(o_ps[:, j, b, :, :], pages[:, n % RING, p, j * P:(j + 1) * P],
                                             sp_t[:, p, c:c + 8], start=(p == 0), stop=False)
                        last = nc.tensor.matmul(o_ps[:, j, b, :, :], pages[0:NQ, n % RING, PAGES, j * P:(j + 1) * P],
                                                sp_n[:, c:c + 8], start=False, stop=True)
                    last.then_inc(s["pv_done"], 1)

            @block.vector
            def _(dve):
                nc.vector.memset(qd[:, :, :, :, :], 0.0).then_inc(s["q_zero"], 1)
                dve.wait_ge(s["q_zero"], 1)
                for g in range(2):
                    r = slice(64 * g, 64 * g + 64)
                    nc.vector.tensor_copy(qd[r, :, :, g, :], k.qT[r, :, TP:T].rearrange("p k (b q) -> p k b q", q=NQ))\
                      .then_inc(s["q_made"], 1)
                dve.wait_ge(s["kz_done"], NB + 1)
                for p in range(PAGES):
                    if p >= 2:
                        dve.wait_ge(s["e_done"], p - 1)
                    nc.vector.tensor_tensor(grid(zb[:, p % 2, :]), grid(z_ps[p][:, :]), bias(P), ALU.add)\
                      .then_inc(s["wz_done"], 1)
                    dve.wait_ge(s["wz_done"], p + 1)
                    nc.vector.tensor_scalar(zb[:, p % 2, :], zb[:, p % 2, :], 40.0, None, ALU.min)\
                      .then_inc(s["zb_done"], 1)
                nc.vector.tensor_tensor(grid(zb_n[:, :]), grid(zn_ps[0:NQ, :]), bias(NQ), ALU.add)\
                  .then_inc(s["wz_done"], 1)
                dve.wait_ge(s["wz_done"], PAGES + 1)
                nc.vector.tensor_scalar(sp_n[:, :], zb_n[:, :], 40.0, None, ALU.min).then_inc(s["zb_done"], 1)
                for p in range(PAGES):
                    dve.wait_ge(s["l_done"], PAGES + 1)
                    if p >= 2:
                        dve.wait_ge(s["sp_done"], p - 1)
                    nc.vector.tensor_tensor(grid(zb[:, p % 2, :]), grid(z_ps[p][:, :]), bias(P), ALU.add)\
                      .then_inc(s["wz_done"], 1)
                    dve.wait_ge(s["wz_done"], PAGES + 2 + p)
                    nc.vector.tensor_tensor(sp_t[:, p, :], sp_t[:, p, :], zb[:, p % 2, :], ALU.max)\
                      .then_inc(s["sp_done"], 1)
                nc.vector.tensor_tensor(sp_n[:, :], sp_n[:, :], zb_n[:, :], ALU.max).then_inc(s["sp_done"], 1)
                for p in range(PAGES):
                    dve.wait_ge(s["cum_done"], PAGES + 1)
                    nc.vector.tensor_tensor(grid(sp_t[:, p, :]), grid(z_ps[p][:, :]), bias(P), ALU.add)\
                      .then_inc(s["wz_done"], 1)
                nc.vector.tensor_tensor(grid(sp_n[:, :]), grid(zn_ps[0:NQ, :]), bias(NQ), ALU.add)\
                  .then_inc(s["wz_done"], 1)
                dve.wait_ge(s["pv_done"], NB)
                for g in range(2):
                    r = slice(64 * g, 64 * g + 64)
                    nc.vector.tensor_copy(mixT[r, KT:2 * KT, TP:T].rearrange("p k (b q) -> p k b q", q=NQ),
                                          o_ps[r, :, :, g, :]).then_inc(s["o_done"], 1)
                dve.wait_ge(s["o_done"], 2)

            @block.scalar
            def _(act):
                for p in range(PAGES + 1):
                    act.wait_ge(s["zb_done"], p + 1)
                    dst = sp_t[:, p, :] if p < PAGES else sp_n[:, :]
                    src = zb[:, p % 2, :] if p < PAGES else sp_n[:, :]
                    nc.scalar.activation(dst, src, ACT.Exp).then_inc(s["e_done"], 1)
                act.wait_ge(s["e_done"], PAGES + 1)
                for p in range(PAGES + 1):
                    dst = sp_t[:, p, :] if p < PAGES else sp_n[:, :]
                    nc.scalar.activation(dst, dst, ACT.Ln, bias=1.0).then_inc(s["l_done"], 1)
                for p in range(PAGES + 1):
                    dst = sp_t[:, p, :] if p < PAGES else sp_n[:, :]
                    act.wait_ge(s["wz_done"], 2 * PAGES + 2 + p)
                    nc.scalar.activation(dst, dst, ACT.Exp).then_inc(s["w_done"], 1)

            @block.gpsimd
            def _(pool):
                v = sp_n[:, :].rearrange("p (c q) -> p c q", q=NQ)
                for ready, n, done in ((s["sp_done"], PAGES + 1, s["m_done"]), (s["w_done"], PAGES + 1, s["wm_done"])):
                    pool.wait_ge(ready, n)
                    nc.gpsimd.affine_select(out=v, in_=v, pattern=[[0, C // NQ], [1, NQ]], base=0,
                                            channel_multiplier=-1, compare_op=ALU.is_gt, fill=0.0).then_inc(done, 1)


def phase_ssd_project(k, xc, zs, dt_tok):
    nc, io = k.nc, k.io

    def z_vector(dve, tile, ps, _):
        return nc.vector.tensor_copy(by_half(zs[:, bass.ds(tile, 1), :].rearrange("p a t -> p (a t)")), ps)

    def z_scalar(act, tile, ps, _):
        return nc.scalar.activation(by_half(zs[:, bass.ds(tile, 1), :].rearrange("p a t -> p (a t)")), ps, ACT.Copy)

    rhs = lambda j, h: k.hT[:, j, h * HALF:(h + 1) * HALF]
    phase_project(k, "z", io["mix_w_in"][:, 0:1024], KT, 4, rhs, T, z_vector, z_scalar, None, None)
    phase_project(k, "xbc", io["mix_w_in"][:, 1024:2560], KT, 6, rhs, T,
                  lambda e, tile, ps, n: nc.vector.tensor_copy(
                      by_half(xc[:, bass.ds(tile, 1), :].rearrange("p a t -> p (a t)")), ps),
                  lambda e, tile, ps, n: nc.scalar.activation(
                      by_half(xc[:, bass.ds(tile, 1), :].rearrange("p a t -> p (a t)")), ps, ACT.Copy),
                  None, None)

    loaded, state_kept, conv_done, act_done, stored = (k.sem("cv_" + n) for n in
                                                       ("loaded", "kept", "conv", "act", "stored"))
    zsil, own_d, padded, dt_mm, u_done, l_done, dt_done = (k.sem("cv_" + n) for n in
                                                           ("zsil", "own_d", "pad", "dtmm", "u", "l", "dt"))
    with ExitStack() as ctx:
        buf = k.sb("cv_buf", [P, XT, NB, 3], ctx=ctx)
        kept = k.sb("cv_kept", [P, XT, 3 + TS], ctx=ctx)
        raw_p = k.sb("cv_rawp", [P, 2, 3 + TP], ctx=ctx)
        raw_s = k.sb("cv_raws", [P, 2, NB, 3 + NQ], ctx=ctx)
        w_dt = k.sb("cv_wdt", [P, KT, H], ctx=ctx)
        u = k.sb("cv_u", [P, TT, H], ctx=ctx)
        w1 = k.sb("cv_w1", [P, TT, H], ctx=ctx)
        dt_ln = k.sb("cv_ln", [P, TT, H], ctx=ctx)
        dt_ps = k.ps("cv_dtps", [P, TT, H], ctx)
        with nc.Block() as block:
            @block.sync
            def _(sp):
                sp.dma_start(buf[:, :, :, :], io["conv_state"]).then_inc(loaded, 16)
                sp.dma_start(w_dt[:, :, :], io["mix_w_in"][:, 2560:2576].rearrange("(k p) n -> p k n", p=P))\
                  .then_inc(loaded, 16)
                sp.wait_ge(state_kept, 2)
                sp.dma_start(io["conv_out"], kept[:, :, :]).then_inc(stored, 16)
                sp.wait_ge(stored, 16)

            @block.tensor
            def _(pe):
                pe.wait_ge(loaded, 32)
                for i, (a, m) in enumerate(TOK):
                    for j in range(KT):
                        last = nc.tensor.matmul(dt_ps[0:m, i, :], k.hT[:, j, a:a + m], w_dt[:, j, :],
                                                start=(j == 0), stop=(j == KT - 1))
                last.then_inc(dt_mm, 1)

            @block.vector
            def _(dve):
                own = Chain(dve, own_d)
                own.did(nc.vector.memset(raw_p[:, :, 0:3], 0.0))
                own.did(nc.vector.memset(u[:, :, :], 0.0))
                nc.vector.tensor_copy(kept[:, :, 0:3], xc[:, :, TP - 3:TP]).then_inc(state_kept, 1)
                nc.vector.tensor_copy(kept[:, :, 3:3 + TS], xc[:, :, TP:T]).then_inc(state_kept, 1)
                dve.wait_ge(loaded, 32)
                own.settle()
                dve.wait_ge(state_kept, 2)
                for i in range(XT):
                    b = i % 2
                    own.did(nc.vector.tensor_copy(raw_p[:, b, 3:3 + TP], xc[:, i, 0:TP]))
                    own.did(nc.vector.tensor_copy(raw_s[:, b, :, 3:3 + NQ],
                                                  xc[:, i, TP:T].rearrange("p (b q) -> p b q", q=NQ)))
                    own.did(nc.vector.tensor_copy(raw_s[:, b, :, 0:3], buf[:, i, :, :]))
                    own.settle()
                    xs = xc[:, i, TP:T].rearrange("p (b q) -> p b q", q=NQ)
                    own.did(nc.vector.tensor_scalar(xc[:, i, 0:TP], raw_p[:, b, 0:TP], k.col("conv_w", i), None,
                                                    ALU.mult))
                    own.did(nc.vector.tensor_scalar(xs, raw_s[:, b, :, 0:NQ], k.col("conv_w", i), None, ALU.mult))
                    own.settle()
                    for t in range(1, 4):
                        w = k.col("conv_w", t * XT + i)
                        a = nc.vector.scalar_tensor_tensor(out=xc[:, i, 0:TP], in0=raw_p[:, b, t:t + TP], scalar=w,
                                                           in1=xc[:, i, 0:TP], op0=ALU.mult, op1=ALU.add)
                        own.did(a)
                        c = nc.vector.scalar_tensor_tensor(out=xs, in0=raw_s[:, b, :, t:t + NQ], scalar=w, in1=xs,
                                                           op0=ALU.mult, op1=ALU.add)
                        if t < 3:
                            own.did(c)
                            own.settle()
                    c.then_inc(conv_done, 1)
                    dve.wait_ge(conv_done, i + 1)
                    own.settle()
                dve.wait_ge(dt_mm, 1)
                bias = k.small[:, COLS["dt_bias"][0]:COLS["dt_bias"][1]]
                own.step(nc.vector.tensor_tensor(u[:, 0:4, :], dt_ps[:, 0:4, :],
                                                 bias.unsqueeze(1).to_broadcast([P, 4, H]), ALU.add))
                own.step(nc.vector.tensor_tensor(u[0:TS, 4, :], dt_ps[0:TS, 4, :], bias[0:TS, :], ALU.add))
                own.step(nc.vector.tensor_scalar(dt_tok[:, :, :], u[:, :, :], 0.0, None, ALU.max))
                own.step(nc.vector.tensor_scalar(w1[:, :, :], u[:, :, :], -1.0, None, ALU.mult))
                nc.vector.tensor_tensor(u[:, :, :], u[:, :, :], w1[:, :, :], ALU.min).then_inc(u_done, 1)
                dve.wait_ge(l_done, 1)
                nc.vector.tensor_scalar(w1[:, :, :], u[:, :, :], 1.0, None, ALU.add).then_inc(u_done, 1)
                dve.wait_ge(l_done, 2)
                lnw = dt_ln
                own.step(nc.vector.tensor_scalar(w1[:, :, :], w1[:, :, :], 1.0, 1.0e-30, ALU.subtract, ALU.max))
                own.step(nc.vector.reciprocal(w1[:, :, :], w1[:, :, :]))
                own.step(nc.vector.tensor_tensor(w1[:, :, :], w1[:, :, :], u[:, :, :], ALU.mult))
                own.step(nc.vector.tensor_tensor(w1[:, :, :], w1[:, :, :], lnw[:, :, :], ALU.mult))
                own.step(nc.vector.tensor_scalar(lnw[:, :, :], u[:, :, :], -0.5, 1.0, ALU.mult, ALU.add))
                own.step(nc.vector.tensor_tensor(u[:, :, :], u[:, :, :], lnw[:, :, :], ALU.mult))
                own.step(nc.vector.tensor_tensor(w1[:, :, :], w1[:, :, :], u[:, :, :], ALU.max))
                own.step(nc.vector.tensor_tensor(dt_tok[:, :, :], dt_tok[:, :, :], w1[:, :, :], ALU.add))

            @block.scalar
            def _(act):
                for i in range(KT):
                    nc.scalar.activation(zs[:, i, :], zs[:, i, :], ACT.Silu).then_inc(zsil, 1)
                for i in range(XT):
                    act.wait_ge(conv_done, i + 1)
                    nc.scalar.activation(xc[:, i, :], xc[:, i, :], ACT.Silu, bias=k.col("conv_b", i))\
                      .then_inc(act_done, 1)
                act.wait_ge(u_done, 1)
                nc.scalar.activation(u[:, :, :], u[:, :, :], ACT.Exp).then_inc(l_done, 1)
                act.wait_ge(u_done, 2)
                nc.scalar.activation(dt_ln[:, :, :], w1[:, :, :], ACT.Ln).then_inc(l_done, 1)
                act.wait_ge(zsil, KT)
                act.wait_ge(act_done, XT)


def phase_ssd(k, xc, mixT, dt_tok):
    nc, io = k.nc, k.io
    names = ("tr", "trc", "dA", "ac_mm", "ac_ev", "aexp", "own_d", "own_a", "xw", "bm", "cb", "cbc", "bc", "dec",
             "decx", "decm", "e", "m", "cs", "y", "yo", "st_mm", "st", "sload", "sst", "neg", "own_p")
    s = {n: k.sem("ss_" + n) for n in names}
    with ExitStack() as ctx:
        x_tok = k.sb("x_tok", [P, 2, D], ctx=ctx)
        b_tok = k.sb("b_tok", [P, 2, 2 * NS], ctx=ctx)
        xdt = k.sb("xdt", [P, 2, D], ctx=ctx)
        dA = k.sb("dA", [P, TT, H], ctx=ctx)
        neg_a = k.sb("neg_a", [P, H], ctx=ctx)
        nacum = k.sb("nacum", [P, TT, H], ctx=ctx)
        to_end = k.sb("to_end", [P, TT, H], ctx=ctx)
        cd = k.sb("cd", [P, 4, H], ctx=ctx)
        cds = k.sb("cds", [P, NB, H], ctx=ctx)
        dAm = k.sb("dAm", [TS, NB, H], ctx=ctx)
        bm = k.sb("bm", [TS, NB, 2 * NS], ctx=ctx)
        cbs = k.sb("cbs", [P, 2, P], ctx=ctx)
        dec = k.sb("dec", [P, 2, 4, P], ctx=ctx)
        dA_rep = k.sb("dA_rep", [P, H, P], ctx=ctx)
        e_t = k.sb("e_t", [P, 2, 4, P], ctx=ctx)
        st = k.sb("st", [P, D], ctx=ctx)
        sst = k.sb("sst", [P, NB, D], ctx=ctx)
        ac_ps = k.ps("ss_acps", [P, 512], ctx)
        tr_ps = k.ps("ss_trps", [P, 512], ctx)
        bc_ps = [k.ps(f"ss_bc{i}", [P, 4, P], ctx) for i in range(2)]
        y_ps = [k.ps(f"ss_y{i}", [P, 2, P], ctx) for i in range(2)]
        st_ps = [k.ps(f"ss_st{i}", [P, 512], ctx) for i in range(2)]

        def tri(c):
            return k.tri_le[:, :] if c < 4 else k.tri_same[:, :]

        with nc.Block() as block:
            @block.sync
            def _(sp):
                sp.dma_start(sst[:, :, :], io["ssm_state"]).then_inc(s["sload"], 16)
                sp.wait_ge(s["st"], 4)
                sp.dma_start(io["ssm_p"], st[:, :]).then_inc(s["sst"], 16)
                sp.wait_ge(s["st"], 4 + NB)
                sp.dma_start(io["ssm_s"], sst[:, :, :]).then_inc(s["sst"], 16)
                sp.wait_ge(s["sst"], 32)

            @block.tensor
            def _(pe):
                pe.wait_ge(s["dA"], 2)
                for c, (a, n) in enumerate(TOK):
                    nc.tensor.matmul(ac_ps[0:n, c * H:(c + 1) * H], tri(c), dA[0:n, c, :], start=True, stop=True)
                for c in range(4):
                    nc.tensor.matmul(ac_ps[:, 80 + c * H:80 + (c + 1) * H], k.ones[:, :], dA[:, c, :],
                                     start=True, stop=True)
                nc.tensor.matmul(ac_ps[0:TS, 144:160], k.same[:, :], dA[0:TS, 4, :], start=True, stop=True)
                nc.tensor.matmul(ac_ps[:, 160:288], k.ones[0:TS, :], dAm[:, :, :], start=True, stop=True)\
                  .then_inc(s["ac_mm"], 1)
                n_tr = 0
                for c, (a, n) in enumerate(TOK):
                    for g0, g1 in ((0, 4), (4, 8), (8, 10)):
                        if n_tr:
                            pe.wait_ge(s["trc"], n_tr)
                        for i in range(g0, g1):
                            last = nc.tensor.transpose(tr_ps[0:n, (i - g0) * P:(i - g0 + 1) * P], xc[:, i, a:a + n],
                                                       k.ident[:, :])
                        last.then_inc(s["tr"], 1)
                        n_tr += 1
                    if c == 0:
                        pe.wait_ge(s["ac_ev"], 1)
                    else:
                        pe.wait_ge(s["cbc"], c)
                    for g in range(2):
                        last = nc.tensor.matmul(ac_ps[0:n, 256 + g * P:256 + g * P + n], xc[:, 8 + g, a:a + n],
                                                xc[:, 10 + g, a:a + n], start=True, stop=True)
                    last.then_inc(s["cb"], 1)
                    pe.wait_ge(s["neg"], c + 1)
                    for q in range(4):
                        u = 4 * c + q

                        def broadcast_sums(v):
                            if v >= 2:
                                pe.wait_ge(s["dec"], v - 1)
                                pe.wait_ge(s["e"], v - 1)
                            for h in range(4):
                                nn = nc.tensor.matmul(bc_ps[v % 2][:, h, 0:n], dA_rep[0:n, 4 * (v % 4) + h, :], tri(c),
                                                      start=True, stop=True)
                            nn.then_inc(s["bc"], 1)

                        if q == 0:
                            broadcast_sums(u)
                        if q < 3:
                            broadcast_sums(u + 1)
                        pe.wait_ge(s["m"], u + 1)
                        pe.wait_ge(s["cs"], u + 1)
                        if u >= 2:
                            pe.wait_ge(s["yo"], u - 1)
                        if c == 4 and q == 0:
                            pe.wait_ge(s["sload"], 16)
                        for h in (0, 2, 1, 3):
                            r = slice(64 * (h % 2), 64 * (h % 2) + 64)
                            hh = 4 * q + h
                            f = slice(hh * HD, (hh + 1) * HD)
                            last = nc.tensor.matmul(y_ps[u % 2][r, h // 2, 0:n], xdt[0:n, c % 2, f],
                                                    dec[0:n, u % 2, h, 0:n], start=True, stop=(c == 0),
                                                    skip_group_check=True)
                            if 1 <= c < 4:
                                last = nc.tensor.matmul(y_ps[u % 2][r, h // 2, 0:n], st[:, f], e_t[:, u % 2, h, 0:n],
                                                        start=False, stop=True, skip_group_check=True)
                            if c == 4:
                                for b in range(NB):
                                    last = nc.tensor.matmul(y_ps[u % 2][r, h // 2, NQ * b:NQ * (b + 1)],
                                                            sst[:, b, f], e_t[:, u % 2, h, NQ * b:NQ * (b + 1)],
                                                            start=False, stop=(b == NB - 1), skip_group_check=True)
                        last.then_inc(s["y"], 1)
                    pe.wait_ge(s["xw"], c + 1)
                    if c < 4:
                        if c >= 1:
                            pe.wait_ge(s["st"], c)
                        for g in range(2):
                            last = nc.tensor.matmul(st_ps[g][:, :], b_tok[:, c % 2, g * NS:(g + 1) * NS],
                                                    x_tok[:, c % 2, g * 512:(g + 1) * 512], start=True, stop=True)
                        last.then_inc(s["st_mm"], 1)
                    else:
                        pe.wait_ge(s["bm"], NB)
                        for b in range(NB):
                            pe.wait_ge(s["st"], 4 + b)
                            for g in range(2):
                                last = nc.tensor.matmul(st_ps[g][:, :], bm[:, b, g * NS:(g + 1) * NS],
                                                        x_tok[0:TS, 0, g * 512:(g + 1) * 512], start=True, stop=True)
                            last.then_inc(s["st_mm"], 1)

            @block.vector
            def _(dve):
                own = Chain(dve, s["own_d"])
                dve.wait_ge(s["aexp"], 1)
                own.step(nc.vector.tensor_scalar(neg_a[:, :], neg_a[:, :], -1.0, None, ALU.mult))
                nc.vector.tensor_tensor(dA[:, :, :], dt_tok[:, :, :], neg_a[:, :].unsqueeze(1).to_broadcast([P, TT, H]),
                                        ALU.mult).then_inc(s["dA"], 1)
                dve.wait_ge(s["dA"], 1)
                nc.vector.tensor_tensor(dAm[:, :, :], dA[0:TS, 4, :].unsqueeze(1).to_broadcast([TS, NB, H]),
                                        k.member[:, :].unsqueeze(2).to_broadcast([TS, NB, H]), ALU.mult)\
                  .then_inc(s["dA"], 1)
                dve.wait_ge(s["ac_mm"], 1)
                own.did(nc.vector.memset(nacum[:, :, :], 0.0))
                own.did(nc.vector.memset(to_end[:, :, :], 0.0))
                own.settle()
                ac = ac_ps[:, 0:80].rearrange("p (c h) -> p c h", h=H)
                en = ac_ps[:, 80:144].rearrange("p (c h) -> p c h", h=H)
                own.did(nc.vector.tensor_scalar(nacum[:, 0:4, :], ac[:, 0:4, :], -1.0, None, ALU.mult))
                own.did(nc.vector.tensor_scalar(nacum[0:TS, 4, :], ac[0:TS, 4, :], -1.0, None, ALU.mult))
                own.settle()
                own.did(nc.vector.tensor_tensor(to_end[:, 0:4, :], en, nacum[:, 0:4, :], ALU.add))
                own.did(nc.vector.tensor_tensor(to_end[0:TS, 4, :], ac_ps[0:TS, 144:160], nacum[0:TS, 4, :], ALU.add))
                own.did(nc.vector.tensor_copy(cd[:, :, :], en))
                own.did(nc.vector.tensor_copy(cds[:, :, :], ac_ps[:, 160:288].rearrange("p (b h) -> p b h", h=H)))
                own.settle()
                dve.sem_inc(s["ac_ev"], 1)

                n_tr = 0
                for c, (a, n) in enumerate(TOK):
                    if c >= 1:
                        dve.wait_ge(s["st_mm"], c)
                    for g0, g1 in ((0, 4), (4, 8), (8, 10)):
                        n_tr += 1
                        dve.wait_ge(s["tr"], n_tr)
                        dst = x_tok[0:n, c % 2, g0 * P:g1 * P] if g0 < 8 else b_tok[0:n, c % 2, :]
                        nc.vector.tensor_copy(dst, tr_ps[0:n, 0:(g1 - g0) * P]).then_inc(s["trc"], 1)
                    if c >= 1:
                        dve.wait_ge(s["bc"], 4 * c)
                    nc.vector.tensor_copy(dA_rep[0:n, :, :], dA[0:n, c, :].unsqueeze(2).to_broadcast([n, H, P]))\
                      .then_inc(s["neg"], 1)
                    dve.wait_ge(s["trc"], n_tr)
                    xt = x_tok[0:n, c % 2, :].rearrange("p (h e) -> p h e", e=HD)
                    xd = xdt[0:n, c % 2, :].rearrange("p (h e) -> p h e", e=HD)
                    own.step(nc.vector.tensor_tensor(xd, xt, dt_tok[0:n, c, :].unsqueeze(2).to_broadcast([n, H, HD]),
                                                     ALU.mult))
                    dve.wait_ge(s["aexp"], 4)
                    nc.vector.tensor_tensor(xt, xd, to_end[0:n, c, :].unsqueeze(2).to_broadcast([n, H, HD]), ALU.mult)\
                      .then_inc(s["xw"], 1)
                    if c == 4:
                        for b in range(NB):
                            nc.vector.tensor_scalar(bm[:, b, :], b_tok[0:TS, 0, :], k.member[:, b:b + 1], None,
                                                    ALU.mult).then_inc(s["bm"], 1)
                    dve.wait_ge(s["cb"], c + 1)
                    if c >= 1:
                        dve.wait_ge(s["m"], 4 * c)
                    nc.vector.tensor_copy(cbs[0:n, :, 0:n],
                                          ac_ps[0:n, 256:512].rearrange("p (g l) -> p g l", g=2)[:, :, 0:n])\
                      .then_inc(s["cbc"], 1)
                    dve.wait_ge(s["cbc"], c + 1)

                    def seg(v):
                        dve.wait_ge(s["e"], v + 1)
                        if v >= 2:
                            dve.wait_ge(s["y"], v - 1)
                        nc.vector.tensor_tensor(dec[0:n, v % 2, :, 0:n], bc_ps[v % 2][0:n, :, 0:n],
                                                nacum[0:n, c, 4 * (v % 4):4 * (v % 4) + 4].unsqueeze(2)
                                                .to_broadcast([n, 4, n]), ALU.add).then_inc(s["dec"], 1)

                    for q in range(4):
                        u = 4 * c + q
                        if q == 0:
                            seg(u)
                        if q < 3:
                            seg(u + 1)
                        dve.wait_ge(s["decx"], u + 1)
                        nc.vector.tensor_tensor(dec[0:n, u % 2, :, 0:n], dec[0:n, u % 2, :, 0:n],
                                                cbs[0:n, q // 2, 0:n].unsqueeze(1).to_broadcast([n, 4, n]), ALU.mult)\
                          .then_inc(s["m"], 1)
                        dve.wait_ge(s["e"], u + 1)
                        nc.vector.tensor_tensor(e_t[:, u % 2, :, 0:n], e_t[:, u % 2, :, 0:n],
                                                xc[:, 10 + q // 2, a:a + n].unsqueeze(1).to_broadcast([P, 4, n]),
                                                ALU.mult).then_inc(s["cs"], 1)
                        dve.wait_ge(s["y"], u + 1)
                        for i in range(2):
                            j = 2 * q + i
                            ins = nc.vector.scalar_tensor_tensor(out=mixT[:, j, a:a + n], in0=xc[:, j, a:a + n],
                                                                 scalar=k.col("d_skip", j), in1=y_ps[u % 2][:, i, 0:n],
                                                                 op0=ALU.mult, op1=ALU.add)
                            if i == 0:
                                own.did(ins)
                            else:
                                ins.then_inc(s["yo"], 1)
                    own.settle()
                    if c < 4:
                        dve.wait_ge(s["st_mm"], c + 1)
                        if c >= 1:
                            sv = st[:, :].rearrange("p (h e) -> p h e", e=HD)
                            own.step(nc.vector.tensor_tensor(sv, sv, cd[:, c, :].unsqueeze(2)
                                                             .to_broadcast([P, H, HD]), ALU.mult))
                        for g in range(2):
                            f = slice(g * 512, (g + 1) * 512)
                            if c == 0:
                                ins = nc.vector.tensor_copy(st[:, f], st_ps[g][:, :])
                            else:
                                ins = nc.vector.tensor_tensor(st[:, f], st[:, f], st_ps[g][:, :], ALU.add)
                            own.did(ins)
                        own.settle()
                        dve.sem_inc(s["st"], 1)
                    else:
                        dve.wait_ge(s["yo"], 20)
                        for b in range(NB):
                            sv = sst[:, b, :].rearrange("p (h e) -> p h e", e=HD)
                            own.step(nc.vector.tensor_tensor(sv, sv, cds[:, b, :].unsqueeze(2)
                                                             .to_broadcast([P, H, HD]), ALU.mult))
                            dve.wait_ge(s["st_mm"], 5 + b)
                            own.did(nc.vector.tensor_tensor(sst[:, b, 0:512], sst[:, b, 0:512], st_ps[0][:, :],
                                                            ALU.add))
                            own.settle()
                            nc.vector.tensor_tensor(sst[:, b, 512:D], sst[:, b, 512:D], st_ps[1][:, :], ALU.add)\
                              .then_inc(s["st"], 1)
                        dve.wait_ge(s["st"], 4 + NB)

            @block.scalar
            def _(act):
                nc.scalar.activation(neg_a[:, :], k.small[:, COLS["a_log"][0]:COLS["a_log"][1]], ACT.Exp)\
                  .then_inc(s["aexp"], 1)
                act.wait_ge(s["ac_ev"], 1)
                nc.scalar.activation(to_end[:, :, :], to_end[:, :, :], ACT.Exp).then_inc(s["aexp"], 1)
                nc.scalar.activation(cd[:, :, :], cd[:, :, :], ACT.Exp).then_inc(s["aexp"], 1)
                nc.scalar.activation(cds[:, :, :], cds[:, :, :], ACT.Exp).then_inc(s["aexp"], 1)
                for c, (a, n) in enumerate(TOK):
                    for q in range(4):
                        u = 4 * c + q
                        act.wait_ge(s["bc"], u + 1)
                        if u >= 2:
                            act.wait_ge(s["y"], u - 1)
                        nc.scalar.activation(e_t[:, u % 2, :, 0:n], bc_ps[u % 2][:, :, 0:n], ACT.Exp)\
                          .then_inc(s["e"], 1)
                        act.wait_ge(s["decm"], u + 1)
                        d = dec[0:n, u % 2, :, 0:n]
                        nc.scalar.activation(d, d, ACT.Exp).then_inc(s["decx"], 1)
                act.wait_ge(s["decx"], 20)

            @block.gpsimd
            def _(pool):
                own = Chain(pool, s["own_p"])
                for c, (a, n) in enumerate(TOK):
                    for q in range(4):
                        u = 4 * c + q
                        pool.wait_ge(s["dec"], u + 1)
                        if c < 4:
                            d = dec[:, u % 2, :, :]
                            nc.gpsimd.affine_select(out=d, in_=d, pattern=[[0, 4], [1, P]], base=0,
                                                    channel_multiplier=-1, compare_op=ALU.is_ge, fill=NO_DECAY)\
                              .then_inc(s["decm"], 1)
                        else:
                            d = dec[0:TS, u % 2, :, 0:TS]
                            own.step(nc.gpsimd.affine_select(out=d, in_=d, pattern=[[0, 4], [1, TS]], base=0,
                                                             channel_multiplier=-1, compare_op=ALU.is_ge, fill=NO_DECAY))
                            d = d.rearrange("p h (b q) -> p h b q", q=NQ)
                            nc.gpsimd.affine_select(out=d, in_=d, pattern=[[0, 4], [-NQ, NB], [0, NQ]], base=0,
                                                    channel_multiplier=1, compare_op=ALU.is_ge, fill=NO_DECAY)\
                              .then_inc(s["decm"], 1)


def phase_gated_norm(k, zs, mixT):
    nc = k.nc
    gated, squared, summed, root_in, root, done, own_d = (k.sem("gn_" + n) for n in
                                                          ("gated", "sq", "sum", "ri", "root", "done", "own"))
    with ExitStack() as ctx:
        sq = k.sb("gn_sq", [P, 2, T], ctx=ctx)
        rstd = k.sb("gn_rstd", [P, 2, T], ctx=ctx)
        ps = k.ps("gn_ps", [P, 4, 512], ctx)
        with nc.Block() as block:
            @block.vector
            def _(dve):
                own = Chain(dve, own_d)
                for j in range(KT):
                    nc.vector.tensor_tensor(mixT[:, j, :], mixT[:, j, :], zs[:, j, :], ALU.mult).then_inc(gated, 1)
                for g in range(2):
                    dve.wait_ge(summed, 4 * (g + 1))
                    nc.vector.tensor_scalar(by_half(rstd[:, g, :]), ps[:, 2 * g:2 * g + 2, 0:HALF], 2.0 / D, EPS,
                                            ALU.mult, ALU.add).then_inc(root_in, 1)
                for g in range(2):
                    dve.wait_ge(root, g + 1)
                    own.step(nc.vector.reciprocal(rstd[:, g, :], rstd[:, g, :]))
                dve.wait_ge(gated, KT)
                dve.wait_ge(squared, KT)
                for j in range(KT):
                    nc.vector.scalar_tensor_tensor(out=mixT[:, j, :], in0=mixT[:, j, :], scalar=k.col("norm_g", j),
                                                   in1=rstd[:, j // 4, :], op0=ALU.mult, op1=ALU.mult).then_inc(done, 1)
                dve.wait_ge(done, KT)

            @block.scalar
            def _(act):
                for j in range(KT):
                    act.wait_ge(gated, j + 1)
                    if j >= 2:
                        act.wait_ge(summed, j - 1)
                    nc.scalar.activation(sq[:, j % 2, :], mixT[:, j, :], ACT.Square).then_inc(squared, 1)
                for g in range(2):
                    act.wait_ge(root_in, g + 1)
                    nc.scalar.activation(rstd[:, g, :], rstd[:, g, :], ACT.Sqrt).then_inc(root, 1)

            @block.tensor
            def _(pe):
                for j in range(KT):
                    pe.wait_ge(squared, j + 1)
                    for h in range(2):
                        last = nc.tensor.matmul(ps[:, 2 * (j // 4) + h, 0:HALF], k.ones[:, :],
                                                sq[:, j % 2, h * HALF:(h + 1) * HALF],
                                                start=(j % 4 == 0), stop=(j % 4 == 3))
                    last.then_inc(summed, 1)


def phase_out_project(k, name, w, kt, src, layer, chunk):
    nc = k.nc
    m0 = layer * 48 + chunk * KT
    y = k.sb
    with ExitStack() as ctx:
        res = k.sb(f"{name}_res", [P, KT, T], ctx=ctx)

        def flat(tile):
            return by_half(res[:, bass.ds(tile, 1), :].rearrange("p a t -> p (a t)"))

        phase_project(k, name, w, kt, 4, lambda j, h: src[:, j, h * HALF:(h + 1) * HALF], T,
                      lambda e, tile, ps, n: nc.vector.tensor_copy(flat(tile), ps),
                      lambda e, tile, ps, n: nc.scalar.activation(flat(tile), ps, ACT.Copy), None, None)
        phase_residual(k, name, res, m0)


def phase_residual(k, name, res, m0):
    nc = k.nc
    done, scaled = k.sem(f"{name}_added"), k.sem(f"{name}_scaled")
    with nc.Block() as block:
        @block.vector
        def _(dve):
            for j in range(KT):
                nc.vector.scalar_tensor_tensor(out=k.xT[:, j, 0:TP], in0=res[:, j, 0:TP], scalar=k.mod[:, m0 + j, 0:1],
                                               in1=k.xT[:, j, 0:TP], op0=ALU.mult, op1=ALU.add).then_inc(done, 1)
            rs = res[:, :, TP:T].rearrange("p k (b q) -> p k b q", q=NQ)
            g = k.mod[:, m0:m0 + KT, 1:NC9].unsqueeze(3).to_broadcast([P, KT, NB, NQ])
            nc.vector.tensor_tensor(rs, rs, g, ALU.mult).then_inc(scaled, 1)
            dve.wait_ge(scaled, 1)
            nc.vector.tensor_tensor(k.xT[:, :, TP:T], k.xT[:, :, TP:T], res[:, :, TP:T], ALU.add).then_inc(done, 1)
            dve.wait_ge(done, KT + 1)


def phase_short_conv(k, proj, gT):
    nc, io = k.nc, k.io
    loaded, own_d, kept_done, stored = (k.sem("sc_" + n) for n in ("loaded", "own", "kept", "stored"))
    with ExitStack() as ctx:
        buf = k.sb("sc_buf", [P, KT, NB, 2], ctx=ctx)
        kept = k.sb("sc_kept", [P, KT, 2 + TS], ctx=ctx)
        raw_p = k.sb("sc_rawp", [P, 2 + TP], ctx=ctx)
        raw_s = k.sb("sc_raws", [P, NB, 2 + NQ], ctx=ctx)
        with nc.Block() as block:
            @block.sync
            def _(sp):
                sp.dma_start(buf[:, :, :, :], io["sc_state"]).then_inc(loaded, 16)
                sp.wait_ge(kept_done, 2)
                sp.dma_start(io["sc_out"], kept[:, :, :]).then_inc(stored, 16)
                sp.wait_ge(stored, 16)

            @block.vector
            def _(dve):
                own = Chain(dve, own_d)
                own.did(nc.vector.memset(raw_p[:, 0:2], 0.0))
                for j in range(KT):
                    c, u = proj[:, KT + j, :], proj[:, 2 * KT + j, :]
                    own.did(nc.vector.tensor_tensor(u, c, u, ALU.mult))
                own.settle()
                u = proj[:, 2 * KT:3 * KT, :]
                nc.vector.tensor_copy(kept[:, :, 0:2], u[:, :, TP - 2:TP]).then_inc(kept_done, 1)
                nc.vector.tensor_copy(kept[:, :, 2:2 + TS], u[:, :, TP:T]).then_inc(kept_done, 1)
                dve.wait_ge(loaded, 16)
                for j in range(KT):
                    own.did(nc.vector.tensor_copy(raw_p[:, 2:2 + TP], u[:, j, 0:TP]))
                    own.did(nc.vector.tensor_copy(raw_s[:, :, 2:2 + NQ],
                                                  u[:, j, TP:T].rearrange("p (b q) -> p b q", q=NQ)))
                    own.did(nc.vector.tensor_copy(raw_s[:, :, 0:2], buf[:, j, :, :]))
                    own.settle()
                    gs = gT[:, j, TP:T].rearrange("p (b q) -> p b q", q=NQ)
                    own.did(nc.vector.tensor_scalar(gT[:, j, 0:TP], raw_p[:, 0:TP], k.col("sc_w", j), None, ALU.mult))
                    own.did(nc.vector.tensor_scalar(gs, raw_s[:, :, 0:NQ], k.col("sc_w", j), None, ALU.mult))
                    own.settle()
                    for t in range(1, 3):
                        w = k.col("sc_w", t * KT + j)
                        own.did(nc.vector.scalar_tensor_tensor(out=gT[:, j, 0:TP], in0=raw_p[:, t:t + TP], scalar=w,
                                                               in1=gT[:, j, 0:TP], op0=ALU.mult, op1=ALU.add))
                        own.did(nc.vector.scalar_tensor_tensor(out=gs, in0=raw_s[:, :, t:t + NQ], scalar=w, in1=gs,
                                                               op0=ALU.mult, op1=ALU.add))
                        own.settle()
                    own.step(nc.vector.tensor_tensor(gT[:, j, :], gT[:, j, :], proj[:, j, :], ALU.mult))


class Routing:

    def __init__(self, k, ctx, layer):
        self.tok = k.sb(f"route{layer}_tok", [CAP, NBLK], I32, ctx=ctx)
        self.slot = k.sb(f"route{layer}_slot", [P, 2, TT], I32, ctx=ctx)
        self.weight = k.sb(f"route{layer}_weight", [P, 2, TT], ctx=ctx)
        self.more = k.sb(f"route{layer}_more", [1, 1 + OVB], I32, ctx=ctx)


def phase_route(k, layer, r, ex):
    nc, io = k.nc, k.io
    nm = f"rt{layer}_"
    names = ("w", "iota", "tr", "trc", "rows", "lg", "e_in", "e_out", "mask", "rank", "pair", "slots", "own_d", "own_p",
             "done")
    s = {n: k.sem(nm + n) for n in names}
    with ExitStack() as ctx:
        sb = lambda n, shape, dt=F32: k.sb(nm + n, shape, dt, ctx=ctx)
        w_r = sb("wr", [P, KT, 36])
        rows = sb("rowbuf", [P, 2, D])
        lg = sb("lg", [P, TT, 36])
        desc = sb("desc", [P, 8])
        expert = sb("expert", [P, NE])
        block_id = sb("block_id", [P, NBLK])
        row_id = sb("row_id", [P, CAP])
        tok_id = sb("tok_id", [P, TT])
        full = sb("full", [P, MAXQ])
        valid = sb("valid", [P, TT])
        t1, t2, t3, t4 = (sb(f"t{i}", [P, TT, 1]) for i in range(4))
        g4, oh_g = sb("g4", [P, TT, 4]), sb("oh_g", [P, TT, 4])
        e8, sc8 = sb("e8", [P, TT, 8]), sb("sc8", [P, TT, 8])
        oh8 = [sb(f"oh8{i}", [P, TT, 8]) for i in range(2)]
        top = [sb(f"top{i}", [P, TT, 1]) for i in range(2)]
        oh = [sb(f"oh{i}", [P, TT, NE]) for i in range(2)]
        x32, mask, rank = sb("x32", [P, TT, NE]), sb("mask", [P, TT, NE]), sb("rank", [P, TT, NE])
        cnt, nov, ovb = sb("cnt", [P, NE]), sb("nov", [P, NE]), sb("ovb", [P, NE])
        cmp_n = sb("cmp_n", [P, NE, MAXQ])
        cmp_q = sb("cmp_q", [P, TT, MAXQ])
        cmp_o = sb("cmp_o", [1, OVB, NE])
        more_f = sb("more_f", [1, 1 + OVB])
        blk, row, rk, q_, ov = ([sb(f"{n}{i}", [P, TT]) for i in range(2)] for n in ("blk", "row", "rk", "q", "ov"))
        row_hot = sb("row_hot", [P, 2, CAP])
        blk_hot = sb("blk_hot", [P, 2, NBLK])
        slot_f = sb("slot_f", [CAP, NBLK])
        none = sb("none", [CAP, NBLK])
        tr_ps = [k.ps(f"{nm}tr{i}", [P, 512], ctx) for i in range(2)]
        lg_ps = k.ps(nm + "lgps", [P, TT, 36], ctx)
        rk_ps = k.ps(nm + "rkps", [P, TT + 1, NE], ctx)
        sl_ps = k.ps(nm + "slps", [CAP, NBLK], ctx)

        with nc.Block() as block:
            @block.sync
            def _(sp):
                sp.dma_start(w_r[:, :, :], io["w_route"][layer].rearrange("(k p) n -> p k n", p=P)).then_inc(s["w"], 16)
                for b in range(ex.SLOTS):
                    ex.load(k, sp, b, b, ex.w[b])
                for i, (a, m) in enumerate(TOK):
                    sp.wait_ge(s["trc"], 2 * (i + 1))
                    sp.dma_start(k.h_rows[a:a + m, :], rows[0:m, i % 2, :]).then_inc(s["rows"], 16)
                    sp.wait_ge(s["rows"], 16 * (i + 1))

            @block.gpsimd
            def _(pool):
                own = Chain(pool, s["own_p"])
                kw = dict(allow_small_or_imprecise_dtypes=True)
                own.did(nc.gpsimd.iota(desc[:, :], [[-1, 8]], base=8, channel_multiplier=0, **kw))
                own.did(nc.gpsimd.iota(expert[:, :], [[1, NE]], base=0, channel_multiplier=0, **kw))
                own.did(nc.gpsimd.iota(block_id[:, :], [[1, NBLK]], base=0, channel_multiplier=0, **kw))
                own.did(nc.gpsimd.iota(row_id[:, :], [[1, CAP]], base=0, channel_multiplier=0, **kw))
                own.did(nc.gpsimd.iota(tok_id[:, :], [[P, TT]], base=1, channel_multiplier=1, **kw))
                own.did(nc.gpsimd.iota(full[:, :], [[CAP, MAXQ]], base=CAP, channel_multiplier=0, **kw))
                own.step(nc.gpsimd.memset(valid[:, :], 1.0))
                own.step(nc.gpsimd.affine_select(out=valid[:, :], in_=valid[:, :], pattern=[[-P, TT]], base=T - 1,
                                                 channel_multiplier=-1, compare_op=ALU.is_ge, fill=0.0))
                pool.sem_inc(s["iota"], 1)

            @block.tensor
            def _(pe):
                pe.wait_ge(s["w"], 16)
                for i, (a, m) in enumerate(TOK):
                    for j in range(KT):
                        last = nc.tensor.matmul(lg_ps[0:m, i, :], k.hT[:, j, a:a + m], w_r[:, j, :],
                                                start=(j == 0), stop=(j == KT - 1))
                last.then_inc(s["lg"], 1)
                for i, (a, m) in enumerate(TOK):
                    for n in range(2):
                        u = 2 * i + n
                        if u >= 2:
                            pe.wait_ge(s["trc"], u - 1)
                        for j in range(4):
                            last = nc.tensor.transpose(tr_ps[n][0:m, j * P:(j + 1) * P], k.hT[:, 4 * n + j, a:a + m],
                                                       k.ident[:, :])
                        last.then_inc(s["tr"], 1)
                pe.wait_ge(s["mask"], 1)
                for i in range(TT):
                    nc.tensor.matmul(rk_ps[:, i, :], k.tri_lt[:, :], mask[:, i, :], start=True, stop=(i == 0))
                    for ii in range(i):
                        nc.tensor.matmul(rk_ps[:, i, :], k.ones[:, :], mask[:, ii, :], start=False, stop=(ii == i - 1))
                for i in range(TT):
                    last = nc.tensor.matmul(rk_ps[:, TT, :], k.ones[:, :], mask[:, i, :], start=(i == 0),
                                            stop=(i == TT - 1))
                last.then_inc(s["rank"], 1)
                for n in range(2 * TT):
                    m = TOK[n // 2][1]
                    pe.wait_ge(s["pair"], n + 1)
                    last = nc.tensor.matmul(sl_ps[:, :], row_hot[0:m, n % 2, :], blk_hot[0:m, n % 2, :],
                                            start=(n == 0), stop=(n == 2 * TT - 1))
                    last.then_inc(s["slots"], 1)

            @block.scalar
            def _(act):
                for u in range(2 * TT):
                    i, n = u // 2, u % 2
                    m = TOK[i][1]
                    act.wait_ge(s["tr"], u + 1)
                    if i >= 2 and n == 0:
                        act.wait_ge(s["rows"], 16 * (i - 1))
                    nc.scalar.activation(rows[0:m, i % 2, n * 512:(n + 1) * 512], tr_ps[n][0:m, :], ACT.Copy)\
                      .then_inc(s["trc"], 1)
                act.wait_ge(s["e_in"], 1)
                nc.scalar.activation(g4[:, :, :], g4[:, :, :], ACT.Exp).then_inc(s["e_out"], 1)
                act.wait_ge(s["e_in"], 2)
                nc.scalar.activation(e8[:, :, :], e8[:, :, :], ACT.Exp).then_inc(s["e_out"], 1)

            @block.vector
            def _(dve):
                own = Chain(dve, s["own_d"])
                V = nc.vector
                step = own.step
                wide = lambda t, n: t[:, :, :].to_broadcast([P, TT, n])
                step(V.memset(lg[:, :, :], 0.0))
                dve.wait_ge(s["lg"], 1)
                bias = k.small[:, COLS["router_b"][0] + 36 * layer:COLS["router_b"][0] + 36 * (layer + 1)]
                step(V.tensor_tensor(lg[:, 0:4, :], lg_ps[:, 0:4, :], bias.unsqueeze(1).to_broadcast([P, 4, 36]), ALU.add))
                step(V.tensor_tensor(lg[0:TS, 4, :], lg_ps[0:TS, 4, :], bias[0:TS, :], ALU.add))
                step(V.tensor_reduce(t1[:, :, :], lg[:, :, 0:4], AX_X, ALU.max))
                V.tensor_tensor(g4[:, :, :], lg[:, :, 0:4], wide(t1, 4), ALU.subtract).then_inc(s["e_in"], 1)
                dve.wait_ge(s["iota"], 1)
                dve.wait_ge(s["e_out"], 1)
                g_top = t4
                step(V.tensor_reduce(t1[:, :, :], g4[:, :, :], AX_X, ALU.max))
                step(V.tensor_reduce(t2[:, :, :], g4[:, :, :], AX_X, ALU.add))
                step(V.reciprocal(t3[:, :, :], t2[:, :, :]))
                step(V.tensor_tensor(g_top[:, :, :], t1[:, :, :], t3[:, :, :], ALU.mult))

                def first_largest(out, values, largest, n, scratch):
                    step(V.tensor_tensor(out, values, wide(largest, n), ALU.is_equal))
                    step(V.tensor_tensor(out, out, desc[:, 0:n].unsqueeze(1).to_broadcast([P, TT, n]), ALU.mult))
                    step(V.tensor_reduce(scratch[:, :, :], out, AX_X, ALU.max))
                    step(V.tensor_tensor(out, out, wide(scratch, n), ALU.is_equal))

                first_largest(oh_g[:, :, :], g4[:, :, :], t1, 4, t2)
                by_group = lambda t: t[:, :, :].rearrange("p t (g e) -> p t g e", e=8)
                for i in range(TT):
                    own.did(V.tensor_tensor(x32[:, i, :].rearrange("p (g e) -> p g e", e=8),
                                            lg[:, i, 4:36].rearrange("p (g e) -> p g e", e=8),
                                            oh_g[:, i, :].unsqueeze(2).to_broadcast([P, 4, 8]), ALU.mult))
                own.settle()
                step(V.tensor_reduce(sc8[:, :, :].unsqueeze(3), x32[:, :, :].rearrange("p t (g e) -> p t e g", e=8),
                                     AX_X, ALU.add))
                step(V.tensor_reduce(t1[:, :, :], sc8[:, :, :], AX_X, ALU.max))
                V.tensor_tensor(e8[:, :, :], sc8[:, :, :], wide(t1, 8), ALU.subtract).then_inc(s["e_in"], 1)
                dve.wait_ge(s["e_out"], 2)
                for i in range(2):
                    step(V.tensor_reduce(top[i][:, :, :], e8[:, :, :], AX_X, ALU.max))
                    first_largest(oh8[i][:, :, :], e8[:, :, :], top[i], 8, t2)
                    if i == 0:
                        step(V.scalar_tensor_tensor(out=e8[:, :, :], in0=oh8[0][:, :, :], scalar=-2.0, in1=e8[:, :, :],
                                                    op0=ALU.mult, op1=ALU.add))
                step(V.tensor_tensor(t1[:, :, :], top[0][:, :, :], top[1][:, :, :], ALU.add))
                step(V.reciprocal(t2[:, :, :], t1[:, :, :]))
                step(V.tensor_tensor(t2[:, :, :], t2[:, :, :], g_top[:, :, :], ALU.mult))
                for i in range(2):
                    step(V.tensor_tensor(r.weight[:, i, :], top[i][:, :, 0], t2[:, :, 0], ALU.mult))
                    for t in range(TT):
                        own.did(V.tensor_tensor(oh[i][:, t, :].rearrange("p (g e) -> p g e", e=8),
                                                oh_g[:, t, :].unsqueeze(2).to_broadcast([P, 4, 8]),
                                                oh8[i][:, t, :].unsqueeze(1).to_broadcast([P, 4, 8]), ALU.mult))
                own.settle()
                step(V.tensor_tensor(x32[:, :, :], oh[0][:, :, :], oh[1][:, :, :], ALU.add))
                V.tensor_tensor(mask[:, :, :], x32[:, :, :], valid[:, :].unsqueeze(2).to_broadcast([P, TT, NE]), ALU.mult)\
                 .then_inc(s["mask"], 1)
                dve.wait_ge(s["rank"], 1)
                step(V.tensor_copy(rank[:, :, :], rk_ps[:, 0:TT, :]))
                step(V.tensor_copy(cnt[:, :], rk_ps[:, TT, :]))
                step(V.tensor_tensor(cmp_n[:, :, :], cnt[:, :].unsqueeze(2).to_broadcast([P, NE, MAXQ]),
                                     full[:, :].unsqueeze(1).to_broadcast([P, NE, MAXQ]), ALU.is_gt))
                step(V.tensor_reduce(nov[:, :].unsqueeze(2), cmp_n[:, :, :], AX_X, ALU.add))
                step(V.tensor_tensor_scan(ovb[:, :], nov[:, :], nov[:, :], 0.0, ALU.add, ALU.bypass))
                step(V.tensor_tensor(cmp_o[:, :, :], block_id[0:1, 0:OVB].unsqueeze(2).to_broadcast([1, OVB, NE]),
                                     ovb[0:1, :].unsqueeze(1).to_broadcast([1, OVB, NE]), ALU.is_ge))
                step(V.tensor_reduce(more_f[:, 1:1 + OVB].unsqueeze(2), cmp_o[:, :, :], AX_X, ALU.add))
                step(V.tensor_scalar(more_f[:, 1:1 + OVB], more_f[:, 1:1 + OVB], float(NE - 1), None, ALU.min))
                step(V.tensor_copy(more_f[:, 0:1], ovb[0:1, NE - 1:NE]))
                step(V.tensor_copy(r.more[:, :], more_f[:, :]))
                step(V.tensor_tensor(ovb[:, :], ovb[:, :], nov[:, :], ALU.subtract))
                for i in range(2):
                    def pick(dst, table):
                        step(V.tensor_tensor(x32[:, :, :], oh[i][:, :, :], table, ALU.mult))
                        step(V.tensor_reduce(dst.unsqueeze(2), x32[:, :, :], AX_X, ALU.add))
                    pick(rk[i][:, :], rank[:, :, :])
                    pick(blk[i][:, :], expert[:, :].unsqueeze(1).to_broadcast([P, TT, NE]))
                    pick(ov[i][:, :], ovb[:, :].unsqueeze(1).to_broadcast([P, TT, NE]))
                    step(V.tensor_tensor(cmp_q[:, :, :], rk[i][:, :].unsqueeze(2).to_broadcast([P, TT, MAXQ]),
                                         full[:, :].unsqueeze(1).to_broadcast([P, TT, MAXQ]), ALU.is_ge))
                    step(V.tensor_reduce(q_[i][:, :].unsqueeze(2), cmp_q[:, :, :], AX_X, ALU.add))
                    step(V.scalar_tensor_tensor(out=row[i][:, :], in0=q_[i][:, :], scalar=-float(CAP), in1=rk[i][:, :],
                                                op0=ALU.mult, op1=ALU.add))
                    step(V.tensor_tensor(ov[i][:, :], ov[i][:, :], q_[i][:, :], ALU.add))
                    step(V.scalar_tensor_tensor(out=ov[i][:, :], in0=ov[i][:, :], scalar=float(NE - 1), in1=blk[i][:, :],
                                                op0=ALU.add, op1=ALU.subtract))
                    step(V.tensor_scalar(q_[i][:, :], q_[i][:, :], 1.0, None, ALU.min))
                    step(V.tensor_tensor(ov[i][:, :], ov[i][:, :], q_[i][:, :], ALU.mult))
                    step(V.tensor_tensor(blk[i][:, :], blk[i][:, :], ov[i][:, :], ALU.add))
                    step(V.scalar_tensor_tensor(out=rk[i][:, :], in0=blk[i][:, :], scalar=float(CAP), in1=row[i][:, :],
                                                op0=ALU.mult, op1=ALU.add))
                    step(V.tensor_copy(r.slot[:, i, :], rk[i][:, :]))
                for n in range(2 * TT):
                    t, i = n // 2, n % 2
                    if n >= 2:
                        dve.wait_ge(s["slots"], n - 1)
                    own.did(V.tensor_scalar(row_hot[:, i, :], row_id[:, :], row[i][:, t:t + 1], None, ALU.is_equal))
                    own.settle()
                    V.tensor_scalar(blk_hot[:, i, :], block_id[:, :], blk[i][:, t:t + 1], tok_id[:, t:t + 1],
                                    ALU.is_equal, ALU.mult).then_inc(s["pair"], 1)
                dve.wait_ge(s["slots"], 2 * TT)
                step(V.tensor_scalar(none[:, :], sl_ps[:, :], 0.0, BIG, ALU.is_equal, ALU.mult))
                step(V.scalar_tensor_tensor(out=slot_f[:, :], in0=sl_ps[:, :], scalar=-1.0, in1=none[:, :],
                                            op0=ALU.add, op1=ALU.add))
                step(V.tensor_copy(r.tok[:, :], slot_f[:, :]))


class Experts:

    SLOTS = 4

    def __init__(self, k, layer, ctx):
        self.layer = layer
        self.gu = [k.sb(f"ex{layer}_gu{b}", [P, 2, KT, DE], ctx=ctx) for b in range(self.SLOTS)]
        self.dn = [k.sb(f"ex{layer}_dn{b}", [P, 2, D], ctx=ctx) for b in range(self.SLOTS)]
        self.w = [k.sem(f"ex{layer}_w{b}") for b in range(self.SLOTS)]

    def load(self, k, sp, b, e, ready):
        one = lambda w: w[self.layer][bass.ds(e, 1), :, :]
        sp.dma_start(self.gu[b][:, 0, :, :], one(k.io["moe_w_gate"]).rearrange("a (p j) f -> p (a j f)", p=P))\
          .then_inc(ready, 16)
        sp.dma_start(self.gu[b][:, 1, :, :], one(k.io["moe_w_up"]).rearrange("a (p j) f -> p (a j f)", p=P))\
          .then_inc(ready, 16)
        sp.dma_start(self.dn[b][:, :, :], one(k.io["moe_w_down"]).rearrange("a (m p) d -> p (a m) d", p=P))\
          .then_inc(ready, 16)


def phase_experts(k, layer, r, ex):
    nc, io = k.nc, k.io
    nm = f"ex{layer}_"
    S = ex.SLOTS
    with ExitStack() as ctx:
        sb = lambda n, shape, dt=F32: k.sb(nm + n, shape, dt, ctx=ctx)
        hg = [sb(f"hg{b}", [CAP, D]) for b in range(2)]
        he = [sb(f"he{b}", [P, KT, CAP]) for b in range(2)]
        sg = sb("sg", [P, P])
        hid = sb("hid", [P, P])
        hid_t = sb("hid_t", [P, P])
        yo = [sb(f"yo{b}", [P, 512]) for b in range(2)]
        tr_ps = [k.ps(f"{nm}trps{b}", [P, KT, CAP], ctx) for b in range(2)]
        gu_ps = k.ps(f"{nm}gups", [P, 2, P], ctx)
        ht_ps = k.ps(f"{nm}htps", [P, P], ctx)
        y_ps = [k.ps(f"{nm}yps{b}", [P, 512], ctx) for b in range(2)]

        def block_programs(pass_name, rounds, first, load_slot, preloaded, w_ready):
            sems = {n: k.sem(f"{nm}{pass_name}{n}") for n in ("tr", "he", "gu", "sg", "hid", "htp", "ht", "y", "yo")}
            g = [k.sem(f"{nm}{pass_name}g{b}") for b in range(2)]
            st = [k.sem(f"{nm}{pass_name}st{b}") for b in range(2)]

            def sync_program(sp):
                if not preloaded:
                    for b in range(S):
                        load_slot(sp, b, b)
                if rounds > 1:
                    with sp.Fori(0, rounds - 1) as i:
                        for b in range(S):
                            sp.wait_ge(sems["y"], i * S + (b + 1))
                            load_slot(sp, b, i * S + (S + b))

            def pool_program(pool):
                for n in range(S * rounds):
                    if n >= 2:
                        pool.wait_ge(sems["tr"], n - 1)
                        pool.wait_ge(g[n % 2], 16 * (n // 2))
                    nc.gpsimd.indirect_dma_start(out=hg[n % 2][:, :], out_offset=None, in_=k.h_rows,
                                                 in_offset=bass.IndirectOffsetOnAxis(
                                                     ap=r.tok[:, first + n:first + n + 1], axis=0),
                                                 bounds_check=T - 1, oob_is_err=False).then_inc(g[n % 2], 16)

            def tensor_program(pe):
                with pe.Fori(0, rounds) as i:
                    for b in range(S):
                        p = b % 2
                        pe.wait_ge(g[p], i * (8 * S) + 16 * (b // 2 + 1))
                        nc.tensor.matmul(tr_ps[p][:, 0, :], hg[p][:, 0::KT], k.ident[0:CAP, 0:CAP], start=True, stop=True)
                        for j in range(1, KT):
                            last = nc.tensor.transpose(tr_ps[p][:, j, :], hg[p][:, j::KT], k.ident[0:CAP, 0:CAP])
                        last.then_inc(sems["tr"], 1)
                        pe.wait_ge(w_ready[b], i * 48 + 48)
                        pe.wait_ge(sems["he"], i * S + (b + 1))
                        for j in range(KT):
                            for q in range(2):
                                last = nc.tensor.matmul(gu_ps[64 * q:64 * q + 64, :, :], he[p][:, j, :],
                                                        ex.gu[b][:, :, j, q * P:(q + 1) * P],
                                                        start=(j == 0), stop=(j == KT - 1), skip_group_check=True)
                        last.then_inc(sems["gu"], 1)
                        pe.wait_ge(sems["hid"], i * S + (b + 1))
                        nc.tensor.transpose(ht_ps[:, :], hid[:, :], k.ident[:, :]).then_inc(sems["htp"], 1)
                        pe.wait_ge(sems["yo"], i * S + (b + 1))
                        pe.wait_ge(sems["ht"], i * S + (b + 1))
                        for m in range(2):
                            for n in range(2):
                                last = nc.tensor.matmul(y_ps[p][64 * n:64 * n + 64, :], hid_t[:, m * CAP:(m + 1) * CAP],
                                                        ex.dn[b][:, m, n * 512:(n + 1) * 512],
                                                        start=(m == 0), stop=(m == 1), skip_group_check=True)
                        last.then_inc(sems["y"], 1)

            def vector_program(dve):
                with dve.Fori(0, rounds) as i:
                    for b in range(S):
                        dve.wait_ge(sems["tr"], i * S + (b + 1))
                        nc.vector.tensor_copy(he[b % 2][:, :, :], tr_ps[b % 2][:, :, :]).then_inc(sems["he"], 1)
                        dve.wait_ge(sems["sg"], i * S + (b + 1))
                        nc.vector.tensor_tensor(hid[:, :], sg[:, :], gu_ps[:, 1, :], ALU.mult).then_inc(sems["hid"], 1)
                        dve.wait_ge(sems["htp"], i * S + (b + 1))
                        nc.vector.tensor_copy(hid_t[:, :], ht_ps[:, :]).then_inc(sems["ht"], 1)

            def scalar_program(act):
                act.sem_inc(sems["yo"], 1)
                for b in range(2):
                    act.sem_inc(st[b], 32)
                with act.Fori(0, rounds) as i:
                    for b in range(S):
                        p = b % 2
                        act.wait_ge(sems["gu"], i * S + (b + 1))
                        nc.scalar.activation(sg[:, :], gu_ps[:, 0, :], ACT.Silu).then_inc(sems["sg"], 1)
                        act.wait_ge(sems["y"], i * S + (b + 1))
                        act.wait_ge(st[p], i * (16 * S) + 32 * (b // 2 + 1))
                        nc.scalar.activation(yo[p][:, :], y_ps[p][:, :], ACT.Copy).then_inc(sems["yo"], 1)
                        act.wait_ge(sems["yo"], i * S + (b + 2))
                        for n in range(2):
                            act.dma_start(k.y_rows[bass.ds(i * (S * CAP) + (first + b) * CAP, CAP), n * 512:(n + 1) * 512],
                                          yo[p][64 * n:64 * n + 64, :]).then_inc(st[p], 16)
                for b in range(2):
                    act.wait_ge(st[b], 16 * S * rounds + 32)

            return sync_program, tensor_program, vector_program, scalar_program, pool_program

        main = block_programs("a", NE // S, 0, lambda sp, b, n: ex.load(k, sp, b, n, ex.w[b]), True, ex.w)
        rows_clear = k.sem(nm + "rows_clear")
        with nc.Block() as block:
            @block.vector
            def _(dve):
                for b in range(2):
                    nc.vector.memset(hg[b][:, :], 0.0).then_inc(rows_clear, 1)
                main[2](dve)

            @block.sync
            def _(sp):
                main[0](sp)

            @block.tensor
            def _(pe):
                main[1](pe)

            @block.scalar
            def _(act):
                main[3](act)

            @block.gpsimd
            def _(pool):
                pool.wait_ge(rows_clear, 2)
                main[4](pool)

        w_more = [k.sem(f"{nm}w_more{b}") for b in range(S)]

        def load_more(sp, b, n):
            e = sp.value_load(r.more[0:1, bass.ds(n + 1, 1)], min_val=0, max_val=NE - 1)
            ex.load(k, sp, b, e, w_more[b])

        more = block_programs("b", OVB // S, NE, load_more, False, w_more)

        def when_more(eng, program):
            n = eng.value_load(r.more[0:1, 0:1], min_val=0, max_val=OVB)
            with eng.If(n > 0):
                program(eng)

        with nc.Block() as block:
            @block.sync
            def _(sp):
                when_more(sp, more[0])

            @block.tensor
            def _(pe):
                when_more(pe, more[1])

            @block.vector
            def _(dve):
                when_more(dve, more[2])

            @block.scalar
            def _(act):
                when_more(act, more[3])

            @block.gpsimd
            def _(pool):
                when_more(pool, more[4])


def phase_combine(k, layer, r):
    nc = k.nc
    nm = f"co{layer}_"
    g, sc, sm, tr, ev, own_d = (k.sem(nm + n) for n in ("g", "sc", "sm", "tr", "ev", "own"))
    with ExitStack() as ctx:
        y = k.sb(nm + "y", [P, 2, 2, D], ctx=ctx)
        res = k.sb(nm + "res", [P, KT, T], ctx=ctx)
        ps = k.ps(nm + "ps", [P, KT, P], ctx)
        with nc.Block() as block:
            @block.gpsimd
            def _(pool):
                for t, (a, m) in enumerate(TOK):
                    if t >= 2:
                        pool.wait_ge(tr, t - 1)
                    for i in range(2):
                        nc.gpsimd.indirect_dma_start(out=y[0:m, t % 2, i, :], out_offset=None, in_=k.y_rows,
                                                     in_offset=bass.IndirectOffsetOnAxis(ap=r.slot[0:m, i, t:t + 1],
                                                                                         axis=0),
                                                     bounds_check=NBLK * CAP - 1, oob_is_err=False).then_inc(g, 16)
                    pool.wait_ge(g, 32 * (t + 1))

            @block.scalar
            def _(act):
                for t, (a, m) in enumerate(TOK):
                    act.wait_ge(g, 32 * (t + 1))
                    nc.scalar.activation(y[0:m, t % 2, 0, :], y[0:m, t % 2, 0, :], ACT.Copy,
                                         scale=r.weight[0:m, 0, t:t + 1]).then_inc(sc, 1)

            @block.vector
            def _(dve):
                for t, (a, m) in enumerate(TOK):
                    dve.wait_ge(g, 32 * (t + 1))
                    dve.wait_ge(sc, t + 1)
                    nc.vector.scalar_tensor_tensor(out=y[0:m, t % 2, 0, :], in0=y[0:m, t % 2, 1, :],
                                                   scalar=r.weight[0:m, 1, t:t + 1], in1=y[0:m, t % 2, 0, :],
                                                   op0=ALU.mult, op1=ALU.add).then_inc(sm, 1)
                    dve.wait_ge(tr, t + 1)
                    nc.vector.tensor_copy(res[:, :, a:a + m], ps[:, :, 0:m]).then_inc(ev, 1)
                dve.wait_ge(ev, TT)

            @block.tensor
            def _(pe):
                for t, (a, m) in enumerate(TOK):
                    pe.wait_ge(sm, t + 1)
                    if t:
                        pe.wait_ge(ev, t)
                    for j in range(KT):
                        last = nc.tensor.transpose(ps[:, j, 0:m], y[0:m, t % 2, 0, j * P:(j + 1) * P],
                                                   k.ident[0:m, 0:m])
                    last.then_inc(tr, 1)
        phase_residual(k, nm, res, layer * 48 + 5 * KT)


def moe(k, layer):
    with ExitStack() as ctx:
        r = Routing(k, ctx, layer)
        with ExitStack() as c:
            ex = Experts(k, layer, c)
            phase_route(k, layer, r, ex)
            phase_experts(k, layer, r, ex)
        phase_combine(k, layer, r)


def build(nc, io):
    with ExitStack() as ctx:
        k = Trunk(nc, ctx, io)
        k.h_rows = nc.dram_tensor("h_rows", (T, D), F32).ap()
        k.y_rows = nc.dram_tensor("y_rows", (NBLK * CAP, D), F32).ap()
        with ExitStack() as c:
            k.cT = k.sb("cT_sb", [P, KT, NC9], ctx=c)
            phase_constants(k)
            phase_ada(k, 0)
            phase_ada(k, 1)
        phase_norm(k, "n0", 0, 0)
        with ExitStack() as c0:
            mixT = k.sb("mixT", [P, 2 * KT, T], ctx=c0)
            with ExitStack() as c:
                k.qk = k.sb("qk", [P, 2 * KT, T], ctx=c)
                k.qT, k.kT = k.qk[:, 0:KT, :], k.qk[:, KT:2 * KT, :]
                flat = lambda tile: by_half(k.qk[:, bass.ds(tile, 1), :].rearrange("p a t -> p (a t)"))
                rhs = lambda j, h: k.hT[:, j, h * HALF:(h + 1) * HALF]
                for nm, col, first, scale in (("q", 2576, 0, HD ** -0.5), ("kk", 3600, KT, 1.0)):
                    phase_project(k, nm, io["mix_w_in"][:, col:col + D], KT, 4, rhs, T,
                                  lambda e, tile, ps, n, first=first, scale=scale: nc.vector.tensor_scalar(
                                      flat(tile + first), ps, scale, None, ALU.mult),
                                  lambda e, tile, ps, n, first=first, scale=scale: nc.scalar.activation(
                                      flat(tile + first), ps, ACT.Copy, scale=scale), None, None)
                with ExitStack() as cv:
                    vtok = k.sb("vtok", [P, TT, D], ctx=cv)
                    phase_value(k, vtok)
                    phase_attention_prompt(k, vtok, mixT)
                phase_attention_sample(k, mixT)
            k.recycle()
            with ExitStack() as c:
                zs = k.sb("zs", [P, KT, T], ctx=c)
                xc = k.sb("xc", [P, XT, T], ctx=c)
                dt_tok = k.sb("dt_tok", [P, TT, H], ctx=c)
                phase_ssd_project(k, xc, zs, dt_tok)
                phase_ssd(k, xc, mixT, dt_tok)
                phase_gated_norm(k, zs, mixT)
            phase_out_project(k, "out0", io["mix_w_out"], 2 * KT, mixT, 0, 2)
        k.recycle()
        phase_norm(k, "n1", 0, 3)
        moe(k, 0)
        k.recycle()
        phase_norm(k, "n2", 1, 0)
        with ExitStack() as c:
            gT = k.sb("gT", [P, KT, T], ctx=c)
            with ExitStack() as c1:
                proj = k.sb("sc_proj", [P, 3 * KT, T], ctx=c1)
                flat = lambda tile: by_half(proj[:, bass.ds(tile, 1), :].rearrange("p a t -> p (a t)"))
                phase_project(k, "sc", io["sc_w_in"], KT, 12, lambda j, h: k.hT[:, j, h * HALF:(h + 1) * HALF], T,
                              lambda e, tile, ps, n: nc.vector.tensor_copy(flat(tile), ps),
                              lambda e, tile, ps, n: nc.scalar.activation(flat(tile), ps, ACT.Copy), None, None)
                phase_short_conv(k, proj, gT)
            phase_out_project(k, "out1", io["sc_w_out"], KT, gT, 1, 2)
        k.recycle()
        phase_norm(k, "n3", 1, 3)
        moe(k, 1)
        phase_norm(k, "n4", None, 0)


def kernel(x_prompt, x_sample, c_prompt, c_sample, state_ssm, state_ssd_conv, cache_k, cache_v, page_table,
           state_short_conv, ada_w, ada_b, ln_mix_g, ln_ffn_g, mix_w_in, mix_w_out, ssd_conv_w, ssd_conv_b,
           ssd_dt_bias, ssd_a_log, ssd_d, ssd_norm_g, sb_bias, sc_w_in, sc_conv_w, sc_w_out, moe_w_group,
           moe_b_group, moe_w_router, moe_b_router, moe_w_gate, moe_w_up, moe_w_down, final_g):
    import numpy as np
    import concourse.bacc as bacc
    from concourse.bass_utils import run_bass_kernel_spmd as run

    def arr(a):
        return np.asarray(a)

    def feature(a):
        a = arr(a)
        a = a.reshape(-1, a.shape[-1] // P, P)
        return a.transpose(2, 0, 1).reshape(P, -1)

    def row(a):
        return np.broadcast_to(arr(a).reshape(1, -1), (P, arr(a).size))

    small = np.concatenate([
        feature(ada_b), feature(ln_mix_g), feature(ln_ffn_g), feature(final_g[None]), feature(ssd_conv_w[0]),
        feature(ssd_conv_b), np.repeat(arr(ssd_d)[0], HD).reshape(KT, P).T, feature(ssd_norm_g),
        feature(sc_conv_w[0]), row(ssd_dt_bias), row(ssd_a_log), row(sb_bias),
        row(np.concatenate([arr(moe_b_group), arr(moe_b_router)], axis=1))], axis=1)
    assert small.shape == (P, N_SMALL)
    inputs = {
        "xT": np.concatenate([arr(x_prompt)[0], arr(x_sample).reshape(TS, D)], axis=0).T,
        "cT": np.concatenate([arr(c_prompt), arr(c_sample)], axis=0).T,
        "small": small,
        "ssm_state": arr(state_ssm)[0].transpose(3, 0, 1, 2).reshape(NS, NB, D),
        "conv_state": arr(state_ssd_conv)[0].reshape(NB, 3, XT, P).transpose(3, 2, 0, 1),
        "sc_state": arr(state_short_conv)[0].reshape(NB, 2, KT, P).transpose(3, 2, 0, 1),
        "cache_kT": arr(cache_k)[0].reshape(POOL_PAGES, PAGE, KT, P).transpose(0, 3, 2, 1).reshape(POOL_PAGES, P, D),
        "cache_v": arr(cache_v)[0].reshape(POOL_PAGES, PAGE, D),
        "page_table": arr(page_table).reshape(1, NB * PAGES),
        "ada_w": arr(ada_w), "mix_w_in": arr(mix_w_in)[0], "mix_w_out": arr(mix_w_out)[0],
        "sc_w_in": arr(sc_w_in)[0], "sc_w_out": arr(sc_w_out)[0],
        "w_route": np.concatenate([arr(moe_w_group), arr(moe_w_router)], axis=2),
        "moe_w_gate": arr(moe_w_gate), "moe_w_up": arr(moe_w_up), "moe_w_down": arr(moe_w_down),
    }
    inputs = {n: np.ascontiguousarray(a) for n, a in inputs.items()}
    outputs = {"yT": (D, T), "ssm_p": (NS, D), "ssm_s": (NS, NB, D), "conv_out": (P, XT, 3 + TS),
               "kT": (P, KT, T), "v": (T, D), "sc_out": (P, KT, 2 + TS)}
    nc = bacc.Bacc("TRN2", target_bir_lowering=False, num_devices=1)
    io = {n: nc.dram_tensor("in_" + n, a.shape, mybir.dt.from_np(a.dtype), kind="ExternalInput").ap()
          for n, a in inputs.items()}
    io.update({n: nc.dram_tensor("out_" + n, shape, F32, kind="ExternalOutput").ap() for n, shape in outputs.items()})
    build(nc, io)
    r = run(nc, [{"in_" + n: a for n, a in inputs.items()}], core_ids=[0]).results[0]
    r = {n: r["out_" + n] for n in outputs}

    y = r["yT"].T
    conv = r["conv_out"].transpose(2, 1, 0).reshape(3 + TS, XT * P)
    kk = r["kT"].transpose(2, 1, 0).reshape(T, D)
    sc = r["sc_out"].transpose(2, 1, 0).reshape(2 + TS, D)
    c = np.ascontiguousarray
    return (c(y[:TP]).reshape(1, TP, D), c(y[TP:]).reshape(NB, NQ, D),
            c(r["ssm_p"].reshape(NS, H, HD).transpose(1, 2, 0))[None, None],
            c(r["ssm_s"].reshape(NS, NB, H, HD).transpose(1, 2, 3, 0))[None],
            c(conv[:3])[None, None], c(conv[3:].reshape(NB, NQ, XT * P)[:, 1:])[None],
            c(kk[:TP]).reshape(1, 1, TP, H, HD), c(kk[TP:]).reshape(1, NB, NQ, H, HD),
            c(r["v"][:TP]).reshape(1, 1, TP, H, HD), c(r["v"][TP:]).reshape(1, NB, NQ, H, HD),
            c(sc[:2])[None, None], c(sc[2:].reshape(NB, NQ, D)[:, 2:])[None])
```

```python
from contextlib import ExitStack

import concourse.bass as bass
from concourse import mybir

F32 = mybir.dt.float32
I32 = mybir.dt.int32
ALU = mybir.AluOpType
ACT = mybir.ActivationFunctionType
AX_X = mybir.AxisListType.X

P = 128
D = 1024
KT = D // P
TP = 512
NB, NQ = 8, 4
TS = NB * NQ
T = TP + TS
HALF = T // 2
TT = 5
TOK = [(i * P, P) for i in range(4)] + [(TP, TS)]
NC9 = 1 + NB
H, HD = 16, 64
NS = 128
XT = 12
PAGES, PAGE = 4, 128
POOL_PAGES = 40
NE, DE = 32, 256
CAP = 64
OVB = -(-((2 * T - 1) // CAP) // 4) * 4
NBLK = NE + OVB
MAXQ = (T - 1) // CAP
EPS = 1e-6
BIG = 1.0e6
NO_DECAY = -1.0e4

COLS = {}
_at = 0
for _name, _n in (("ada_b", 96), ("ln_mix", 16), ("ln_ffn", 16), ("final_g", 8), ("conv_w", 48), ("conv_b", 12),
                  ("d_skip", 8), ("norm_g", 8), ("sc_w", 24), ("dt_bias", 16), ("a_log", 16), ("sb_bias", 16),
                  ("router_b", 72), ("sb_rows", 1), ("before", NQ), ("own_head", 8)):
    COLS[_name] = (_at, _at + _n)
    _at += _n
N_SMALL = _at


class Chain:

    def __init__(self, eng, sem):
        self.eng, self.sem, self.n = eng, sem, 0

    def did(self, ins):
        ins.then_inc(self.sem, 1)
        self.n += 1
        return ins

    def settle(self):
        if self.n:
            self.eng.wait_ge(self.sem, self.n)

    def step(self, ins):
        self.did(ins)
        self.settle()


class Trunk:

    def __init__(self, nc, ctx, io):
        self.nc, self.ctx, self.io = nc, ctx, io
        self.phase_sems = []
        sb = self.sb
        self.xT = sb("xT", [P, KT, T])
        self.hT = sb("hT", [P, KT, T])
        self.mod = sb("mod", [P, 96, NC9])
        self.small = sb("small", [P, N_SMALL])
        self.ident = sb("ident", [P, P])
        self.ones = sb("ones", [P, P])
        self.neg_ones = sb("neg_ones", [P, P])
        self.neg_tri = sb("neg_tri", [P, P])
        self.tri_le = sb("tri_le", [P, P])
        self.tri_lt = sb("tri_lt", [P, P])
        self.same = sb("same", [TS, TS])
        self.tri_same = sb("tri_same", [TS, TS])
        self.member = sb("member", [TS, NB])
        self.w_ready = [self.sem(f"w_ready{b}") for b in range(2)]
        self.mm_done = [[self.sem(f"mm_done{b}{t}") for t in range(2)] for b in range(2)]
        self.ps_free = [[self.sem(f"ps_free{b}{t}") for t in range(2)] for b in range(2)]
        self.phase_sems = []
        self.rounds = 0

    def sb(self, name, shape, dt=F32, ctx=None):
        return (ctx or self.ctx).enter_context(self.nc.sbuf_tensor(name, shape, dt))

    def ps(self, name, shape, ctx):
        return ctx.enter_context(self.nc.psum_tensor(name, shape, F32))

    def sem(self, name):
        one = self.nc.alloc_semaphore(name=name)
        self.phase_sems.append(one)
        return one

    def recycle(self):
        self.nc.clear_and_free_semaphores(self.phase_sems)
        self.nc.all_engine_barrier()
        self.phase_sems = []

    def col(self, name, i, n=1):
        a = COLS[name][0] + i
        return self.small[:, a:a + n]

    def mod_tiles(self, layer, chunk):
        a = layer * 48 + chunk * KT
        return self.mod[:, a:a + KT, :]


def phase_constants(k, ada):
    nc, io = k.nc, k.io
    cT = k.cT
    loaded, made, cond_ready = k.sem("loaded"), k.sem("made"), k.sem("cond_ready")
    zeroed, cleared, padded = k.sem("zeroed"), k.sem("cleared"), k.sem("padded")
    zero_rows = k.hT[:, :, :].rearrange("p k t -> p (k t)")[:, 0:D]
    with nc.Block() as block:
        @block.sync
        def _(sp):
            sp.wait_ge(padded, 1)
            sp.dma_start(cT[:, :, 0:NC9], io["cT"].rearrange("(k p) c -> p k c", p=P)).then_inc(loaded, 16)
            sp.dma_start(k.small[:, :], io["small"]).then_inc(loaded, 16)
            for j in range(KT):
                ada.load(sp, 0, 0, j)
            sp.dma_start(k.xT[:, :, :], io["xT"].rearrange("(k p) t -> p k t", p=P)).then_inc(loaded, 16)
            sp.wait_ge(loaded, 48)
            sp.wait_ge(zeroed, 1)
            for i in range(NE * CAP, NBLK * CAP, P):
                sp.dma_start(k.y_rows[i:i + P, :], zero_rows).then_inc(cleared, 16)
            sp.wait_ge(cleared, 16 * (OVB * CAP // P))

        @block.scalar
        def _(act):
            act.wait_ge(loaded, 48)
            nc.scalar.activation(cT[:, :, :], cT[:, :, :], ACT.Silu).then_inc(cond_ready, 1)
            act.wait_ge(cond_ready, 1)

        @block.vector
        def _(dve):
            nc.vector.memset(cT[:, :, :], 0.0).then_inc(padded, 1)
            nc.vector.memset(zero_rows, 0.0).then_inc(zeroed, 1)
            for b in range(2):
                for t in range(2):
                    dve.sem_inc(k.ps_free[b][t], 1)

        @block.gpsimd
        def _(pool):
            own = Chain(pool, made)
            own.did(nc.gpsimd.memset(k.ident[:, :], 0.0))
            own.did(nc.gpsimd.memset(k.ones[:, :], 1.0))
            own.did(nc.gpsimd.memset(k.neg_ones[:, :], -1.0))
            own.did(nc.gpsimd.memset(k.neg_tri[:, :], -1.0))
            own.did(nc.gpsimd.memset(k.tri_le[:, :], 1.0))
            own.did(nc.gpsimd.memset(k.tri_lt[:, :], 1.0))
            own.did(nc.gpsimd.memset(k.same[:, :], 1.0))
            own.did(nc.gpsimd.memset(k.member[:, :], 1.0))
            own.settle()

            def keep(m, pattern, base, mult, op, fill):
                own.did(nc.gpsimd.affine_select(out=m, in_=m, pattern=pattern, base=base, channel_multiplier=mult,
                                                compare_op=op, fill=fill))

            keep(k.ident[:, :], [[-1, P]], 0, 1, ALU.not_equal, 1.0)
            keep(k.neg_tri[:, :], [[-1, P]], 0, 1, ALU.is_ge, 0.0)
            keep(k.tri_le[:, :], [[1, P]], 0, -1, ALU.is_ge, 0.0)
            keep(k.tri_lt[:, :], [[1, P]], 0, -1, ALU.is_gt, 0.0)
            same = k.same[:, :].rearrange("j (b q) -> j b q", q=NQ)
            keep(same, [[-NQ, NB], [0, NQ]], 0, 1, ALU.is_ge, 0.0)
            keep(k.member[:, :], [[-NQ, NB]], 0, 1, ALU.is_ge, 0.0)
            own.settle()
            keep(same, [[NQ, NB], [0, NQ]], NQ - 1, -1, ALU.is_ge, 0.0)
            keep(k.member[:, :], [[NQ, NB]], NQ - 1, -1, ALU.is_ge, 0.0)
            own.settle()
            own.step(nc.gpsimd.tensor_tensor(k.tri_same[:, :], k.same[:, :], k.tri_le[0:TS, 0:TS], ALU.mult))


def phase_project(k, name, w, kt, steps, rhs, width, take_vector, take_scalar):
    nc = k.nc
    halves = 1 if width <= 512 and width != T else 2
    cols = width // halves
    rounds = steps // 2
    base = k.rounds
    with ExitStack() as ctx:
        slots = [k.sb(f"{name}_w{b}", [P, kt, 256], ctx=ctx) for b in range(2)]
        ps = [[k.ps(f"{name}_ps{b}{t}", [P, 2, 512], ctx) for t in range(2)] for b in range(2)]
        w_view = w.rearrange("(k p) n -> p k n", p=P)

        with nc.Block() as block:
            @block.sync
            def _(sp):
                for b in range(2):
                    sp.dma_start(slots[b][:, :, :], w_view[:, :, b * 256:(b + 1) * 256]).then_inc(k.w_ready[b], 16)
                if rounds > 1:
                    with sp.Fori(0, rounds - 1) as i:
                        for b in range(2):
                            sp.wait_ge(k.mm_done[b][1], i + (base + 1))
                            sp.dma_start(slots[b][:, :, :], w_view[:, :, bass.ds(i * 512 + (512 + b * 256), 256)])\
                              .then_inc(k.w_ready[b], 16)

            @block.tensor
            def _(pe):
                with pe.Fori(0, rounds) as i:
                    for b in range(2):
                        pe.wait_ge(k.w_ready[b], i * 16 + 16 * (base + 1))
                        for t in range(2):
                            pe.wait_ge(k.ps_free[b][t], i + (base + 1))
                            for h in range(halves):
                                for j in range(kt):
                                    last = nc.tensor.matmul(ps[b][t][:, h, 0:cols], slots[b][:, j, t * P:(t + 1) * P],
                                                            rhs(j, h), start=(j == 0), stop=(j == kt - 1))
                            last.then_inc(k.mm_done[b][t], 1)

            @block.vector
            def _(dve):
                with dve.Fori(0, rounds) as i:
                    for b in range(2):
                        dve.wait_ge(k.mm_done[b][0], i + (base + 1))
                        take_vector(dve, i * 4 + 2 * b, ps[b][0][:, 0:halves, 0:cols], i * 2 + (b + 1))\
                            .then_inc(k.ps_free[b][0], 1)

            @block.scalar
            def _(act):
                with act.Fori(0, rounds) as i:
                    for b in range(2):
                        act.wait_ge(k.mm_done[b][1], i + (base + 1))
                        take_scalar(act, i * 4 + (2 * b + 1), ps[b][1][:, 0:halves, 0:cols], i * 2 + (b + 1))\
                            .then_inc(k.ps_free[b][1], 1)
    k.rounds += rounds


def by_half(dst):
    return dst.rearrange("p (h t) -> p h t", h=2)


class AdaWeights:
    COLS = 2048
    PARTS = 6 * D // COLS

    def __init__(self, k, ctx):
        self.w = k.sb("ada_w", [P, KT, self.COLS], ctx=ctx)
        self.ready = [k.sem(f"ada_ready{j}") for j in range(KT)]
        self.view = [k.io["ada_w"][layer].rearrange("(k p) n -> p k n", p=P) for layer in range(2)]

    def load(self, sp, layer, part, j):
        sp.dma_start(self.w[:, j, :], self.view[layer][:, j, bass.ds(part * self.COLS, self.COLS)])\
          .then_inc(self.ready[j], 16)


def phase_ada(k, ada):
    nc = k.nc
    used, copied, turned, out, folded = (k.sem("ada_" + n) for n in
                                                 ("used", "copied", "turned", "out", "folded"))
    bias0 = COLS["ada_b"][0]
    tiles = ada.COLS // P
    with ExitStack() as ctx:
        rows = k.sb("ada_rows", [P, 512], ctx=ctx)
        sum_ps = k.ps("ada_sum", [P, 512], ctx)
        turn_ps = k.ps("ada_turn", [P, 4, P], ctx)
        with nc.Block() as block:
            @block.sync
            def _(sp):
                for layer in range(2):
                    first = 1 - layer
                    with sp.Fori(0, ada.PARTS - first) as i:
                        for j in range(KT):
                            sp.wait_ge(used, i * KT + (layer * (ada.PARTS - 1) * KT + j + 1))
                            ada.load(sp, layer, i + first, j)

            @block.tensor
            def _(pe):
                with pe.Fori(0, 2 * ada.PARTS) as i:
                    pe.wait_ge(copied, i + 1)
                    for j in range(KT):
                        pe.wait_ge(ada.ready[j], i * 16 + 16)
                        for g in range(4):
                            last = nc.tensor.matmul(sum_ps[32 * g:32 * g + 32, :], k.cT[:, j, :],
                                                    ada.w[:, j, g * 512:(g + 1) * 512], start=(j == 0),
                                                    stop=(j == KT - 1), skip_group_check=True)
                        last.then_inc(used, 1)
                    pe.wait_ge(copied, i + 2)
                    pe.wait_ge(out, i + 1)
                    for c in range(4):
                        last = nc.tensor.transpose(turn_ps[:, c, :], rows[:, c * P:(c + 1) * P], k.ident[:, :])
                    last.then_inc(turned, 1)

            @block.vector
            def _(dve):
                dve.sem_inc(out, 1)
                with dve.Fori(0, 2 * ada.PARTS) as i:
                    dve.wait_ge(turned, i + 1)
                    nc.vector.tensor_tensor(
                        k.mod[:, bass.ds(i * tiles, tiles), :].rearrange("p (g c) r -> p g c r", g=4),
                        turn_ps[:, :, :].rearrange("p c (g r) -> p g c r", g=4)[:, :, :, 0:NC9],
                        k.small[:, bass.ds(i * tiles + bias0, tiles)].rearrange("p (g c) -> p g c", g=4)
                        .unsqueeze(3).to_broadcast([P, 4, 4, NC9]), ALU.add).then_inc(out, 1)
                dve.wait_ge(out, 2 * ada.PARTS + 1)
                for layer in range(2):
                    for chunk, gain in ((1, "ln_mix"), (4, "ln_ffn")):
                        s = k.mod_tiles(layer, chunk)
                        g = k.col(gain, layer * KT, KT).unsqueeze(2).to_broadcast([P, KT, NC9])
                        nc.vector.scalar_tensor_tensor(out=s, in0=s, scalar=1.0, in1=g, op0=ALU.add, op1=ALU.mult)\
                          .then_inc(folded, 1)
                dve.wait_ge(folded, 4)

            @block.scalar
            def _(act):
                act.sem_inc(copied, 1)
                with act.Fori(0, 2 * ada.PARTS) as i:
                    act.wait_ge(used, i * KT + KT)
                    nc.scalar.activation(rows[:, :], sum_ps[:, :], ACT.Copy).then_inc(copied, 1)


def phase_norm(k, name, layer, chunk):
    nc = k.nc
    squared, summed, root, scaled = (k.sem(f"{name}_{s}") for s in ("squared", "summed", "root", "scaled"))
    root_in, own_d, own_a = (k.sem(f"{name}_{s}") for s in ("root_in", "own_d", "own_a"))
    with ExitStack() as ctx:
        sq = k.sb(f"{name}_sq", [P, 2, T], ctx=ctx)
        rstd = k.sb(f"{name}_rstd", [P, T], ctx=ctx)
        ps = k.ps(f"{name}_ps", [P, 2, 512], ctx)
        with nc.Block() as block:
            @block.scalar
            def _(act):
                for j in range(KT):
                    if j >= 2:
                        act.wait_ge(summed, j - 1)
                    nc.scalar.activation(sq[:, j % 2, :], k.xT[:, j, :], ACT.Square).then_inc(squared, 1)
                act.wait_ge(root_in, 1)
                nc.scalar.activation(rstd[:, :], rstd[:, :], ACT.Sqrt).then_inc(root, 1)
                for j in range(KT):
                    act.wait_ge(scaled, j + 1)
                    if layer is not None:
                        nc.scalar.activation(k.hT[:, j, 0:TP], k.hT[:, j, 0:TP], ACT.Identity,
                                             bias=k.mod[:, layer * 48 + chunk * KT + j, 0:1],
                                             scale=k.mod[:, layer * 48 + (chunk + 1) * KT + j, 0:1]).then_inc(own_a, 1)
                if layer is not None:
                    act.wait_ge(own_a, KT)

            @block.tensor
            def _(pe):
                for j in range(KT):
                    pe.wait_ge(squared, j + 1)
                    for h in range(2):
                        last = nc.tensor.matmul(ps[:, h, 0:HALF], k.ones[:, :], sq[:, j % 2, h * HALF:(h + 1) * HALF],
                                                start=(j == 0), stop=(j == KT - 1))
                    last.then_inc(summed, 1)

            @block.vector
            def _(dve):
                own = Chain(dve, own_d)
                dve.wait_ge(summed, KT)
                nc.vector.tensor_scalar(by_half(rstd[:, :]), ps[:, :, 0:HALF], 1.0 / D, EPS, ALU.mult, ALU.add)\
                  .then_inc(root_in, 1)
                dve.wait_ge(root, 1)
                own.step(nc.vector.reciprocal(rstd[:, :], rstd[:, :]))
                for j in range(KT):
                    if layer is None:
                        nc.vector.scalar_tensor_tensor(out=k.hT[:, j, :], in0=k.xT[:, j, :],
                                                       scalar=k.col("final_g", j), in1=rstd[:, :],
                                                       op0=ALU.mult, op1=ALU.mult).then_inc(scaled, 1)
                    else:
                        nc.vector.tensor_tensor(k.hT[:, j, :], k.xT[:, j, :], rstd[:, :], ALU.mult).then_inc(scaled, 1)
                dve.wait_ge(scaled, KT)
                if layer is not None:
                    hs = k.hT[:, :, TP:T].rearrange("p k (b q) -> p k b q", q=NQ)
                    a = k.mod_tiles(layer, chunk + 1)[:, :, 1:NC9].unsqueeze(3).to_broadcast([P, KT, NB, NQ])
                    s = k.mod_tiles(layer, chunk)[:, :, 1:NC9].unsqueeze(3).to_broadcast([P, KT, NB, NQ])
                    own.step(nc.vector.tensor_tensor(hs, hs, a, ALU.mult))
                    own.step(nc.vector.tensor_tensor(hs, hs, s, ALU.add))

            if layer is None:
                stored = k.sem("y_stored")

                @block.sync
                def _(sp):
                    y = k.io["yT"].rearrange("(k p) t -> p k t", p=P)
                    for j in range(KT):
                        sp.wait_ge(scaled, j + 1)
                        sp.dma_start(y[:, j, :], k.hT[:, j, :]).then_inc(stored, 16)
                    sp.wait_ge(stored, 16 * KT)


def phase_value(k, vtok, qz, kn):
    nc = k.nc
    cleared, kept = k.sem("qz_cleared"), k.sem("qz_kept")
    ready, done, free, stored = k.sem("wv_ready"), k.sem("v_done"), k.sem("v_free"), k.sem("kv_stored")
    with ExitStack() as ctx:
        wv = k.sb("wv", [P, 2, KT, 512], ctx=ctx)
        ps = k.ps("v_ps", [P, 2, 512], ctx)
        w = k.io["mix_w_in"][:, 4624:5648].rearrange("(k p) n -> p k n", p=P)
        with nc.Block() as block:
            @block.sync
            def _(sp):
                for n in range(2):
                    sp.dma_start(wv[:, n, :, :], w[:, :, n * 512:(n + 1) * 512]).then_inc(ready, 16)
                    sp.wait_ge(ready, 16 * (n + 1))
                sp.dma_start(k.io["kT"], k.kT[:, :, :]).then_inc(stored, 16)
                for i, (a, m) in enumerate(TOK):
                    sp.wait_ge(free, 2 * (i + 1))
                    sp.dma_start(k.io["v"][a:a + m, :], vtok[0:m, i, :]).then_inc(stored, 16)
                sp.wait_ge(stored, 16 * (1 + TT))

            @block.tensor
            def _(pe):
                pe.wait_ge(ready, 32)
                for i, (a, m) in enumerate(TOK):
                    for n in range(2):
                        u = 2 * i + n
                        if u >= 2:
                            pe.wait_ge(free, u - 1)
                        for j in range(KT):
                            last = nc.tensor.matmul(ps[0:m, u % 2, :], k.hT[:, j, a:a + m], wv[:, n, j, :],
                                                    start=(j == 0), stop=(j == KT - 1))
                        last.then_inc(done, 1)

            @block.vector
            def _(dve):
                for i, (a, m) in enumerate(TOK):
                    for n in range(2):
                        u = 2 * i + n
                        dve.wait_ge(done, u + 1)
                        nc.vector.tensor_copy(vtok[0:m, i, n * 512:(n + 1) * 512], ps[0:m, u % 2, :]).then_inc(free, 1)

            @block.gpsimd
            def _(pool):
                nc.gpsimd.memset(qz[:, :, :, :], 0.0).then_inc(cleared, 1)

            @block.scalar
            def _(act):
                nc.scalar.activation(kn[:, :, :, :], k.kT[:, :, TP:T].rearrange("p k (b q) -> p k b q", q=NQ),
                                     ACT.Copy).then_inc(kept, 1)
                act.wait_ge(cleared, 1)
                for j in range(KT):
                    for g in range(2):
                        r = slice(64 * g, 64 * g + 64)
                        c = (2 * (j % 4) + g) * NQ
                        nc.scalar.activation(qz[r, j, :, c:c + NQ],
                                             k.qT[r, j, TP:T].rearrange("p (b q) -> p b q", q=NQ), ACT.Copy)\
                          .then_inc(kept, 1)
                act.wait_ge(kept, 1 + 2 * KT)


def phase_attention_prompt(k, vtok, mixT):
    nc = k.nc
    units = [(h, j) for h in range(H) for j in (3, 2, 1, 0)]
    NZ, NSP, NW, LAG = 6, 8, 4, 3
    names = ("z_done", "zb_done", "e_done", "l_done", "sp_done", "spm_done", "cum_done", "w_done", "wm_done",
             "pv_done", "o_done")
    s = {n: k.sem("ap_" + n) for n in names}
    with ExitStack() as ctx:
        zb = k.sb("ap_zb", [P, 3, 512], ctx=ctx)
        sp_t = k.sb("ap_sp", [P, NSP, 512], ctx=ctx)
        w_t = k.sb("ap_w", [P, NW, 512], ctx=ctx)
        z_ps = [k.ps(f"ap_z{i}", [P, 512], ctx) for i in range(NZ)]
        o_ps = [k.ps(f"ap_o{i}", [P, 512], ctx) for i in range(2)]
        n_units = len(units)

        with nc.Block() as block:
            @block.tensor
            def _(pe):
                def scores(u):
                    h, j = units[u]
                    r = slice(64 * (h % 2), 64 * (h % 2) + 64)
                    if u >= NZ:
                        pe.wait_ge(s["w_done"], u - NZ + 1)
                    nc.tensor.matmul(z_ps[u % NZ][:, j * P:512], k.kT[r, h // 2, j * P:(j + 1) * P],
                                     k.qT[r, h // 2, j * P:TP], start=True, stop=False, skip_group_check=True)\
                      .then_inc(s["z_done"], 1)

                def cumulate(u):
                    h, j = units[u]
                    pe.wait_ge(s["spm_done"], u + 1)
                    z = z_ps[u % NZ]
                    last = nc.tensor.matmul(z[:, j * P:512], k.neg_tri[:, :], sp_t[:, u % NSP, j * P:512],
                                            start=False, stop=(j == 3), skip_group_check=True)
                    for back in range(1, 4 - j):
                        jj = j + back
                        last = nc.tensor.matmul(z[:, jj * P:512], k.neg_ones[:, :],
                                                sp_t[:, (u - back) % NSP, jj * P:512],
                                                start=False, stop=(jj == 3), skip_group_check=True)
                    last.then_inc(s["cum_done"], 1)

                def values(u):
                    h, j = units[u]
                    r = slice(64 * (h % 2), 64 * (h % 2) + 64)
                    pe.wait_ge(s["wm_done"], u + 1)
                    if j == 3 and h % 2 == 0 and h >= 4:
                        pe.wait_ge(s["o_done"], h // 2 - 1)
                    nc.tensor.matmul(o_ps[(h // 2) % 2][r, j * P:512], vtok[:, j, h * HD:(h + 1) * HD],
                                     w_t[:, u % NW, j * P:512], start=(j == 3), stop=(j == 0), skip_group_check=True)\
                      .then_inc(s["pv_done"], 1)

                for u in range(n_units + LAG + 2):
                    if u < n_units:
                        scores(u)
                    if LAG <= u < n_units + LAG:
                        cumulate(u - LAG)
                    if u >= LAG + 2:
                        values(u - LAG - 2)

            @block.vector
            def _(dve):
                def bounded(u):
                    h, j = units[u]
                    dve.wait_ge(s["z_done"], u + 1)
                    if u >= 3:
                        dve.wait_ge(s["e_done"], u - 2)
                    nc.vector.tensor_scalar(zb[:, u % 3, j * P:512], z_ps[u % NZ][:, j * P:512],
                                            k.col("sb_bias", h), 40.0, ALU.add, ALU.min).then_inc(s["zb_done"], 1)

                def softplus(u):
                    h, j = units[u]
                    dve.wait_ge(s["l_done"], u + 1)
                    nc.vector.scalar_tensor_tensor(out=sp_t[:, u % NSP, j * P:512], in0=z_ps[u % NZ][:, j * P:512],
                                                   scalar=k.col("sb_bias", h), in1=sp_t[:, u % NSP, j * P:512],
                                                   op0=ALU.add, op1=ALU.max).then_inc(s["sp_done"], 1)

                def output(pair):
                    dve.wait_ge(s["pv_done"], 8 * (pair + 1))
                    nc.vector.tensor_copy(mixT[:, KT + pair, 0:TP], o_ps[pair % 2][:, :]).then_inc(s["o_done"], 1)

                for u in range(n_units + 1):
                    if u < n_units:
                        bounded(u)
                    if u >= 1:
                        softplus(u - 1)
                    if u >= 14 and (u - 14) % 8 == 0:
                        output((u - 14) // 8)
                for pair in range((n_units - 14) // 8 + 1, H // 2):
                    output(pair)
                dve.wait_ge(s["o_done"], H // 2)

            @block.scalar
            def _(act):
                nc.scalar.preload_act_table_set("natural_log_exp_and_others")

                def exponential(u):
                    h, j = units[u]
                    act.wait_ge(s["zb_done"], u + 1)
                    if u >= NSP:
                        act.wait_ge(s["cum_done"], (u - NSP) // 4 * 4 + 4)
                    nc.scalar.activation(sp_t[:, u % NSP, j * P:512], zb[:, u % 3, j * P:512], ACT.Exp)\
                      .then_inc(s["e_done"], 1)
                    act.wait_ge(s["e_done"], u + 1)
                    nc.scalar.activation(sp_t[:, u % NSP, j * P:512], sp_t[:, u % NSP, j * P:512], ACT.Ln, bias=1.0)\
                      .then_inc(s["l_done"], 1)

                def weights(u):
                    h, j = units[u]
                    act.wait_ge(s["cum_done"], u + 1)
                    if u >= NW:
                        act.wait_ge(s["pv_done"], u - NW + 1)
                    nc.scalar.activation(w_t[:, u % NW, j * P:512], z_ps[u % NZ][:, j * P:512], ACT.Exp,
                                         bias=k.col("sb_bias", h)).then_inc(s["w_done"], 1)

                for u in range(n_units + LAG):
                    if u < n_units:
                        exponential(u)
                    if u >= LAG:
                        weights(u - LAG)

            @block.gpsimd
            def _(pool):
                def mask(tile, buf, ready, done, u):
                    h, j = units[u]
                    pool.wait_ge(ready, u + 1)
                    d = tile[:, buf, j * P:(j + 1) * P]
                    nc.gpsimd.affine_select(out=d, in_=d, pattern=[[1, P]], base=0, channel_multiplier=-1,
                                            compare_op=ALU.is_gt, fill=0.0).then_inc(done, 1)

                for u in range(n_units + LAG):
                    if u < n_units:
                        mask(sp_t, u % NSP, s["sp_done"], s["spm_done"], u)
                    if u >= LAG:
                        mask(w_t, (u - LAG) % NW, s["w_done"], s["wm_done"], u - LAG)


def phase_attention_sample(k, mixT, qz, kn):
    nc = k.nc
    RING, ROUNDS = 4, NB // 2
    KEYS = PAGES * PAGE
    names = ("table", "zn", "zb", "ln", "sp", "z", "arg", "w", "tr", "wt", "pv", "masked", "oc", "turn",
             "out", "own_d", "nb", "ne", "narg", "nw", "ntr", "nwt", "e_own")
    s = {n: k.sem("as_" + n) for n in names}
    arrived = [k.sem(f"as_slot{r}") for r in range(RING)]
    vn_ready = [k.sem(f"as_vn{r}") for r in range(2)]
    order = [("k", 0), ("k", 1)]
    for t in range(ROUNDS):
        order.append(("v", t))
        if t + 2 < ROUNDS:
            order.append(("k", t + 2))
    place = {what: n for n, what in enumerate(order)}
    with ExitStack() as ctx:
        pages = k.sb("as_pages", [P, RING, PAGES, D], ctx=ctx)
        vn = k.sb("as_vn", [NQ, 2, 2, D], ctx=ctx)
        table = k.sb("as_table", [1, NB * PAGES], I32, ctx=ctx)
        zb = k.sb("as_zb", [P, 2, KEYS], ctx=ctx)
        sp_t = k.sb("as_sp", [P, 2, 1 + KEYS], ctx=ctx)
        cum = k.sb("as_cum", [P, 2, 1 + KEYS], ctx=ctx)
        w_t = k.sb("as_w", [P, 2, KEYS], ctx=ctx)
        wT = k.sb("as_wT", [P, 2, PAGES, P], ctx=ctx)
        om = k.sb("as_om", [P, 8, HD], ctx=ctx)
        oc = k.sb("as_oc", [P, 2, HD], ctx=ctx)
        z_n = k.sb("as_zn_sb", [P, ROUNDS, NQ], ctx=ctx)
        sp_n = k.sb("as_sp_n", [P, ROUNDS, NQ], ctx=ctx)
        w_n = k.sb("as_w_n", [P, ROUNDS, NQ], ctx=ctx)
        wT_n = k.sb("as_wT_n", [NQ, ROUNDS, P], ctx=ctx)
        z_ps = [k.ps(f"as_z{i}", [P, KEYS], ctx) for i in range(2)]
        zn_ps = k.ps("as_znps", [P, 512], ctx)
        tr_ps = k.ps("as_tr", [P, PAGES, P], ctx)
        o_ps = [k.ps(f"as_o{i}", [P, 512], ctx) for i in range(2)]
        turn_ps = k.ps("as_turn", [P, 2, 8, 2, NQ], ctx)
        bias = k.col("sb_rows", 0)

        def groups():
            return [(slice(32 * (2 * bb + o), 32 * (2 * bb + o) + 32), bb, 4 * o) for bb in range(2) for o in range(2)]

        with nc.Block() as block:
            @block.sync
            def _(sp):
                sp.dma_start(table[:, :], k.io["page_table"]).then_inc(s["table"], 16)
                sp.wait_ge(s["table"], 16)
                for n, (kind, t) in enumerate(order):
                    if n >= 2:
                        was, wt = order[n - 2]
                        sp.wait_ge(s["z"] if was == "k" else s["pv"], wt + 1)
                    for bb in range(2):
                        b, r = 2 * t + bb, 2 * (n % 2) + bb
                        for p in range(PAGES):
                            page = sp.value_load(table[0:1, b * PAGES + p:b * PAGES + p + 1], min_val=0,
                                                 max_val=POOL_PAGES - 1)
                            src = k.io["cache_kT"] if kind == "k" else k.io["cache_v"]
                            sp.dma_start(pages[:, r, PAGES - 1 - p, :],
                                         src[bass.ds(page, 1), :, :].rearrange("a p n -> p (a n)"))\
                              .then_inc(arrived[r], 16)
                        if kind == "v":
                            if t >= 2:
                                sp.wait_ge(s["pv"], t - 1)
                            sp.dma_start(vn[:, t % 2, bb, :], k.io["v"][TP + NQ * b:TP + NQ * (b + 1), :])\
                              .then_inc(vn_ready[t % 2], 16)

            @block.tensor
            def _(pe):
                def arrive(what):
                    n = place[what]
                    for bb in range(2):
                        pe.wait_ge(arrived[2 * (n % 2) + bb], 16 * PAGES * (n // 2 + 1))
                    return 2 * (n % 2)

                for t in range(ROUNDS):
                    for j in range(4):
                        for r, bb, j0 in groups():
                            last = nc.tensor.matmul(zn_ps[r, t * NQ:(t + 1) * NQ], qz[:, j0 + j, 2 * t + bb, :],
                                                    kn[:, j0 + j, 2 * t + bb, :], start=(j == 0), stop=(j == 3),
                                                    skip_group_check=True)
                last.then_inc(s["zn"], 1)

                def scores(t):
                    if t >= 2:
                        pe.wait_ge(s["arg"], t - 1)
                    slot = arrive(("k", t))
                    for j in range(4):
                        for r, bb, j0 in groups():
                            last = nc.tensor.matmul(z_ps[t % 2][r, :], qz[:, j0 + j, 2 * t + bb, :],
                                                    pages[:, slot + bb, :, (j0 + j) * P:(j0 + j + 1) * P],
                                                    start=(j == 0), stop=(j == 3), skip_group_check=True)
                    last.then_inc(s["z"], 1)

                def turned_weights(t):
                    pe.wait_ge(s["w"], t + 1)
                    if t >= 1:
                        pe.wait_ge(s["wt"], t)
                    for p in range(PAGES):
                        last = nc.tensor.transpose(tr_ps[:, p, :], w_t[:, t % 2, p * P:(p + 1) * P], k.ident[:, :])
                    last.then_inc(s["tr"], 1)

                def sums(t):
                    pe.wait_ge(s["wt"], t + 1)
                    slot = arrive(("v", t))
                    pe.wait_ge(vn_ready[t % 2], 32 * (t // 2 + 1))
                    if t >= 2:
                        pe.wait_ge(s["masked"], t - 1)
                    for p in range(PAGES):
                        for r, bb, j0 in groups():
                            nc.tensor.matmul(o_ps[t % 2][r, :], wT[:, t % 2, p, r], pages[:, slot + bb, p, j0 * P:(j0 + 4) * P],
                                             start=(p == 0), stop=False, skip_group_check=True)
                    for r, bb, j0 in groups():
                        last = nc.tensor.matmul(o_ps[t % 2][r, :], wT_n[:, t, r], vn[:, t % 2, bb, j0 * P:(j0 + 4) * P],
                                                start=False, stop=True, skip_group_check=True)
                    last.then_inc(s["pv"], 1)

                def turned_sums(t):
                    pe.wait_ge(s["oc"], t + 1)
                    if t >= 1:
                        pe.wait_ge(s["out"], 2 * t)
                    nc.tensor.transpose(turn_ps[:, :, :, :, :].rearrange("p b j g q -> p (b j g q)"),
                                        oc[:, :, :].rearrange("p d e -> p (d e)"), k.ident[:, :]).then_inc(s["turn"], 1)

                scores(0)
                pe.wait_ge(s["nw"], 2)
                for t in range(ROUNDS):
                    last = nc.tensor.transpose(zn_ps[0:NQ, t * P:(t + 1) * P], w_n[:, t, :], k.ident[:, :])
                last.then_inc(s["ntr"], 1)
                pe.wait_ge(s["nwt"], 1)
                for t in range(ROUNDS):
                    if t + 1 < ROUNDS:
                        scores(t + 1)
                    turned_weights(t)
                    sums(t)
                    if t >= 1:
                        turned_sums(t - 1)
                turned_sums(ROUNDS - 1)

            @block.vector
            def _(dve):
                own = Chain(dve, s["own_d"])
                V = nc.vector
                before = k.col("before", 0, NQ).unsqueeze(1).to_broadcast([P, ROUNDS, NQ])
                dve.wait_ge(s["zn"], 1)
                own.step(V.tensor_scalar(z_n[:, :, :], zn_ps[:, 0:ROUNDS * NQ].rearrange("p (t n) -> p t n", n=NQ),
                                         bias, None, ALU.add))
                V.tensor_scalar(sp_n[:, :, :], z_n[:, :, :], 40.0, None, ALU.min).then_inc(s["nb"], 1)
                dve.wait_ge(s["ne"], 1)
                own.step(V.tensor_tensor(sp_n[:, :, :], sp_n[:, :, :], z_n[:, :, :], ALU.max))
                own.step(V.tensor_tensor(sp_n[:, :, :], sp_n[:, :, :], before, ALU.mult))
                for n in (2, 1, 0):
                    own.step(V.tensor_tensor(sp_n[:, :, n], sp_n[:, :, n], sp_n[:, :, n + 1], ALU.add))
                own.step(V.tensor_tensor(z_n[:, :, :], z_n[:, :, :], sp_n[:, :, :], ALU.subtract))
                V.tensor_scalar(w_n[:, :, :], z_n[:, :, :], 40.0, None, ALU.min).then_inc(s["narg"], 1)
                dve.wait_ge(s["nw"], 1)
                V.tensor_tensor(w_n[:, :, :], w_n[:, :, :], before, ALU.mult).then_inc(s["nw"], 1)

                def bounded(t):
                    dve.wait_ge(s["z"], t + 1)
                    if t >= 2:
                        dve.wait_ge(s["ln"], t - 1)
                    V.tensor_scalar(zb[:, t % 2, :], z_ps[t % 2][:, :], bias, 40.0, ALU.add, ALU.min)\
                     .then_inc(s["zb"], 1)

                def running(t):
                    own.did(V.tensor_copy(sp_t[:, t % 2, 0:1], sp_n[:, t, 0:1]))
                    dve.wait_ge(s["ln"], t + 1)
                    own.did(V.scalar_tensor_tensor(out=sp_t[:, t % 2, 1:1 + KEYS], in0=z_ps[t % 2][:, :], scalar=bias,
                                                   in1=sp_t[:, t % 2, 1:1 + KEYS], op0=ALU.add, op1=ALU.max))
                    own.settle()
                    own.step(V.tensor_tensor_scan(cum[:, t % 2, :], sp_t[:, t % 2, :], sp_t[:, t % 2, :], 0.0, ALU.add,
                                                  ALU.bypass))
                    if t >= 2:
                        dve.wait_ge(s["tr"], t - 1)
                    V.scalar_tensor_tensor(out=w_t[:, t % 2, :], in0=z_ps[t % 2][:, :], scalar=bias,
                                           in1=cum[:, t % 2, 1:1 + KEYS], op0=ALU.add, op1=ALU.subtract)\
                     .then_inc(s["arg"], 1)

                def result(t):
                    dve.wait_ge(s["pv"], t + 1)
                    V.tensor_tensor(om[:, :, :], o_ps[t % 2][:, :].rearrange("p (h e) -> p h e", e=HD),
                                    k.col("own_head", 0, 8).unsqueeze(2).to_broadcast([P, 8, HD]), ALU.mult)\
                     .then_inc(s["masked"], 1)
                    dve.wait_ge(s["masked"], t + 1)
                    if t >= 1:
                        dve.wait_ge(s["turn"], t)
                    own.step(V.tensor_reduce(oc[:, 0, :].unsqueeze(2), om[:, :, :].rearrange("p h e -> p e h"), AX_X,
                                             ALU.add))
                    V.tensor_copy(oc[:, 1, :], oc[:, 0, :]).then_inc(s["oc"], 1)
                    dve.wait_ge(s["turn"], t + 1)
                    for g in range(2):
                        r = slice(64 * g, 64 * g + 64)
                        for bb in range(2):
                            a = TP + NQ * (2 * t + bb)
                            ins = V.tensor_copy(mixT[r, KT:2 * KT, a:a + NQ], turn_ps[r, bb, :, g, :])
                        ins.then_inc(s["out"], 1)

                bounded(0)
                for t in range(ROUNDS):
                    running(t)
                    if t + 1 < ROUNDS:
                        bounded(t + 1)
                    if t >= 1:
                        result(t - 1)
                result(ROUNDS - 1)
                dve.wait_ge(s["out"], 2 * ROUNDS)

            @block.scalar
            def _(act):
                nc.scalar.preload_act_table_set("natural_log_exp_and_others")
                own = Chain(act, s["e_own"])
                act.wait_ge(s["nb"], 1)
                own.step(nc.scalar.activation(sp_n[:, :, :], sp_n[:, :, :], ACT.Exp))
                nc.scalar.activation(sp_n[:, :, :], sp_n[:, :, :], ACT.Ln, bias=1.0).then_inc(s["ne"], 1)
                act.wait_ge(s["narg"], 1)
                nc.scalar.activation(w_n[:, :, :], w_n[:, :, :], ACT.Exp).then_inc(s["nw"], 1)
                act.wait_ge(s["ntr"], 1)
                nc.scalar.activation(wT_n[:, :, :].rearrange("n t r -> n (t r)"), zn_ps[0:NQ, :], ACT.Copy)\
                  .then_inc(s["nwt"], 1)

                def softplus(t):
                    act.wait_ge(s["zb"], t + 1)
                    if t >= 2:
                        act.wait_ge(s["arg"], t - 1)
                    own.step(nc.scalar.activation(sp_t[:, t % 2, 1:1 + KEYS], zb[:, t % 2, :], ACT.Exp))
                    nc.scalar.activation(sp_t[:, t % 2, 1:1 + KEYS], sp_t[:, t % 2, 1:1 + KEYS], ACT.Ln, bias=1.0)\
                      .then_inc(s["ln"], 1)

                softplus(0)
                for t in range(ROUNDS):
                    act.wait_ge(s["arg"], t + 1)
                    nc.scalar.activation(w_t[:, t % 2, :], w_t[:, t % 2, :], ACT.Exp).then_inc(s["w"], 1)
                    if t + 1 < ROUNDS:
                        softplus(t + 1)
                    act.wait_ge(s["tr"], t + 1)
                    if t >= 2:
                        act.wait_ge(s["pv"], t - 1)
                    nc.scalar.activation(wT[:, t % 2, :, :], tr_ps[:, :, :], ACT.Copy).then_inc(s["wt"], 1)


def phase_ssd_project(k, xc, zs, dt_tok):
    nc, io = k.nc, k.io

    def z_vector(dve, tile, ps, _):
        return nc.vector.tensor_copy(by_half(zs[:, bass.ds(tile, 1), :].rearrange("p a t -> p (a t)")), ps)

    def z_scalar(act, tile, ps, _):
        return nc.scalar.activation(by_half(zs[:, bass.ds(tile, 1), :].rearrange("p a t -> p (a t)")), ps, ACT.Copy)

    rhs = lambda j, h: k.hT[:, j, h * HALF:(h + 1) * HALF]
    phase_project(k, "z", io["mix_w_in"][:, 0:1024], KT, 4, rhs, T, z_vector, z_scalar)
    phase_project(k, "xbc", io["mix_w_in"][:, 1024:2560], KT, 6, rhs, T,
                  lambda e, tile, ps, n: nc.vector.tensor_copy(
                      by_half(xc[:, bass.ds(tile, 1), :].rearrange("p a t -> p (a t)")), ps),
                  lambda e, tile, ps, n: nc.scalar.activation(
                      by_half(xc[:, bass.ds(tile, 1), :].rearrange("p a t -> p (a t)")), ps, ACT.Copy))

    loaded, state_kept, conv_done, act_done, stored = (k.sem("cv_" + n) for n in
                                                       ("loaded", "kept", "conv", "act", "stored"))
    zsil, own_d, padded, dt_mm, u_done, l_done, dt_done = (k.sem("cv_" + n) for n in
                                                           ("zsil", "own_d", "pad", "dtmm", "u", "l", "dt"))
    with ExitStack() as ctx:
        buf = k.sb("cv_buf", [P, XT, NB, 3], ctx=ctx)
        kept = k.sb("cv_kept", [P, XT, 3 + TS], ctx=ctx)
        raw_p = k.sb("cv_rawp", [P, 2, 3 + TP], ctx=ctx)
        raw_s = k.sb("cv_raws", [P, 2, NB, 3 + NQ], ctx=ctx)
        w_dt = k.sb("cv_wdt", [P, KT, H], ctx=ctx)
        u = k.sb("cv_u", [P, TT, H], ctx=ctx)
        w1 = k.sb("cv_w1", [P, TT, H], ctx=ctx)
        dt_ln = k.sb("cv_ln", [P, TT, H], ctx=ctx)
        dt_ps = k.ps("cv_dtps", [P, TT, H], ctx)
        with nc.Block() as block:
            @block.sync
            def _(sp):
                sp.dma_start(buf[:, :, :, :], io["conv_state"]).then_inc(loaded, 16)
                sp.dma_start(w_dt[:, :, :], io["mix_w_in"][:, 2560:2576].rearrange("(k p) n -> p k n", p=P))\
                  .then_inc(loaded, 16)
                sp.wait_ge(state_kept, 2)
                sp.dma_start(io["conv_out"], kept[:, :, :]).then_inc(stored, 16)
                sp.wait_ge(stored, 16)

            @block.tensor
            def _(pe):
                pe.wait_ge(loaded, 32)
                for i, (a, m) in enumerate(TOK):
                    for j in range(KT):
                        last = nc.tensor.matmul(dt_ps[0:m, i, :], k.hT[:, j, a:a + m], w_dt[:, j, :],
                                                start=(j == 0), stop=(j == KT - 1))
                last.then_inc(dt_mm, 1)

            @block.vector
            def _(dve):
                own = Chain(dve, own_d)
                own.did(nc.vector.memset(raw_p[:, :, 0:3], 0.0))
                own.did(nc.vector.memset(u[:, :, :], 0.0))
                nc.vector.tensor_copy(kept[:, :, 0:3], xc[:, :, TP - 3:TP]).then_inc(state_kept, 1)
                nc.vector.tensor_copy(kept[:, :, 3:3 + TS], xc[:, :, TP:T]).then_inc(state_kept, 1)
                dve.wait_ge(loaded, 32)
                own.settle()
                dve.wait_ge(state_kept, 2)
                for i in range(XT):
                    b = i % 2
                    own.did(nc.vector.tensor_copy(raw_p[:, b, 3:3 + TP], xc[:, i, 0:TP]))
                    own.did(nc.vector.tensor_copy(raw_s[:, b, :, 3:3 + NQ],
                                                  xc[:, i, TP:T].rearrange("p (b q) -> p b q", q=NQ)))
                    own.did(nc.vector.tensor_copy(raw_s[:, b, :, 0:3], buf[:, i, :, :]))
                    own.settle()
                    xs = xc[:, i, TP:T].rearrange("p (b q) -> p b q", q=NQ)
                    own.did(nc.vector.tensor_scalar(xc[:, i, 0:TP], raw_p[:, b, 0:TP], k.col("conv_w", i), None,
                                                    ALU.mult))
                    own.did(nc.vector.tensor_scalar(xs, raw_s[:, b, :, 0:NQ], k.col("conv_w", i), None, ALU.mult))
                    own.settle()
                    for t in range(1, 4):
                        w = k.col("conv_w", t * XT + i)
                        a = nc.vector.scalar_tensor_tensor(out=xc[:, i, 0:TP], in0=raw_p[:, b, t:t + TP], scalar=w,
                                                           in1=xc[:, i, 0:TP], op0=ALU.mult, op1=ALU.add)
                        own.did(a)
                        c = nc.vector.scalar_tensor_tensor(out=xs, in0=raw_s[:, b, :, t:t + NQ], scalar=w, in1=xs,
                                                           op0=ALU.mult, op1=ALU.add)
                        if t < 3:
                            own.did(c)
                            own.settle()
                    c.then_inc(conv_done, 1)
                    dve.wait_ge(conv_done, i + 1)
                    own.settle()
                dve.wait_ge(dt_mm, 1)
                bias = k.small[:, COLS["dt_bias"][0]:COLS["dt_bias"][1]]
                own.step(nc.vector.tensor_tensor(u[:, 0:4, :], dt_ps[:, 0:4, :],
                                                 bias.unsqueeze(1).to_broadcast([P, 4, H]), ALU.add))
                own.step(nc.vector.tensor_tensor(u[0:TS, 4, :], dt_ps[0:TS, 4, :], bias[0:TS, :], ALU.add))
                own.step(nc.vector.tensor_scalar(dt_tok[:, :, :], u[:, :, :], 0.0, None, ALU.max))
                own.step(nc.vector.tensor_scalar(w1[:, :, :], u[:, :, :], -1.0, None, ALU.mult))
                nc.vector.tensor_tensor(u[:, :, :], u[:, :, :], w1[:, :, :], ALU.min).then_inc(u_done, 1)
                dve.wait_ge(l_done, 1)
                nc.vector.tensor_scalar(w1[:, :, :], u[:, :, :], 1.0, None, ALU.add).then_inc(u_done, 1)
                dve.wait_ge(l_done, 2)
                lnw = dt_ln
                own.step(nc.vector.tensor_scalar(w1[:, :, :], w1[:, :, :], 1.0, 1.0e-30, ALU.subtract, ALU.max))
                own.step(nc.vector.reciprocal(w1[:, :, :], w1[:, :, :]))
                own.step(nc.vector.tensor_tensor(w1[:, :, :], w1[:, :, :], u[:, :, :], ALU.mult))
                own.step(nc.vector.tensor_tensor(w1[:, :, :], w1[:, :, :], lnw[:, :, :], ALU.mult))
                own.step(nc.vector.tensor_scalar(lnw[:, :, :], u[:, :, :], -0.5, 1.0, ALU.mult, ALU.add))
                own.step(nc.vector.tensor_tensor(u[:, :, :], u[:, :, :], lnw[:, :, :], ALU.mult))
                own.step(nc.vector.tensor_tensor(w1[:, :, :], w1[:, :, :], u[:, :, :], ALU.max))
                own.step(nc.vector.tensor_tensor(dt_tok[:, :, :], dt_tok[:, :, :], w1[:, :, :], ALU.add))

            @block.scalar
            def _(act):
                for i in range(KT):
                    nc.scalar.activation(zs[:, i, :], zs[:, i, :], ACT.Silu).then_inc(zsil, 1)
                for i in range(XT):
                    act.wait_ge(conv_done, i + 1)
                    nc.scalar.activation(xc[:, i, :], xc[:, i, :], ACT.Silu, bias=k.col("conv_b", i))\
                      .then_inc(act_done, 1)
                nc.scalar.preload_act_table_set("natural_log_exp_and_others")
                act.wait_ge(u_done, 1)
                nc.scalar.activation(u[:, :, :], u[:, :, :], ACT.Exp).then_inc(l_done, 1)
                act.wait_ge(u_done, 2)
                nc.scalar.activation(dt_ln[:, :, :], w1[:, :, :], ACT.Ln).then_inc(l_done, 1)
                act.wait_ge(zsil, KT)
                act.wait_ge(act_done, XT)


def phase_ssd(k, xc, mixT, dt_tok):
    nc, io = k.nc, k.io
    names = ("tr", "trc", "dA", "ac_mm", "ac_ev", "aexp", "own_d", "xdt", "xw", "bm", "cb", "cbc", "bc", "seg",
             "kept", "decx", "e", "m", "cs", "y", "yo", "st_mm", "st", "sload", "sst", "own_p", "decayed", "sst_done",
             "st_own")
    s = {n: k.sem("ss_" + n) for n in names}
    UNITS = 4 * TT
    with ExitStack() as ctx:
        x_tok = k.sb("x_tok", [P, 2, D], ctx=ctx)
        b_tok = k.sb("b_tok", [P, 2, 2 * NS], ctx=ctx)
        xdt = k.sb("xdt", [P, 2, D], ctx=ctx)
        dA = k.sb("dA", [P, TT, H], ctx=ctx)
        neg_a = k.sb("neg_a", [P, H], ctx=ctx)
        nacum = k.sb("nacum", [P, TT, H], ctx=ctx)
        to_end = k.sb("to_end", [P, TT, H], ctx=ctx)
        cd = k.sb("cd", [P, 4, H], ctx=ctx)
        cds = k.sb("cds", [P, NB, H], ctx=ctx)
        dAm = k.sb("dAm", [TS, NB, H], ctx=ctx)
        bm = k.sb("bm", [TS, NB, 2 * NS], ctx=ctx)
        cbs = k.sb("cbs", [P, 2, 2, P], ctx=ctx)
        dec = k.sb("dec", [P, 3, 4, P], ctx=ctx)
        e_t = k.sb("e_t", [P, 3, 4, P], ctx=ctx)
        st = k.sb("st", [P, 2, D], ctx=ctx)
        sst = k.sb("sst", [P, NB, D], ctx=ctx)
        ac_ps = k.ps("ss_acps", [P, 512], ctx)
        tr_ps = k.ps("ss_trps", [P, 512], ctx)
        bc_ps = [k.ps(f"ss_bc{i}", [P, 4, P], ctx) for i in range(2)]
        y_ps = [k.ps(f"ss_y{i}", [P, 2, P], ctx) for i in range(2)]
        st_ps = [k.ps(f"ss_st{i}", [P, 512], ctx) for i in range(2)]
        GROUPS = ((0, 4), (4, 8), (8, 10))

        def tri(c):
            return k.tri_le[:, :] if c < 4 else k.tri_same[:, :]

        with nc.Block() as block:
            @block.sync
            def _(sp):
                sp.dma_start(sst[:, :, :], io["ssm_state"]).then_inc(s["sload"], 16)
                sp.wait_ge(s["st"], 4)
                sp.dma_start(io["ssm_p"], st[:, 1, :]).then_inc(s["sst"], 16)
                for b in range(NB):
                    sp.wait_ge(s["sst_done"], b + 1)
                    sp.dma_start(io["ssm_s"][:, b, :], sst[:, b, :]).then_inc(s["sst"], 16)
                sp.wait_ge(s["sst"], 16 * (1 + NB))

            @block.tensor
            def _(pe):
                pe.wait_ge(s["dA"], 2)
                for c, (a, n) in enumerate(TOK):
                    nc.tensor.matmul(ac_ps[0:n, c * H:(c + 1) * H], tri(c), dA[0:n, c, :], start=True, stop=True)
                for c in range(4):
                    nc.tensor.matmul(ac_ps[:, 80 + c * H:80 + (c + 1) * H], k.ones[:, :], dA[:, c, :],
                                     start=True, stop=True)
                nc.tensor.matmul(ac_ps[0:TS, 144:160], k.same[:, :], dA[0:TS, 4, :], start=True, stop=True)
                nc.tensor.matmul(ac_ps[:, 160:288], k.ones[0:TS, :], dAm[:, :, :], start=True, stop=True)\
                  .then_inc(s["ac_mm"], 1)

                def turn(c, part):
                    a, n = TOK[c]
                    if part < 3:
                        if 3 * c + part:
                            pe.wait_ge(s["trc"], 3 * c + part)
                        g0, g1 = GROUPS[part]
                        for i in range(g0, g1):
                            last = nc.tensor.transpose(tr_ps[0:n, (i - g0) * P:(i - g0 + 1) * P], xc[:, i, a:a + n],
                                                       k.ident[:, :])
                        last.then_inc(s["tr"], 1)
                    if part == 2:
                        if c == 0:
                            pe.wait_ge(s["ac_ev"], 1)
                        else:
                            pe.wait_ge(s["cbc"], c)
                        for g in range(2):
                            last = nc.tensor.matmul(ac_ps[0:n, 256 + g * P:256 + g * P + n], xc[:, 8 + g, a:a + n],
                                                    xc[:, 10 + g, a:a + n], start=True, stop=True)
                        last.then_inc(s["cb"], 1)

                def broadcast_sums(u):
                    c, n = u // 4, TOK[u // 4][1]
                    if u >= 2:
                        pe.wait_ge(s["seg"], u - 1)
                        pe.wait_ge(s["e"], u - 1)
                    for h in range(4):
                        last = nc.tensor.matmul(bc_ps[u % 2][:, h, 0:n],
                                                dA[0:n, c, 4 * (u % 4) + h:4 * (u % 4) + h + 1].to_broadcast([n, P]),
                                                tri(c), start=True, stop=True)
                    last.then_inc(s["bc"], 1)

                def outputs(u):
                    c, q = u // 4, u % 4
                    n = TOK[c][1]
                    pe.wait_ge(s["m"], u + 1)
                    pe.wait_ge(s["cs"], u + 1)
                    if u >= 2:
                        pe.wait_ge(s["yo"], u - 1)
                    if 1 <= c < 4:
                        pe.wait_ge(s["st"], c)
                    if u == 16:
                        pe.wait_ge(s["sload"], 16)
                    for h in (0, 2, 1, 3):
                        r = slice(64 * (h % 2), 64 * (h % 2) + 64)
                        hh = 4 * q + h
                        f = slice(hh * HD, (hh + 1) * HD)
                        last = nc.tensor.matmul(y_ps[u % 2][r, h // 2, 0:n], xdt[0:n, c % 2, f],
                                                dec[0:n, u % 3, h, 0:n], start=True, stop=(c == 0),
                                                skip_group_check=True)
                        if 1 <= c < 4:
                            last = nc.tensor.matmul(y_ps[u % 2][r, h // 2, 0:n], st[:, (c - 1) % 2, f],
                                                    e_t[:, u % 3, h, 0:n], start=False, stop=True,
                                                    skip_group_check=True)
                        if c == 4:
                            for b in range(NB):
                                last = nc.tensor.matmul(y_ps[u % 2][r, h // 2, NQ * b:NQ * (b + 1)],
                                                        sst[:, b, f], e_t[:, u % 3, h, NQ * b:NQ * (b + 1)],
                                                        start=False, stop=(b == NB - 1), skip_group_check=True)
                    last.then_inc(s["y"], 1)

                def state_product(c):
                    pe.wait_ge(s["xw"], c + 1)
                    if c >= 1:
                        pe.wait_ge(s["st"], c)
                    for g in range(2):
                        last = nc.tensor.matmul(st_ps[g][:, :], b_tok[:, c % 2, g * NS:(g + 1) * NS],
                                                x_tok[:, c % 2, g * 512:(g + 1) * 512], start=True, stop=True)
                    last.then_inc(s["st_mm"], 1)

                for part in range(3):
                    turn(0, part)
                for i in range(UNITS + 2):
                    if i < UNITS:
                        broadcast_sums(i)
                    if i < UNITS - 4:
                        turn(i // 4 + 1, i % 4)
                    if i >= 2:
                        outputs(i - 2)
                    if i % 4 == 3 and i // 4 < 4:
                        state_product(i // 4)
                pe.wait_ge(s["bm"], NB)
                pe.wait_ge(s["xw"], TT)
                for b in range(NB):
                    for g in range(2):
                        if b == 0:
                            pe.wait_ge(s["st"], 4)
                        else:
                            pe.wait_ge(s["st_own"], 2 * b + g - 1)
                        nc.tensor.matmul(st_ps[g][:, :], bm[:, b, g * NS:(g + 1) * NS],
                                         x_tok[0:TS, 0, g * 512:(g + 1) * 512], start=True, stop=True)\
                          .then_inc(s["st_mm"], 1)

            @block.vector
            def _(dve):
                own = Chain(dve, s["own_d"])
                dve.wait_ge(s["aexp"], 1)
                own.step(nc.vector.tensor_scalar(neg_a[:, :], neg_a[:, :], -1.0, None, ALU.mult))
                nc.vector.tensor_tensor(dA[:, :, :], dt_tok[:, :, :], neg_a[:, :].unsqueeze(1).to_broadcast([P, TT, H]),
                                        ALU.mult).then_inc(s["dA"], 1)
                dve.wait_ge(s["dA"], 1)
                nc.vector.tensor_tensor(dAm[:, :, :], dA[0:TS, 4, :].unsqueeze(1).to_broadcast([TS, NB, H]),
                                        k.member[:, :].unsqueeze(2).to_broadcast([TS, NB, H]), ALU.mult)\
                  .then_inc(s["dA"], 1)
                dve.wait_ge(s["ac_mm"], 1)
                own.did(nc.vector.memset(nacum[:, :, :], 0.0))
                own.did(nc.vector.memset(to_end[:, :, :], 0.0))
                own.settle()
                ac = ac_ps[:, 0:80].rearrange("p (c h) -> p c h", h=H)
                en = ac_ps[:, 80:144].rearrange("p (c h) -> p c h", h=H)
                own.did(nc.vector.tensor_scalar(nacum[:, 0:4, :], ac[:, 0:4, :], -1.0, None, ALU.mult))
                own.did(nc.vector.tensor_scalar(nacum[0:TS, 4, :], ac[0:TS, 4, :], -1.0, None, ALU.mult))
                own.settle()
                own.did(nc.vector.tensor_tensor(to_end[:, 0:4, :], en, nacum[:, 0:4, :], ALU.add))
                own.did(nc.vector.tensor_tensor(to_end[0:TS, 4, :], ac_ps[0:TS, 144:160], nacum[0:TS, 4, :], ALU.add))
                own.did(nc.vector.tensor_copy(cd[:, :, :], en))
                own.did(nc.vector.tensor_copy(cds[:, :, :], ac_ps[:, 160:288].rearrange("p (b h) -> p b h", h=H)))
                own.settle()
                dve.sem_inc(s["ac_ev"], 1)

                def prepare(c, part):
                    a, n = TOK[c]
                    xt = x_tok[0:n, c % 2, :].rearrange("p (h e) -> p h e", e=HD)
                    xd = xdt[0:n, c % 2, :].rearrange("p (h e) -> p h e", e=HD)
                    if part == 2:
                        dve.wait_ge(s["trc"], 3 * c + 2)
                        if c >= 2:
                            dve.wait_ge(s["y"], 4 * (c - 1))
                        nc.vector.tensor_tensor(xd, xt, dt_tok[0:n, c, :].unsqueeze(2).to_broadcast([n, H, HD]),
                                                ALU.mult).then_inc(s["xdt"], 1)
                    if part == 3:
                        dve.wait_ge(s["xdt"], c + 1)
                        if c == 0:
                            dve.wait_ge(s["aexp"], 4)
                        nc.vector.tensor_tensor(xt, xd, to_end[0:n, c, :].unsqueeze(2).to_broadcast([n, H, HD]),
                                                ALU.mult).then_inc(s["xw"], 1)
                        dve.wait_ge(s["cb"], c + 1)
                        if c >= 2:
                            dve.wait_ge(s["m"], 4 * (c - 1))
                        nc.vector.tensor_copy(cbs[0:n, c % 2, :, 0:n],
                                              ac_ps[0:n, 256:512].rearrange("p (g l) -> p g l", g=2)[:, :, 0:n])\
                          .then_inc(s["cbc"], 1)

                def segment(u):
                    c, q, n = u // 4, u % 4, TOK[u // 4][1]
                    dve.wait_ge(s["e"], u + 1)
                    if u >= 3:
                        dve.wait_ge(s["y"], u - 2)
                    nc.vector.tensor_tensor(dec[0:n, u % 3, :, 0:n], bc_ps[u % 2][0:n, :, 0:n],
                                            nacum[0:n, c, 4 * q:4 * q + 4].unsqueeze(2).to_broadcast([n, 4, n]),
                                            ALU.add).then_inc(s["seg"], 1)

                def weigh(u):
                    c, q, n = u // 4, u % 4, TOK[u // 4][1]
                    dve.wait_ge(s["decx"], u + 1)
                    dve.wait_ge(s["cbc"], c + 1)
                    nc.vector.tensor_tensor(dec[0:n, u % 3, :, 0:n], dec[0:n, u % 3, :, 0:n],
                                            cbs[0:n, c % 2, q // 2, 0:n].unsqueeze(1).to_broadcast([n, 4, n]),
                                            ALU.mult).then_inc(s["m"], 1)

                def skip(u):
                    c, q = u // 4, u % 4
                    a, n = TOK[c]
                    dve.wait_ge(s["y"], u + 1)
                    for i in range(2):
                        j = 2 * q + i
                        ins = nc.vector.scalar_tensor_tensor(out=mixT[:, j, a:a + n], in0=xc[:, j, a:a + n],
                                                             scalar=k.col("d_skip", j), in1=y_ps[u % 2][:, i, 0:n],
                                                             op0=ALU.mult, op1=ALU.add)
                        if i == 0:
                            own.did(ins)
                        else:
                            ins.then_inc(s["yo"], 1)

                def state(c):
                    dve.wait_ge(s["st_mm"], c + 1)
                    if c >= 1:
                        if c >= 2:
                            dve.wait_ge(s["y"], 4 * c)
                        own.step(nc.vector.tensor_tensor(
                            st[:, c % 2, :].rearrange("p (h e) -> p h e", e=HD),
                            st[:, (c - 1) % 2, :].rearrange("p (h e) -> p h e", e=HD),
                            cd[:, c, :].unsqueeze(2).to_broadcast([P, H, HD]), ALU.mult))
                    for g in range(2):
                        f = slice(g * 512, (g + 1) * 512)
                        if c == 0:
                            ins = nc.vector.tensor_copy(st[:, 0, f], st_ps[g][:, :])
                        else:
                            ins = nc.vector.tensor_tensor(st[:, c % 2, f], st[:, c % 2, f], st_ps[g][:, :], ALU.add)
                        own.did(ins)
                    own.settle()
                    dve.sem_inc(s["st"], 1)

                prepare(0, 2)
                prepare(0, 3)
                for i in range(UNITS + 3):
                    if i < UNITS:
                        segment(i)
                    if 1 <= i < UNITS + 1:
                        weigh(i - 1)
                    if i >= 3:
                        skip(i - 3)
                    if i < UNITS - 4:
                        prepare(i // 4 + 1, i % 4)
                    if i % 4 == 0 and 4 <= i <= 16:
                        state(i // 4 - 1)
                    if i == 16:
                        for b in range(NB):
                            nc.vector.tensor_scalar(bm[:, b, :], b_tok[0:TS, 0, :], k.member[:, b:b + 1], None,
                                                    ALU.mult).then_inc(s["bm"], 1)
                for b in range(NB):
                    dve.wait_ge(s["decayed"], b + 1)
                    for g in range(2):
                        f = slice(g * 512, (g + 1) * 512)
                        dve.wait_ge(s["st_mm"], 4 + 2 * b + g + 1)
                        nc.vector.tensor_tensor(sst[:, b, f], sst[:, b, f], st_ps[g][:, :], ALU.add)\
                          .then_inc(s["st_own"], 1)
                    dve.wait_ge(s["st_own"], 2 * b + 2)
                    dve.sem_inc(s["sst_done"], 1)
                own.settle()
                dve.wait_ge(s["yo"], UNITS)

            @block.scalar
            def _(act):
                nc.scalar.activation(neg_a[:, :], k.small[:, COLS["a_log"][0]:COLS["a_log"][1]], ACT.Exp)\
                  .then_inc(s["aexp"], 1)

                def keep(c, part):
                    n = TOK[c][1]
                    if c >= 2 and part == 0:
                        act.wait_ge(s["st_mm"], c - 1)
                    g0, g1 = GROUPS[part]
                    act.wait_ge(s["tr"], 3 * c + part + 1)
                    dst = x_tok[0:n, c % 2, g0 * P:g1 * P] if part < 2 else b_tok[0:n, c % 2, :]
                    nc.scalar.activation(dst, tr_ps[0:n, 0:(g1 - g0) * P], ACT.Copy).then_inc(s["trc"], 1)

                for part in range(2):
                    keep(0, part)
                act.wait_ge(s["ac_ev"], 1)
                nc.scalar.activation(to_end[:, :, :], to_end[:, :, :], ACT.Exp).then_inc(s["aexp"], 1)
                nc.scalar.activation(cd[:, :, :], cd[:, :, :], ACT.Exp).then_inc(s["aexp"], 1)
                nc.scalar.activation(cds[:, :, :], cds[:, :, :], ACT.Exp).then_inc(s["aexp"], 1)
                keep(0, 2)
                for i in range(UNITS + 1):
                    if i < UNITS:
                        n = TOK[i // 4][1]
                        act.wait_ge(s["bc"], i + 1)
                        if i >= 3:
                            act.wait_ge(s["y"], i - 2)
                        nc.scalar.activation(e_t[:, i % 3, :, 0:n], bc_ps[i % 2][:, :, 0:n], ACT.Exp)\
                          .then_inc(s["e"], 1)
                    if i < UNITS - 4 and i % 4 < 3:
                        keep(i // 4 + 1, i % 4)
                    if i >= 1:
                        u = i - 1
                        n = TOK[u // 4][1]
                        act.wait_ge(s["kept"], u + 1)
                        d = dec[0:n, u % 3, :, 0:n]
                        nc.scalar.activation(d, d, ACT.Exp).then_inc(s["decx"], 1)
                act.wait_ge(s["decx"], UNITS)

            @block.gpsimd
            def _(pool):
                own = Chain(pool, s["own_p"])
                for i in range(UNITS + 1):
                    if i < UNITS:
                        n = TOK[i // 4][1]
                        pool.wait_ge(s["seg"], i + 1)
                        d = dec[0:n, i % 3, :, 0:n]
                        ins = nc.gpsimd.affine_select(out=d, in_=d, pattern=[[0, 4], [1, n]], base=0,
                                                      channel_multiplier=-1, compare_op=ALU.is_ge, fill=NO_DECAY)
                        if i >= 16:
                            own.step(ins)
                            d = d.rearrange("p h (b q) -> p h b q", q=NQ)
                            ins = nc.gpsimd.affine_select(out=d, in_=d, pattern=[[0, 4], [-NQ, NB], [0, NQ]], base=0,
                                                          channel_multiplier=1, compare_op=ALU.is_ge, fill=NO_DECAY)
                        ins.then_inc(s["kept"], 1)
                        pool.wait_ge(s["kept"], i + 1)
                    if i >= 1:
                        u = i - 1
                        q, (a, n) = u % 4, TOK[u // 4]
                        pool.wait_ge(s["e"], u + 1)
                        nc.gpsimd.tensor_tensor(e_t[:, u % 3, :, 0:n], e_t[:, u % 3, :, 0:n],
                                                xc[:, 10 + q // 2, a:a + n].unsqueeze(1).to_broadcast([P, 4, n]),
                                                ALU.mult).then_inc(s["cs"], 1)
                        pool.wait_ge(s["cs"], u + 1)
                pool.wait_ge(s["y"], UNITS)
                for b in range(NB):
                    sv = sst[:, b, :].rearrange("p (h e) -> p h e", e=HD)
                    nc.gpsimd.tensor_tensor(sv, sv, cds[:, b, :].unsqueeze(2).to_broadcast([P, H, HD]), ALU.mult)\
                      .then_inc(s["decayed"], 1)
                    pool.wait_ge(s["decayed"], b + 1)


def phase_gated_norm(k, zs, mixT):
    nc = k.nc
    gated, squared, summed, root_in, root, done, own_d = (k.sem("gn_" + n) for n in
                                                          ("gated", "sq", "sum", "ri", "root", "done", "own"))
    with ExitStack() as ctx:
        sq = k.sb("gn_sq", [P, 2, T], ctx=ctx)
        rstd = k.sb("gn_rstd", [P, 2, T], ctx=ctx)
        ps = k.ps("gn_ps", [P, 4, 512], ctx)
        with nc.Block() as block:
            @block.vector
            def _(dve):
                own = Chain(dve, own_d)
                for j in range(KT):
                    nc.vector.tensor_tensor(mixT[:, j, :], mixT[:, j, :], zs[:, j, :], ALU.mult).then_inc(gated, 1)
                for g in range(2):
                    dve.wait_ge(summed, 4 * (g + 1))
                    nc.vector.tensor_scalar(by_half(rstd[:, g, :]), ps[:, 2 * g:2 * g + 2, 0:HALF], 2.0 / D, EPS,
                                            ALU.mult, ALU.add).then_inc(root_in, 1)
                for g in range(2):
                    dve.wait_ge(root, g + 1)
                    own.step(nc.vector.reciprocal(rstd[:, g, :], rstd[:, g, :]))
                dve.wait_ge(gated, KT)
                dve.wait_ge(squared, KT)
                for j in range(KT):
                    nc.vector.scalar_tensor_tensor(out=mixT[:, j, :], in0=mixT[:, j, :], scalar=k.col("norm_g", j),
                                                   in1=rstd[:, j // 4, :], op0=ALU.mult, op1=ALU.mult).then_inc(done, 1)
                dve.wait_ge(done, KT)

            @block.scalar
            def _(act):
                for j in range(KT):
                    act.wait_ge(gated, j + 1)
                    if j >= 2:
                        act.wait_ge(summed, j - 1)
                    nc.scalar.activation(sq[:, j % 2, :], mixT[:, j, :], ACT.Square).then_inc(squared, 1)
                for g in range(2):
                    act.wait_ge(root_in, g + 1)
                    nc.scalar.activation(rstd[:, g, :], rstd[:, g, :], ACT.Sqrt).then_inc(root, 1)

            @block.tensor
            def _(pe):
                for j in range(KT):
                    pe.wait_ge(squared, j + 1)
                    for h in range(2):
                        last = nc.tensor.matmul(ps[:, 2 * (j // 4) + h, 0:HALF], k.ones[:, :],
                                                sq[:, j % 2, h * HALF:(h + 1) * HALF],
                                                start=(j % 4 == 0), stop=(j % 4 == 3))
                    last.then_inc(summed, 1)


def phase_out_project(k, name, w, kt, src, layer, chunk):
    nc = k.nc
    m0 = layer * 48 + chunk * KT
    with ExitStack() as ctx:
        res = k.sb(f"{name}_res", [P, KT, T], ctx=ctx)

        def flat(tile):
            return by_half(res[:, bass.ds(tile, 1), :].rearrange("p a t -> p (a t)"))

        phase_project(k, name, w, kt, 4, lambda j, h: src[:, j, h * HALF:(h + 1) * HALF], T,
                      lambda e, tile, ps, n: nc.vector.tensor_copy(flat(tile), ps),
                      lambda e, tile, ps, n: nc.scalar.activation(flat(tile), ps, ACT.Copy))
        phase_residual(k, name, res, m0)


def phase_residual(k, name, res, m0):
    nc = k.nc
    done, scaled = k.sem(f"{name}_added"), k.sem(f"{name}_scaled")
    with nc.Block() as block:
        @block.vector
        def _(dve):
            for j in range(KT):
                nc.vector.scalar_tensor_tensor(out=k.xT[:, j, 0:TP], in0=res[:, j, 0:TP], scalar=k.mod[:, m0 + j, 0:1],
                                               in1=k.xT[:, j, 0:TP], op0=ALU.mult, op1=ALU.add).then_inc(done, 1)
            rs = res[:, :, TP:T].rearrange("p k (b q) -> p k b q", q=NQ)
            g = k.mod[:, m0:m0 + KT, 1:NC9].unsqueeze(3).to_broadcast([P, KT, NB, NQ])
            nc.vector.tensor_tensor(rs, rs, g, ALU.mult).then_inc(scaled, 1)
            dve.wait_ge(scaled, 1)
            nc.vector.tensor_tensor(k.xT[:, :, TP:T], k.xT[:, :, TP:T], res[:, :, TP:T], ALU.add).then_inc(done, 1)
            dve.wait_ge(done, KT + 1)


def phase_short_conv(k, proj, gT):
    nc, io = k.nc, k.io
    loaded, own_d, kept_done, stored = (k.sem("sc_" + n) for n in ("loaded", "own", "kept", "stored"))
    with ExitStack() as ctx:
        buf = k.sb("sc_buf", [P, KT, NB, 2], ctx=ctx)
        kept = k.sb("sc_kept", [P, KT, 2 + TS], ctx=ctx)
        raw_p = k.sb("sc_rawp", [P, 2 + TP], ctx=ctx)
        raw_s = k.sb("sc_raws", [P, NB, 2 + NQ], ctx=ctx)
        with nc.Block() as block:
            @block.sync
            def _(sp):
                sp.dma_start(buf[:, :, :, :], io["sc_state"]).then_inc(loaded, 16)
                sp.wait_ge(kept_done, 2)
                sp.dma_start(io["sc_out"], kept[:, :, :]).then_inc(stored, 16)
                sp.wait_ge(stored, 16)

            @block.vector
            def _(dve):
                own = Chain(dve, own_d)
                own.did(nc.vector.memset(raw_p[:, 0:2], 0.0))
                for j in range(KT):
                    c, u = proj[:, KT + j, :], proj[:, 2 * KT + j, :]
                    own.did(nc.vector.tensor_tensor(u, c, u, ALU.mult))
                own.settle()
                u = proj[:, 2 * KT:3 * KT, :]
                nc.vector.tensor_copy(kept[:, :, 0:2], u[:, :, TP - 2:TP]).then_inc(kept_done, 1)
                nc.vector.tensor_copy(kept[:, :, 2:2 + TS], u[:, :, TP:T]).then_inc(kept_done, 1)
                dve.wait_ge(loaded, 16)
                for j in range(KT):
                    own.did(nc.vector.tensor_copy(raw_p[:, 2:2 + TP], u[:, j, 0:TP]))
                    own.did(nc.vector.tensor_copy(raw_s[:, :, 2:2 + NQ],
                                                  u[:, j, TP:T].rearrange("p (b q) -> p b q", q=NQ)))
                    own.did(nc.vector.tensor_copy(raw_s[:, :, 0:2], buf[:, j, :, :]))
                    own.settle()
                    gs = gT[:, j, TP:T].rearrange("p (b q) -> p b q", q=NQ)
                    own.did(nc.vector.tensor_scalar(gT[:, j, 0:TP], raw_p[:, 0:TP], k.col("sc_w", j), None, ALU.mult))
                    own.did(nc.vector.tensor_scalar(gs, raw_s[:, :, 0:NQ], k.col("sc_w", j), None, ALU.mult))
                    own.settle()
                    for t in range(1, 3):
                        w = k.col("sc_w", t * KT + j)
                        own.did(nc.vector.scalar_tensor_tensor(out=gT[:, j, 0:TP], in0=raw_p[:, t:t + TP], scalar=w,
                                                               in1=gT[:, j, 0:TP], op0=ALU.mult, op1=ALU.add))
                        own.did(nc.vector.scalar_tensor_tensor(out=gs, in0=raw_s[:, :, t:t + NQ], scalar=w, in1=gs,
                                                               op0=ALU.mult, op1=ALU.add))
                        own.settle()
                    own.step(nc.vector.tensor_tensor(gT[:, j, :], gT[:, j, :], proj[:, j, :], ALU.mult))


class Routing:

    def __init__(self, k, ctx, layer):
        self.tok = k.sb(f"route{layer}_tok", [CAP, NBLK], I32, ctx=ctx)
        self.slot = k.sb(f"route{layer}_slot", [P, 2, TT], I32, ctx=ctx)
        self.weight = k.sb(f"route{layer}_weight", [P, 2, TT], ctx=ctx)
        self.more = k.sb(f"route{layer}_more", [1, 1 + OVB], I32, ctx=ctx)


def phase_route(k, layer, r, ex):
    nc, io = k.nc, k.io
    nm = f"rt{layer}_"
    names = ("w", "iota", "tr", "trc", "rows", "lg", "e_in", "e_out", "mask", "rank", "pair", "slots", "own_d", "own_p",
             "done")
    s = {n: k.sem(nm + n) for n in names}
    with ExitStack() as ctx:
        sb = lambda n, shape, dt=F32: k.sb(nm + n, shape, dt, ctx=ctx)
        w_r = sb("wr", [P, KT, 36])
        rows = sb("rowbuf", [P, 2, D])
        lg = sb("lg", [P, TT, 36])
        desc = sb("desc", [P, 8])
        expert = sb("expert", [P, NE])
        block_id = sb("block_id", [P, NBLK])
        row_id = sb("row_id", [P, CAP])
        tok_id = sb("tok_id", [P, TT])
        full = sb("full", [P, MAXQ])
        valid = sb("valid", [P, TT])
        t1, t2, t3, t4 = (sb(f"t{i}", [P, TT, 1]) for i in range(4))
        g4, oh_g = sb("g4", [P, TT, 4]), sb("oh_g", [P, TT, 4])
        e8, sc8 = sb("e8", [P, TT, 8]), sb("sc8", [P, TT, 8])
        oh8 = [sb(f"oh8{i}", [P, TT, 8]) for i in range(2)]
        top = [sb(f"top{i}", [P, TT, 1]) for i in range(2)]
        oh = [sb(f"oh{i}", [P, TT, NE]) for i in range(2)]
        x32, mask, rank = sb("x32", [P, TT, NE]), sb("mask", [P, TT, NE]), sb("rank", [P, TT, NE])
        cnt, nov, ovb = sb("cnt", [P, NE]), sb("nov", [P, NE]), sb("ovb", [P, NE])
        cmp_n = sb("cmp_n", [P, NE, MAXQ])
        cmp_q = sb("cmp_q", [P, TT, MAXQ])
        cmp_o = sb("cmp_o", [1, OVB, NE])
        more_f = sb("more_f", [1, 1 + OVB])
        blk, row, rk, q_, ov = ([sb(f"{n}{i}", [P, TT]) for i in range(2)] for n in ("blk", "row", "rk", "q", "ov"))
        row_hot = sb("row_hot", [P, 2, CAP])
        blk_hot = sb("blk_hot", [P, 2, NBLK])
        slot_f = sb("slot_f", [CAP, NBLK])
        none = sb("none", [CAP, NBLK])
        tr_ps = [k.ps(f"{nm}tr{i}", [P, 512], ctx) for i in range(2)]
        lg_ps = k.ps(nm + "lgps", [P, TT, 36], ctx)
        rk_ps = k.ps(nm + "rkps", [P, TT + 1, NE], ctx)
        sl_ps = k.ps(nm + "slps", [CAP, NBLK], ctx)

        with nc.Block() as block:
            @block.sync
            def _(sp):
                sp.dma_start(w_r[:, :, :], io["w_route"][layer].rearrange("(k p) n -> p k n", p=P)).then_inc(s["w"], 16)
                for b in range(ex.SLOTS):
                    ex.load(k, sp, b, b, ex.w[b])
                for i, (a, m) in enumerate(TOK):
                    sp.wait_ge(s["trc"], 2 * (i + 1))
                    sp.dma_start(k.h_rows[a:a + m, :], rows[0:m, i % 2, :]).then_inc(s["rows"], 16)
                    sp.wait_ge(s["rows"], 16 * (i + 1))

            @block.gpsimd
            def _(pool):
                own = Chain(pool, s["own_p"])
                kw = dict(allow_small_or_imprecise_dtypes=True)
                own.did(nc.gpsimd.iota(desc[:, :], [[-1, 8]], base=8, channel_multiplier=0, **kw))
                own.did(nc.gpsimd.iota(expert[:, :], [[1, NE]], base=0, channel_multiplier=0, **kw))
                own.did(nc.gpsimd.iota(block_id[:, :], [[1, NBLK]], base=0, channel_multiplier=0, **kw))
                own.did(nc.gpsimd.iota(row_id[:, :], [[1, CAP]], base=0, channel_multiplier=0, **kw))
                own.did(nc.gpsimd.iota(tok_id[:, :], [[P, TT]], base=1, channel_multiplier=1, **kw))
                own.did(nc.gpsimd.iota(full[:, :], [[CAP, MAXQ]], base=CAP, channel_multiplier=0, **kw))
                own.step(nc.gpsimd.memset(valid[:, :], 1.0))
                own.step(nc.gpsimd.affine_select(out=valid[:, :], in_=valid[:, :], pattern=[[-P, TT]], base=T - 1,
                                                 channel_multiplier=-1, compare_op=ALU.is_ge, fill=0.0))
                pool.sem_inc(s["iota"], 1)

            @block.tensor
            def _(pe):
                pe.wait_ge(s["w"], 16)
                for i, (a, m) in enumerate(TOK):
                    for j in range(KT):
                        last = nc.tensor.matmul(lg_ps[0:m, i, :], k.hT[:, j, a:a + m], w_r[:, j, :],
                                                start=(j == 0), stop=(j == KT - 1))
                last.then_inc(s["lg"], 1)
                for i, (a, m) in enumerate(TOK):
                    for n in range(2):
                        u = 2 * i + n
                        if u >= 2:
                            pe.wait_ge(s["trc"], u - 1)
                        for j in range(4):
                            last = nc.tensor.transpose(tr_ps[n][0:m, j * P:(j + 1) * P], k.hT[:, 4 * n + j, a:a + m],
                                                       k.ident[:, :])
                        last.then_inc(s["tr"], 1)
                pe.wait_ge(s["mask"], 1)
                for i in range(TT):
                    nc.tensor.matmul(rk_ps[:, i, :], k.tri_lt[:, :], mask[:, i, :], start=True, stop=(i == 0))
                    for ii in range(i):
                        nc.tensor.matmul(rk_ps[:, i, :], k.ones[:, :], mask[:, ii, :], start=False, stop=(ii == i - 1))
                for i in range(TT):
                    last = nc.tensor.matmul(rk_ps[:, TT, :], k.ones[:, :], mask[:, i, :], start=(i == 0),
                                            stop=(i == TT - 1))
                last.then_inc(s["rank"], 1)
                for n in range(2 * TT):
                    m = TOK[n // 2][1]
                    pe.wait_ge(s["pair"], n + 1)
                    last = nc.tensor.matmul(sl_ps[:, :], row_hot[0:m, n % 2, :], blk_hot[0:m, n % 2, :],
                                            start=(n == 0), stop=(n == 2 * TT - 1))
                    last.then_inc(s["slots"], 1)

            @block.scalar
            def _(act):
                for u in range(2 * TT):
                    i, n = u // 2, u % 2
                    m = TOK[i][1]
                    act.wait_ge(s["tr"], u + 1)
                    if i >= 2 and n == 0:
                        act.wait_ge(s["rows"], 16 * (i - 1))
                    nc.scalar.activation(rows[0:m, i % 2, n * 512:(n + 1) * 512], tr_ps[n][0:m, :], ACT.Copy)\
                      .then_inc(s["trc"], 1)
                act.wait_ge(s["e_in"], 1)
                nc.scalar.activation(g4[:, :, :], g4[:, :, :], ACT.Exp).then_inc(s["e_out"], 1)
                act.wait_ge(s["e_in"], 2)
                nc.scalar.activation(e8[:, :, :], e8[:, :, :], ACT.Exp).then_inc(s["e_out"], 1)

            @block.vector
            def _(dve):
                own = Chain(dve, s["own_d"])
                V = nc.vector
                step = own.step
                wide = lambda t, n: t[:, :, :].to_broadcast([P, TT, n])
                step(V.memset(lg[:, :, :], 0.0))
                dve.wait_ge(s["lg"], 1)
                bias = k.small[:, COLS["router_b"][0] + 36 * layer:COLS["router_b"][0] + 36 * (layer + 1)]
                step(V.tensor_tensor(lg[:, 0:4, :], lg_ps[:, 0:4, :], bias.unsqueeze(1).to_broadcast([P, 4, 36]), ALU.add))
                step(V.tensor_tensor(lg[0:TS, 4, :], lg_ps[0:TS, 4, :], bias[0:TS, :], ALU.add))
                step(V.tensor_reduce(t1[:, :, :], lg[:, :, 0:4], AX_X, ALU.max))
                V.tensor_tensor(g4[:, :, :], lg[:, :, 0:4], wide(t1, 4), ALU.subtract).then_inc(s["e_in"], 1)
                dve.wait_ge(s["iota"], 1)
                dve.wait_ge(s["e_out"], 1)
                g_top = t4
                step(V.tensor_reduce(t1[:, :, :], g4[:, :, :], AX_X, ALU.max))
                step(V.tensor_reduce(t2[:, :, :], g4[:, :, :], AX_X, ALU.add))
                step(V.reciprocal(t3[:, :, :], t2[:, :, :]))
                step(V.tensor_tensor(g_top[:, :, :], t1[:, :, :], t3[:, :, :], ALU.mult))

                def first_largest(out, values, largest, n, scratch):
                    step(V.tensor_tensor(out, values, wide(largest, n), ALU.is_equal))
                    step(V.tensor_tensor(out, out, desc[:, 0:n].unsqueeze(1).to_broadcast([P, TT, n]), ALU.mult))
                    step(V.tensor_reduce(scratch[:, :, :], out, AX_X, ALU.max))
                    step(V.tensor_tensor(out, out, wide(scratch, n), ALU.is_equal))

                first_largest(oh_g[:, :, :], g4[:, :, :], t1, 4, t2)
                by_group = lambda t: t[:, :, :].rearrange("p t (g e) -> p t g e", e=8)
                for i in range(TT):
                    own.did(V.tensor_tensor(x32[:, i, :].rearrange("p (g e) -> p g e", e=8),
                                            lg[:, i, 4:36].rearrange("p (g e) -> p g e", e=8),
                                            oh_g[:, i, :].unsqueeze(2).to_broadcast([P, 4, 8]), ALU.mult))
                own.settle()
                step(V.tensor_reduce(sc8[:, :, :].unsqueeze(3), x32[:, :, :].rearrange("p t (g e) -> p t e g", e=8),
                                     AX_X, ALU.add))
                step(V.tensor_reduce(t1[:, :, :], sc8[:, :, :], AX_X, ALU.max))
                V.tensor_tensor(e8[:, :, :], sc8[:, :, :], wide(t1, 8), ALU.subtract).then_inc(s["e_in"], 1)
                dve.wait_ge(s["e_out"], 2)
                for i in range(2):
                    step(V.tensor_reduce(top[i][:, :, :], e8[:, :, :], AX_X, ALU.max))
                    first_largest(oh8[i][:, :, :], e8[:, :, :], top[i], 8, t2)
                    if i == 0:
                        step(V.scalar_tensor_tensor(out=e8[:, :, :], in0=oh8[0][:, :, :], scalar=-2.0, in1=e8[:, :, :],
                                                    op0=ALU.mult, op1=ALU.add))
                step(V.tensor_tensor(t1[:, :, :], top[0][:, :, :], top[1][:, :, :], ALU.add))
                step(V.reciprocal(t2[:, :, :], t1[:, :, :]))
                step(V.tensor_tensor(t2[:, :, :], t2[:, :, :], g_top[:, :, :], ALU.mult))
                for i in range(2):
                    step(V.tensor_tensor(r.weight[:, i, :], top[i][:, :, 0], t2[:, :, 0], ALU.mult))
                    for t in range(TT):
                        own.did(V.tensor_tensor(oh[i][:, t, :].rearrange("p (g e) -> p g e", e=8),
                                                oh_g[:, t, :].unsqueeze(2).to_broadcast([P, 4, 8]),
                                                oh8[i][:, t, :].unsqueeze(1).to_broadcast([P, 4, 8]), ALU.mult))
                own.settle()
                step(V.tensor_tensor(x32[:, :, :], oh[0][:, :, :], oh[1][:, :, :], ALU.add))
                V.tensor_tensor(mask[:, :, :], x32[:, :, :], valid[:, :].unsqueeze(2).to_broadcast([P, TT, NE]), ALU.mult)\
                 .then_inc(s["mask"], 1)
                dve.wait_ge(s["rank"], 1)
                step(V.tensor_copy(rank[:, :, :], rk_ps[:, 0:TT, :]))
                step(V.tensor_copy(cnt[:, :], rk_ps[:, TT, :]))
                step(V.tensor_tensor(cmp_n[:, :, :], cnt[:, :].unsqueeze(2).to_broadcast([P, NE, MAXQ]),
                                     full[:, :].unsqueeze(1).to_broadcast([P, NE, MAXQ]), ALU.is_gt))
                step(V.tensor_reduce(nov[:, :].unsqueeze(2), cmp_n[:, :, :], AX_X, ALU.add))
                step(V.tensor_tensor_scan(ovb[:, :], nov[:, :], nov[:, :], 0.0, ALU.add, ALU.bypass))
                step(V.tensor_tensor(cmp_o[:, :, :], block_id[0:1, 0:OVB].unsqueeze(2).to_broadcast([1, OVB, NE]),
                                     ovb[0:1, :].unsqueeze(1).to_broadcast([1, OVB, NE]), ALU.is_ge))
                step(V.tensor_reduce(more_f[:, 1:1 + OVB].unsqueeze(2), cmp_o[:, :, :], AX_X, ALU.add))
                step(V.tensor_scalar(more_f[:, 1:1 + OVB], more_f[:, 1:1 + OVB], float(NE - 1), None, ALU.min))
                step(V.tensor_copy(more_f[:, 0:1], ovb[0:1, NE - 1:NE]))
                step(V.tensor_copy(r.more[:, :], more_f[:, :]))
                step(V.tensor_tensor(ovb[:, :], ovb[:, :], nov[:, :], ALU.subtract))
                for i in range(2):
                    def pick(dst, table):
                        step(V.tensor_tensor(x32[:, :, :], oh[i][:, :, :], table, ALU.mult))
                        step(V.tensor_reduce(dst.unsqueeze(2), x32[:, :, :], AX_X, ALU.add))
                    pick(rk[i][:, :], rank[:, :, :])
                    pick(blk[i][:, :], expert[:, :].unsqueeze(1).to_broadcast([P, TT, NE]))
                    pick(ov[i][:, :], ovb[:, :].unsqueeze(1).to_broadcast([P, TT, NE]))
                    step(V.tensor_tensor(cmp_q[:, :, :], rk[i][:, :].unsqueeze(2).to_broadcast([P, TT, MAXQ]),
                                         full[:, :].unsqueeze(1).to_broadcast([P, TT, MAXQ]), ALU.is_ge))
                    step(V.tensor_reduce(q_[i][:, :].unsqueeze(2), cmp_q[:, :, :], AX_X, ALU.add))
                    step(V.scalar_tensor_tensor(out=row[i][:, :], in0=q_[i][:, :], scalar=-float(CAP), in1=rk[i][:, :],
                                                op0=ALU.mult, op1=ALU.add))
                    step(V.tensor_tensor(ov[i][:, :], ov[i][:, :], q_[i][:, :], ALU.add))
                    step(V.scalar_tensor_tensor(out=ov[i][:, :], in0=ov[i][:, :], scalar=float(NE - 1), in1=blk[i][:, :],
                                                op0=ALU.add, op1=ALU.subtract))
                    step(V.tensor_scalar(q_[i][:, :], q_[i][:, :], 1.0, None, ALU.min))
                    step(V.tensor_tensor(ov[i][:, :], ov[i][:, :], q_[i][:, :], ALU.mult))
                    step(V.tensor_tensor(blk[i][:, :], blk[i][:, :], ov[i][:, :], ALU.add))
                    step(V.scalar_tensor_tensor(out=rk[i][:, :], in0=blk[i][:, :], scalar=float(CAP), in1=row[i][:, :],
                                                op0=ALU.mult, op1=ALU.add))
                    step(V.tensor_copy(r.slot[:, i, :], rk[i][:, :]))
                for n in range(2 * TT):
                    t, i = n // 2, n % 2
                    if n >= 2:
                        dve.wait_ge(s["slots"], n - 1)
                    own.did(V.tensor_scalar(row_hot[:, i, :], row_id[:, :], row[i][:, t:t + 1], None, ALU.is_equal))
                    own.settle()
                    V.tensor_scalar(blk_hot[:, i, :], block_id[:, :], blk[i][:, t:t + 1], tok_id[:, t:t + 1],
                                    ALU.is_equal, ALU.mult).then_inc(s["pair"], 1)
                dve.wait_ge(s["slots"], 2 * TT)
                step(V.tensor_scalar(none[:, :], sl_ps[:, :], 0.0, BIG, ALU.is_equal, ALU.mult))
                step(V.scalar_tensor_tensor(out=slot_f[:, :], in0=sl_ps[:, :], scalar=-1.0, in1=none[:, :],
                                            op0=ALU.add, op1=ALU.add))
                step(V.tensor_copy(r.tok[:, :], slot_f[:, :]))


class Experts:

    SLOTS = 4

    def __init__(self, k, layer, ctx):
        self.layer = layer
        self.gu = [k.sb(f"ex{layer}_gu{b}", [P, 2, KT, DE], ctx=ctx) for b in range(self.SLOTS)]
        self.dn = [k.sb(f"ex{layer}_dn{b}", [P, 2, D], ctx=ctx) for b in range(self.SLOTS)]
        self.w = [k.sem(f"ex{layer}_w{b}") for b in range(self.SLOTS)]

    def load(self, k, sp, b, e, ready):
        one = lambda w: w[self.layer][bass.ds(e, 1), :, :]
        sp.dma_start(self.gu[b][:, 0, :, :], one(k.io["moe_w_gate"]).rearrange("a (p j) f -> p (a j f)", p=P))\
          .then_inc(ready, 16)
        sp.dma_start(self.gu[b][:, 1, :, :], one(k.io["moe_w_up"]).rearrange("a (p j) f -> p (a j f)", p=P))\
          .then_inc(ready, 16)
        sp.dma_start(self.dn[b][:, :, :], one(k.io["moe_w_down"]).rearrange("a (m p) d -> p (a m) d", p=P))\
          .then_inc(ready, 16)


def phase_experts(k, layer, r, ex):
    nc, io = k.nc, k.io
    nm = f"ex{layer}_"
    S = ex.SLOTS
    with ExitStack() as ctx:
        sb = lambda n, shape, dt=F32: k.sb(nm + n, shape, dt, ctx=ctx)
        hg = [sb(f"hg{b}", [CAP, D]) for b in range(2)]
        he = [sb(f"he{b}", [P, KT, CAP]) for b in range(2)]
        sg = sb("sg", [P, P])
        hid = sb("hid", [P, P])
        hid_t = sb("hid_t", [P, P])
        yo = [sb(f"yo{b}", [P, 512]) for b in range(2)]
        tr_ps = [k.ps(f"{nm}trps{b}", [P, KT, CAP], ctx) for b in range(2)]
        gu_ps = k.ps(f"{nm}gups", [P, 2, P], ctx)
        ht_ps = k.ps(f"{nm}htps", [P, P], ctx)
        y_ps = [k.ps(f"{nm}yps{b}", [P, 512], ctx) for b in range(2)]

        def block_programs(pass_name, rounds, first, load_slot, preloaded, w_ready):
            sems = {n: k.sem(f"{nm}{pass_name}{n}") for n in ("tr", "he", "gu", "sg", "hid", "htp", "ht", "y", "yo")}
            g = [k.sem(f"{nm}{pass_name}g{b}") for b in range(2)]
            st = [k.sem(f"{nm}{pass_name}st{b}") for b in range(2)]

            def sync_program(sp):
                if not preloaded:
                    for b in range(S):
                        load_slot(sp, b, b)
                if rounds > 1:
                    with sp.Fori(0, rounds - 1) as i:
                        for b in range(S):
                            sp.wait_ge(sems["y"], i * S + (b + 1))
                            load_slot(sp, b, i * S + (S + b))

            def pool_program(pool):
                for n in range(S * rounds):
                    if n >= 2:
                        pool.wait_ge(sems["tr"], n - 1)
                        pool.wait_ge(g[n % 2], 16 * (n // 2))
                    nc.gpsimd.indirect_dma_start(out=hg[n % 2][:, :], out_offset=None, in_=k.h_rows,
                                                 in_offset=bass.IndirectOffsetOnAxis(
                                                     ap=r.tok[:, first + n:first + n + 1], axis=0),
                                                 bounds_check=T - 1, oob_is_err=False).then_inc(g[n % 2], 16)

            def tensor_program(pe):
                with pe.Fori(0, rounds) as i:
                    for b in range(S):
                        p = b % 2
                        pe.wait_ge(g[p], i * (8 * S) + 16 * (b // 2 + 1))
                        nc.tensor.matmul(tr_ps[p][:, 0, :], hg[p][:, 0::KT], k.ident[0:CAP, 0:CAP], start=True, stop=True)
                        for j in range(1, KT):
                            last = nc.tensor.transpose(tr_ps[p][:, j, :], hg[p][:, j::KT], k.ident[0:CAP, 0:CAP])
                        last.then_inc(sems["tr"], 1)
                        pe.wait_ge(w_ready[b], i * 48 + 48)
                        pe.wait_ge(sems["he"], i * S + (b + 1))
                        for j in range(KT):
                            for q in range(2):
                                last = nc.tensor.matmul(gu_ps[64 * q:64 * q + 64, :, :], he[p][:, j, :],
                                                        ex.gu[b][:, :, j, q * P:(q + 1) * P],
                                                        start=(j == 0), stop=(j == KT - 1), skip_group_check=True)
                        last.then_inc(sems["gu"], 1)
                        pe.wait_ge(sems["hid"], i * S + (b + 1))
                        nc.tensor.transpose(ht_ps[:, :], hid[:, :], k.ident[:, :]).then_inc(sems["htp"], 1)
                        pe.wait_ge(sems["yo"], i * S + (b + 1))
                        pe.wait_ge(sems["ht"], i * S + (b + 1))
                        for m in range(2):
                            for n in range(2):
                                last = nc.tensor.matmul(y_ps[p][64 * n:64 * n + 64, :], hid_t[:, m * CAP:(m + 1) * CAP],
                                                        ex.dn[b][:, m, n * 512:(n + 1) * 512],
                                                        start=(m == 0), stop=(m == 1), skip_group_check=True)
                        last.then_inc(sems["y"], 1)

            def vector_program(dve):
                with dve.Fori(0, rounds) as i:
                    for b in range(S):
                        dve.wait_ge(sems["tr"], i * S + (b + 1))
                        nc.vector.tensor_copy(he[b % 2][:, :, :], tr_ps[b % 2][:, :, :]).then_inc(sems["he"], 1)
                        dve.wait_ge(sems["sg"], i * S + (b + 1))
                        nc.vector.tensor_tensor(hid[:, :], sg[:, :], gu_ps[:, 1, :], ALU.mult).then_inc(sems["hid"], 1)
                        dve.wait_ge(sems["htp"], i * S + (b + 1))
                        nc.vector.tensor_copy(hid_t[:, :], ht_ps[:, :]).then_inc(sems["ht"], 1)

            def scalar_program(act):
                act.sem_inc(sems["yo"], 1)
                for b in range(2):
                    act.sem_inc(st[b], 32)
                with act.Fori(0, rounds) as i:
                    for b in range(S):
                        p = b % 2
                        act.wait_ge(sems["gu"], i * S + (b + 1))
                        nc.scalar.activation(sg[:, :], gu_ps[:, 0, :], ACT.Silu).then_inc(sems["sg"], 1)
                        act.wait_ge(sems["y"], i * S + (b + 1))
                        act.wait_ge(st[p], i * (16 * S) + 32 * (b // 2 + 1))
                        nc.scalar.activation(yo[p][:, :], y_ps[p][:, :], ACT.Copy).then_inc(sems["yo"], 1)
                        act.wait_ge(sems["yo"], i * S + (b + 2))
                        for n in range(2):
                            act.dma_start(k.y_rows[bass.ds(i * (S * CAP) + (first + b) * CAP, CAP), n * 512:(n + 1) * 512],
                                          yo[p][64 * n:64 * n + 64, :]).then_inc(st[p], 16)
                for b in range(2):
                    act.wait_ge(st[b], 16 * S * rounds + 32)

            return sync_program, tensor_program, vector_program, scalar_program, pool_program

        main = block_programs("a", NE // S, 0, lambda sp, b, n: ex.load(k, sp, b, n, ex.w[b]), True, ex.w)
        rows_clear = k.sem(nm + "rows_clear")
        with nc.Block() as block:
            @block.vector
            def _(dve):
                for b in range(2):
                    nc.vector.memset(hg[b][:, :], 0.0).then_inc(rows_clear, 1)
                main[2](dve)

            @block.sync
            def _(sp):
                main[0](sp)

            @block.tensor
            def _(pe):
                main[1](pe)

            @block.scalar
            def _(act):
                main[3](act)

            @block.gpsimd
            def _(pool):
                pool.wait_ge(rows_clear, 2)
                main[4](pool)

        w_more = [k.sem(f"{nm}w_more{b}") for b in range(S)]

        def load_more(sp, b, n):
            e = sp.value_load(r.more[0:1, bass.ds(n + 1, 1)], min_val=0, max_val=NE - 1)
            ex.load(k, sp, b, e, w_more[b])

        more = block_programs("b", OVB // S, NE, load_more, False, w_more)

        def when_more(eng, program):
            n = eng.value_load(r.more[0:1, 0:1], min_val=0, max_val=OVB)
            with eng.If(n > 0):
                program(eng)

        with nc.Block() as block:
            @block.sync
            def _(sp):
                when_more(sp, more[0])

            @block.tensor
            def _(pe):
                when_more(pe, more[1])

            @block.vector
            def _(dve):
                when_more(dve, more[2])

            @block.scalar
            def _(act):
                when_more(act, more[3])

            @block.gpsimd
            def _(pool):
                when_more(pool, more[4])


def phase_combine(k, layer, r):
    nc = k.nc
    nm = f"co{layer}_"
    g, sc, sm, tr, ev, own_d = (k.sem(nm + n) for n in ("g", "sc", "sm", "tr", "ev", "own"))
    with ExitStack() as ctx:
        y = k.sb(nm + "y", [P, 2, 2, D], ctx=ctx)
        res = k.sb(nm + "res", [P, KT, T], ctx=ctx)
        ps = k.ps(nm + "ps", [P, KT, P], ctx)
        with nc.Block() as block:
            @block.gpsimd
            def _(pool):
                for t, (a, m) in enumerate(TOK):
                    if t >= 2:
                        pool.wait_ge(tr, t - 1)
                    for i in range(2):
                        nc.gpsimd.indirect_dma_start(out=y[0:m, t % 2, i, :], out_offset=None, in_=k.y_rows,
                                                     in_offset=bass.IndirectOffsetOnAxis(ap=r.slot[0:m, i, t:t + 1],
                                                                                         axis=0),
                                                     bounds_check=NBLK * CAP - 1, oob_is_err=False).then_inc(g, 16)
                    pool.wait_ge(g, 32 * (t + 1))

            @block.scalar
            def _(act):
                for t, (a, m) in enumerate(TOK):
                    act.wait_ge(g, 32 * (t + 1))
                    nc.scalar.activation(y[0:m, t % 2, 0, :], y[0:m, t % 2, 0, :], ACT.Copy,
                                         scale=r.weight[0:m, 0, t:t + 1]).then_inc(sc, 1)

            @block.vector
            def _(dve):
                for t, (a, m) in enumerate(TOK):
                    dve.wait_ge(g, 32 * (t + 1))
                    dve.wait_ge(sc, t + 1)
                    nc.vector.scalar_tensor_tensor(out=y[0:m, t % 2, 0, :], in0=y[0:m, t % 2, 1, :],
                                                   scalar=r.weight[0:m, 1, t:t + 1], in1=y[0:m, t % 2, 0, :],
                                                   op0=ALU.mult, op1=ALU.add).then_inc(sm, 1)
                    dve.wait_ge(tr, t + 1)
                    nc.vector.tensor_copy(res[:, :, a:a + m], ps[:, :, 0:m]).then_inc(ev, 1)
                dve.wait_ge(ev, TT)

            @block.tensor
            def _(pe):
                for t, (a, m) in enumerate(TOK):
                    pe.wait_ge(sm, t + 1)
                    if t:
                        pe.wait_ge(ev, t)
                    for j in range(KT):
                        last = nc.tensor.transpose(ps[:, j, 0:m], y[0:m, t % 2, 0, j * P:(j + 1) * P],
                                                   k.ident[0:m, 0:m])
                    last.then_inc(tr, 1)
        phase_residual(k, nm, res, layer * 48 + 5 * KT)


def moe(k, layer):
    with ExitStack() as ctx:
        r = Routing(k, ctx, layer)
        with ExitStack() as c:
            ex = Experts(k, layer, c)
            phase_route(k, layer, r, ex)
            phase_experts(k, layer, r, ex)
        phase_combine(k, layer, r)


def build(nc, io):
    with ExitStack() as ctx:
        k = Trunk(nc, ctx, io)
        k.h_rows = nc.dram_tensor("h_rows", (T, D), F32).ap()
        k.y_rows = nc.dram_tensor("y_rows", (NBLK * CAP, D), F32).ap()
        with ExitStack() as c:
            k.cT = k.sb("cT_sb", [P, KT, 32], ctx=c)
            ada = AdaWeights(k, c)
            phase_constants(k, ada)
            phase_ada(k, ada)
        phase_norm(k, "n0", 0, 0)
        with ExitStack() as c0:
            mixT = k.sb("mixT", [P, 2 * KT, T], ctx=c0)
            ca = ExitStack()
            qz = k.sb("qz", [P, KT, NB, 32], ctx=ca)
            kn = k.sb("kn", [P, KT, NB, NQ], ctx=ca)
            with ExitStack() as c:
                k.qk = k.sb("qk", [P, 2 * KT, T], ctx=c)
                k.qT, k.kT = k.qk[:, 0:KT, :], k.qk[:, KT:2 * KT, :]
                flat = lambda tile: by_half(k.qk[:, bass.ds(tile, 1), :].rearrange("p a t -> p (a t)"))
                rhs = lambda j, h: k.hT[:, j, h * HALF:(h + 1) * HALF]
                for nm, col, first, scale in (("q", 2576, 0, HD ** -0.5), ("kk", 3600, KT, 1.0)):
                    phase_project(k, nm, io["mix_w_in"][:, col:col + D], KT, 4, rhs, T,
                                  lambda e, tile, ps, n, first=first, scale=scale: nc.vector.tensor_scalar(
                                      flat(tile + first), ps, scale, None, ALU.mult),
                                  lambda e, tile, ps, n, first=first, scale=scale: nc.scalar.activation(
                                      flat(tile + first), ps, ACT.Copy, scale=scale))
                with ExitStack() as cv:
                    vtok = k.sb("vtok", [P, TT, D], ctx=cv)
                    phase_value(k, vtok, qz, kn)
                    phase_attention_prompt(k, vtok, mixT)
            with ca:
                phase_attention_sample(k, mixT, qz, kn)
            k.recycle()
            with ExitStack() as c:
                zs = k.sb("zs", [P, KT, T], ctx=c)
                xc = k.sb("xc", [P, XT, T], ctx=c)
                dt_tok = k.sb("dt_tok", [P, TT, H], ctx=c)
                phase_ssd_project(k, xc, zs, dt_tok)
                phase_ssd(k, xc, mixT, dt_tok)
                phase_gated_norm(k, zs, mixT)
            phase_out_project(k, "out0", io["mix_w_out"], 2 * KT, mixT, 0, 2)
        k.recycle()
        phase_norm(k, "n1", 0, 3)
        moe(k, 0)
        k.recycle()
        phase_norm(k, "n2", 1, 0)
        with ExitStack() as c:
            gT = k.sb("gT", [P, KT, T], ctx=c)
            with ExitStack() as c1:
                proj = k.sb("sc_proj", [P, 3 * KT, T], ctx=c1)
                flat = lambda tile: by_half(proj[:, bass.ds(tile, 1), :].rearrange("p a t -> p (a t)"))
                phase_project(k, "sc", io["sc_w_in"], KT, 12, lambda j, h: k.hT[:, j, h * HALF:(h + 1) * HALF], T,
                              lambda e, tile, ps, n: nc.vector.tensor_copy(flat(tile), ps),
                              lambda e, tile, ps, n: nc.scalar.activation(flat(tile), ps, ACT.Copy))
                phase_short_conv(k, proj, gT)
            phase_out_project(k, "out1", io["sc_w_out"], KT, gT, 1, 2)
        k.recycle()
        phase_norm(k, "n3", 1, 3)
        moe(k, 1)
        phase_norm(k, "n4", None, 0)


def kernel(x_prompt, x_sample, c_prompt, c_sample, state_ssm, state_ssd_conv, cache_k, cache_v, page_table,
           state_short_conv, ada_w, ada_b, ln_mix_g, ln_ffn_g, mix_w_in, mix_w_out, ssd_conv_w, ssd_conv_b,
           ssd_dt_bias, ssd_a_log, ssd_d, ssd_norm_g, sb_bias, sc_w_in, sc_conv_w, sc_w_out, moe_w_group,
           moe_b_group, moe_w_router, moe_b_router, moe_w_gate, moe_w_up, moe_w_down, final_g):
    import numpy as np
    import concourse.bacc as bacc
    from concourse.bass_utils import run_bass_kernel_spmd as run

    def arr(a):
        return np.asarray(a)

    def feature(a):
        a = arr(a)
        a = a.reshape(-1, a.shape[-1] // P, P)
        return a.transpose(2, 0, 1).reshape(P, -1)

    def row(a):
        return np.broadcast_to(arr(a).reshape(1, -1), (P, arr(a).size))

    p = np.arange(P)[:, None]
    before = (np.arange(NQ)[None] < p % NQ).astype(np.float32)
    own_head = (np.arange(8)[None] == p // NQ % 8).astype(np.float32)
    small = np.concatenate([
        feature(ada_b), feature(ln_mix_g), feature(ln_ffn_g), feature(final_g[None]), feature(ssd_conv_w[0]),
        feature(ssd_conv_b), np.repeat(arr(ssd_d)[0], HD).reshape(KT, P).T, feature(ssd_norm_g),
        feature(sc_conv_w[0]), row(ssd_dt_bias), row(ssd_a_log), row(sb_bias),
        row(np.concatenate([arr(moe_b_group), arr(moe_b_router)], axis=1)),
        np.tile(np.repeat(arr(sb_bias).reshape(-1), NQ), 2).reshape(P, 1), before, own_head], axis=1)
    assert small.shape == (P, N_SMALL)
    inputs = {
        "xT": np.concatenate([arr(x_prompt)[0], arr(x_sample).reshape(TS, D)], axis=0).T,
        "cT": np.concatenate([arr(c_prompt), arr(c_sample)], axis=0).T,
        "small": small,
        "ssm_state": arr(state_ssm)[0].transpose(3, 0, 1, 2).reshape(NS, NB, D),
        "conv_state": arr(state_ssd_conv)[0].reshape(NB, 3, XT, P).transpose(3, 2, 0, 1),
        "sc_state": arr(state_short_conv)[0].reshape(NB, 2, KT, P).transpose(3, 2, 0, 1),
        "cache_kT": arr(cache_k)[0].reshape(POOL_PAGES, PAGE, KT, P).transpose(0, 3, 2, 1)[:, :, :, ::-1]
        .reshape(POOL_PAGES, P, D),
        "cache_v": arr(cache_v)[0].reshape(POOL_PAGES, PAGE, D)[:, ::-1],
        "page_table": arr(page_table).reshape(1, NB * PAGES),
        "ada_w": arr(ada_w), "mix_w_in": arr(mix_w_in)[0], "mix_w_out": arr(mix_w_out)[0],
        "sc_w_in": arr(sc_w_in)[0], "sc_w_out": arr(sc_w_out)[0],
        "w_route": np.concatenate([arr(moe_w_group), arr(moe_w_router)], axis=2),
        "moe_w_gate": arr(moe_w_gate), "moe_w_up": arr(moe_w_up), "moe_w_down": arr(moe_w_down),
    }
    inputs = {n: np.ascontiguousarray(a) for n, a in inputs.items()}
    outputs = {"yT": (D, T), "ssm_p": (NS, D), "ssm_s": (NS, NB, D), "conv_out": (P, XT, 3 + TS),
               "kT": (P, KT, T), "v": (T, D), "sc_out": (P, KT, 2 + TS)}
    nc = bacc.Bacc("TRN2", target_bir_lowering=False, num_devices=1)
    io = {n: nc.dram_tensor("in_" + n, a.shape, mybir.dt.from_np(a.dtype), kind="ExternalInput").ap()
          for n, a in inputs.items()}
    io.update({n: nc.dram_tensor("out_" + n, shape, F32, kind="ExternalOutput").ap() for n, shape in outputs.items()})
    build(nc, io)
    r = run(nc, [{"in_" + n: a for n, a in inputs.items()}], core_ids=[0]).results[0]
    r = {n: r["out_" + n] for n in outputs}

    y = r["yT"].T
    conv = r["conv_out"].transpose(2, 1, 0).reshape(3 + TS, XT * P)
    kk = r["kT"].transpose(2, 1, 0).reshape(T, D)
    sc = r["sc_out"].transpose(2, 1, 0).reshape(2 + TS, D)
    c = np.ascontiguousarray
    return (c(y[:TP]).reshape(1, TP, D), c(y[TP:]).reshape(NB, NQ, D),
            c(r["ssm_p"].reshape(NS, H, HD).transpose(1, 2, 0))[None, None],
            c(r["ssm_s"].reshape(NS, NB, H, HD).transpose(1, 2, 3, 0))[None],
            c(conv[:3])[None, None], c(conv[3:].reshape(NB, NQ, XT * P)[:, 1:])[None],
            c(kk[:TP]).reshape(1, 1, TP, H, HD), c(kk[TP:]).reshape(1, NB, NQ, H, HD),
            c(r["v"][:TP]).reshape(1, 1, TP, H, HD), c(r["v"][TP:]).reshape(1, NB, NQ, H, HD),
            c(sc[:2])[None, None], c(sc[2:].reshape(NB, NQ, D)[:, 2:])[None])
```

```python
from contextlib import ExitStack

import concourse.bass as bass
from concourse import mybir

F32 = mybir.dt.float32
F32R = mybir.dt.float32r
I32 = mybir.dt.int32
ALU = mybir.AluOpType
ACT = mybir.ActivationFunctionType
AX_X = mybir.AxisListType.X

P = 128
D = 1024
KT = D // P
TP = 512
NB, NQ = 8, 4
TS = NB * NQ
T = TP + TS
HALF = T // 2
TT = 5
TOK = [(i * P, P) for i in range(4)] + [(TP, TS)]
NC9 = 1 + NB
H, HD = 16, 64
NS = 128
XT = 12
PAGES, PAGE = 4, 128
POOL_PAGES = 40
NE, DE = 32, 256
CAP = 64
OVB = -(-((2 * T - 1) // CAP) // 4) * 4
NBLK = NE + OVB
MAXQ = (T - 1) // CAP
EPS = 1e-6
BIG = 1.0e6
NO_DECAY = -1.0e4

COLS = {}
_at = 0
for _name, _n in (("ada_b", 96), ("ln_mix", 16), ("ln_ffn", 16), ("final_g", 8), ("conv_w", 48), ("conv_b", 12),
                  ("d_skip", 8), ("norm_g", 8), ("sc_w", 24), ("dt_bias", 16), ("a_log", 16), ("sb_bias", 16),
                  ("router_b", 72), ("sb_rows", 1), ("before", NQ), ("own_head", 8)):
    COLS[_name] = (_at, _at + _n)
    _at += _n
N_SMALL = _at


class Chain:

    def __init__(self, eng, sem):
        self.eng, self.sem, self.n = eng, sem, 0

    def did(self, ins):
        ins.then_inc(self.sem, 1)
        self.n += 1
        return ins

    def settle(self):
        if self.n:
            self.eng.wait_ge(self.sem, self.n)

    def step(self, ins):
        self.did(ins)
        self.settle()


class Trunk:

    def __init__(self, nc, ctx, io):
        self.nc, self.ctx, self.io = nc, ctx, io
        self.phase_sems = []
        self.offset = {}
        sb = self.sb
        self.xT = sb("xT", [P, KT, T])
        self.hT = sb("hT", [P, KT, T])
        self.mod = sb("mod", [P, 96, NC9])
        self.small = sb("small", [P, N_SMALL])
        self.ident = sb("ident", [P, P])
        self.ones = sb("ones", [P, P])
        self.neg_ones = sb("neg_ones", [P, P])
        self.neg_tri = sb("neg_tri", [P, P])
        self.tri_le = sb("tri_le", [P, P])
        self.tri_lt = sb("tri_lt", [P, P])
        self.same = sb("same", [TS, TS])
        self.tri_same = sb("tri_same", [TS, TS])
        self.member = sb("member", [TS, NB])
        self.hT_r = self.split_view("hT", [P, KT, T])
        self.w_ready = [self.sem(f"w_ready{b}") for b in range(2)]
        self.w_hi = [self.sem(f"w_hi{b}") for b in range(2)]
        self.w_lo = [self.sem(f"w_lo{b}") for b in range(2)]
        self.mm_done = [[self.sem(f"mm_done{b}{t}") for t in range(2)] for b in range(2)]
        self.ps_free = [[self.sem(f"ps_free{b}{t}") for t in range(2)] for b in range(2)]
        self.phase_sems = []
        self.rounds = 0

    def sb(self, name, shape, dt=F32, ctx=None):
        self.offset[name] = -(-self.nc.sbuf_base // 32) * 32
        return (ctx or self.ctx).enter_context(self.nc.sbuf_tensor(name, shape, dt))

    def split_view(self, name, shape, suffix="_r"):
        return self.nc.alloc_sbuf_tensor_at(name + suffix, shape, F32R, offset=self.offset[name])

    def ps(self, name, shape, ctx):
        return ctx.enter_context(self.nc.psum_tensor(name, shape, F32))

    def sem(self, name):
        one = self.nc.alloc_semaphore(name=name)
        self.phase_sems.append(one)
        return one

    def recycle(self):
        self.nc.clear_and_free_semaphores(self.phase_sems)
        self.nc.all_engine_barrier()
        self.phase_sems = []

    def col(self, name, i, n=1):
        a = COLS[name][0] + i
        return self.small[:, a:a + n]

    def mod_tiles(self, layer, chunk):
        a = layer * 48 + chunk * KT
        return self.mod[:, a:a + KT, :]


def phase_constants(k, ada):
    nc, io = k.nc, k.io
    cT = k.cT
    loaded, made, cond_ready = k.sem("loaded"), k.sem("made"), k.sem("cond_ready")
    cond_loaded, padded = k.sem("cond_loaded"), k.sem("padded")
    with nc.Block() as block:
        @block.sync
        def _(sp):
            sp.wait_ge(padded, 1)
            sp.dma_start(cT[:, :, 0:NC9], io["cT"].rearrange("(k p) c -> p k c", p=P)).then_inc(cond_loaded, 16)
            sp.dma_start(k.small[:, :], io["small"]).then_inc(loaded, 16)
            for j in range(KT):
                ada.load(sp, 0, j)
            sp.dma_start(k.xT[:, :, :], io["xT"].rearrange("(k p) t -> p k t", p=P)).then_inc(loaded, 16)
            sp.wait_ge(loaded, 32)

        @block.scalar
        def _(act):
            act.wait_ge(cond_loaded, 16)
            nc.scalar.activation(cT[:, :, :], cT[:, :, :], ACT.Silu).then_inc(cond_ready, 1)
            act.wait_ge(cond_ready, 1)

        @block.vector
        def _(dve):
            nc.vector.memset(cT[:, :, :], 0.0).then_inc(padded, 1)
            for b in range(2):
                for t in range(2):
                    dve.sem_inc(k.ps_free[b][t], 1)

        @block.gpsimd
        def _(pool):
            own = Chain(pool, made)
            own.did(nc.gpsimd.memset(k.ident[:, :], 0.0))
            own.did(nc.gpsimd.memset(k.ones[:, :], 1.0))
            own.did(nc.gpsimd.memset(k.neg_ones[:, :], -1.0))
            own.did(nc.gpsimd.memset(k.neg_tri[:, :], -1.0))
            own.did(nc.gpsimd.memset(k.tri_le[:, :], 1.0))
            own.did(nc.gpsimd.memset(k.tri_lt[:, :], 1.0))
            own.did(nc.gpsimd.memset(k.same[:, :], 1.0))
            own.did(nc.gpsimd.memset(k.member[:, :], 1.0))
            own.settle()

            def keep(m, pattern, base, mult, op, fill):
                own.did(nc.gpsimd.affine_select(out=m, in_=m, pattern=pattern, base=base, channel_multiplier=mult,
                                                compare_op=op, fill=fill))

            keep(k.ident[:, :], [[-1, P]], 0, 1, ALU.not_equal, 1.0)
            keep(k.neg_tri[:, :], [[-1, P]], 0, 1, ALU.is_ge, 0.0)
            keep(k.tri_le[:, :], [[1, P]], 0, -1, ALU.is_ge, 0.0)
            keep(k.tri_lt[:, :], [[1, P]], 0, -1, ALU.is_gt, 0.0)
            same = k.same[:, :].rearrange("j (b q) -> j b q", q=NQ)
            keep(same, [[-NQ, NB], [0, NQ]], 0, 1, ALU.is_ge, 0.0)
            keep(k.member[:, :], [[-NQ, NB]], 0, 1, ALU.is_ge, 0.0)
            own.settle()
            keep(same, [[NQ, NB], [0, NQ]], NQ - 1, -1, ALU.is_ge, 0.0)
            keep(k.member[:, :], [[NQ, NB]], NQ - 1, -1, ALU.is_ge, 0.0)
            own.settle()
            own.step(nc.gpsimd.tensor_tensor(k.tri_same[:, :], k.same[:, :], k.tri_le[0:TS, 0:TS], ALU.mult))


class Part:

    def __init__(self, w, steps, products, take, scalar_takes_all=False, beside=None):
        self.source = w
        self.w, self.rounds, self.products, self.take = w.rearrange("(k p) n -> p k n", p=P), steps // 2, products, take
        self.scalar_takes_all, self.beside = scalar_takes_all, beside


def feature_products(nc, x_hi, x_lo, kt):
    def products(hi, lo, t, ps):
        for h in range(2):
            cols = slice(h * HALF, (h + 1) * HALF)
            for j in range(kt):
                f = slice(t * P, (t + 1) * P)
                for n, (w, x) in enumerate(((hi, x_hi), (hi, x_lo), (lo, x_hi))):
                    last = nc.tensor.matmul(ps[:, h, 0:HALF], w[:, j, f], x(j)[:, cols],
                                            start=(j == 0 and n == 0), stop=(j == kt - 1 and n == 2))
        return last
    return products


class Slots:

    def __init__(self, k, name, kt, w, ctx):
        self.k = k
        self.aim(w)
        self.raw = [k.sb(f"{name}_w{b}", [P, kt, 256], ctx=ctx) for b in range(2)]
        self.lo = [k.split_view(f"{name}_w{b}", [P, kt, 256]) for b in range(2)]
        self.hi = [k.sb(f"{name}_hi{b}", [P, kt, 256], F32R, ctx=ctx) for b in range(2)]

    def aim(self, w):
        self.first, self.ahead = w.rearrange("(k p) n -> p k n", p=P), False

    def load(self, sp):
        for b in range(2):
            sp.dma_start(self.raw[b][:, :, :], self.first[:, :, b * 256:(b + 1) * 256]).then_inc(self.k.w_ready[b], 16)

    def split_first(self, pool):
        k = self.k
        self.ahead = True
        pool.wait_ge(k.w_ready[0], 16 * (k.rounds + 1))
        k.nc.gpsimd.tensor_copy(self.hi[0][:, :, :], self.raw[0][:, :, :]).then_inc(k.w_hi[0], 1)
        pool.wait_ge(k.w_hi[0], k.rounds + 1)
        k.nc.gpsimd.tensor_tensor(self.lo[0][:, :, :], self.raw[0][:, :, :], self.hi[0][:, :, :], ALU.subtract)\
         .then_inc(k.w_lo[0], 1)
        pool.wait_ge(k.w_lo[0], k.rounds + 1)


def phase_project(k, name, kt, parts, slots=None):
    nc = k.nc
    base = k.rounds
    with ExitStack() as ctx:
        slots = slots or Slots(k, name, kt, parts[0].source, ctx)
        raw, lo, hi = slots.raw, slots.lo, slots.hi
        ps = [[k.ps(f"{name}_ps{b}{t}", [P, 2, 512], ctx) for t in range(2)] for b in range(2)]
        firsts = []
        for part in parts:
            firsts.append(k.rounds)
            k.rounds += part.rounds

        def each_round(eng, body, unroll=lambda part: False):
            for n, part in enumerate(parts):
                final = n == len(parts) - 1
                if unroll(part):
                    for i in range(part.rounds):
                        body(part, i, firsts[n], not (final and i == part.rounds - 1))
                else:
                    whole = part.rounds - final
                    if whole > 1:
                        with eng.Fori(0, whole) as i:
                            body(part, i, firsts[n], True)
                    elif whole == 1:
                        body(part, 0, firsts[n], True)
                    if final:
                        body(part, part.rounds - 1, firsts[n], False)

        with nc.Block() as block:
            @block.sync
            def _(sp):
                if not slots.ahead:
                    slots.load(sp)
                for n, part in enumerate(parts):
                    a = 1 if n == 0 else 0
                    if part.rounds - a > 0:
                        with sp.Fori(0, part.rounds - a) as i:
                            for b in range(2):
                                sp.wait_ge(k.mm_done[b][1], i + (firsts[n] + a))
                                sp.dma_start(raw[b][:, :, :], part.w[:, :, bass.ds(i * 512 + (a * 512 + b * 256), 256)])\
                                  .then_inc(k.w_ready[b], 16)

            @block.tensor
            def _(pe):
                def body(part, i, first, _):
                    for b in range(2):
                        pe.wait_ge(k.w_lo[b], i + (first + 1))
                        for t in range(2):
                            pe.wait_ge(k.ps_free[b][t], i + (first + 1))
                            part.products(hi[b], lo[b], t, ps[b][t]).then_inc(k.mm_done[b][t], 1)
                each_round(pe, body)

            @block.vector
            def _(dve):
                def low(b, r):
                    dve.wait_ge(k.w_hi[b], r)
                    nc.vector.tensor_tensor(lo[b][:, :, :], raw[b][:, :, :], hi[b][:, :, :], ALU.subtract)\
                      .then_inc(k.w_lo[b], 1)

                def body(part, i, first, more):
                    for b in range(2):
                        if b == 0:
                            low(1, i + (first + 1))
                        elif more:
                            low(0, i + (first + 2))
                        if part.beside:
                            part.beside[0](dve, 2 * i + b)
                        if not part.scalar_takes_all:
                            dve.wait_ge(k.mm_done[b][0], i + (first + 1))
                            part.take[0](i * 4 + 2 * b, ps[b][0]).then_inc(k.ps_free[b][0], 1)

                if not slots.ahead:
                    low(0, base + 1)
                each_round(dve, body, lambda part: part.beside)

            @block.scalar
            def _(act):
                def high(b, r):
                    act.wait_ge(k.w_ready[b], r * 16)
                    nc.scalar.activation(hi[b][:, :, :], raw[b][:, :, :], ACT.Copy).then_inc(k.w_hi[b], 1)

                def body(part, i, first, more):
                    for b in range(2):
                        if b == 0:
                            high(1, i + (first + 1))
                        elif more:
                            high(0, i + (first + 2))
                        if part.beside:
                            part.beside[1](act, 2 * i + b)
                        for t in range(0 if part.scalar_takes_all else 1, 2):
                            act.wait_ge(k.mm_done[b][t], i + (first + 1))
                            part.take[t](i * 4 + (2 * b + t), ps[b][t]).then_inc(k.ps_free[b][t], 1)

                if not slots.ahead:
                    high(0, base + 1)
                each_round(act, body, lambda part: part.beside)


def by_half(dst):
    return dst.rearrange("p (h t) -> p h t", h=2)


def copies_to(nc, dst, first=0, pad=0):
    def at(tile):
        return by_half(dst[:, bass.ds(tile + first, 1), pad:pad + T].rearrange("p a t -> p (a t)"))
    return (lambda tile, ps: nc.vector.tensor_copy(at(tile), ps[:, :, 0:HALF]),
            lambda tile, ps: nc.scalar.activation(at(tile), ps[:, :, 0:HALF], ACT.Copy))


class AdaWeights:
    COLS = 2048

    def __init__(self, k, name, parts, slots, ctx):
        self.k, self.parts, self.slots = k, parts, slots
        self.w = k.sb(f"{name}_w", [P, slots, self.COLS], ctx=ctx)
        self.rows = k.sb(f"{name}_rows", [P, 512], ctx=ctx)
        self.ready = [k.sem(f"{name}_ready{j}") for j in range(slots)]
        self.used, self.copied, self.turned, self.out, self.folded = (
            k.sem(f"{name}_{n}") for n in ("used", "copied", "turned", "out", "folded"))

    def load(self, sp, part, j):
        layer, third = self.parts[part]
        slot = (part * KT + j) % self.slots
        sp.dma_start(self.w[:, slot, :], self.k.io["ada_w"][layer][j * P:(j + 1) * P,
                                                                  third * self.COLS:(third + 1) * self.COLS])\
          .then_inc(self.ready[slot], 16)

    def products(self, sum_ps, part, j):
        nc = self.k.nc
        for g in range(4):
            last = nc.tensor.matmul(sum_ps[32 * g:32 * g + 32, :], self.k.cT[:, j, :],
                                    self.w[:, (part * KT + j) % self.slots, g * 512:(g + 1) * 512], start=(j == 0),
                                    stop=(j == KT - 1), skip_group_check=True)
        last.then_inc(self.used, 1)

    def turn(self, turn_ps):
        for c in range(4):
            last = self.k.nc.tensor.transpose(turn_ps[:, c * P:(c + 1) * P], self.rows[:, c * P:(c + 1) * P],
                                              self.k.ident[:, :])
        last.then_inc(self.turned, 1)

    def store(self, turn_ps, part):
        k, nc = self.k, self.k.nc
        layer, third = self.parts[part]
        tiles = self.COLS // P
        m0 = layer * 48 + third * tiles
        bias0 = COLS["ada_b"][0] + m0
        nc.vector.tensor_tensor(
            k.mod[:, m0:m0 + tiles, :].rearrange("p (g c) r -> p g c r", g=4),
            turn_ps.rearrange("p (c g r) -> p g c r", c=4, g=4)[:, :, :, 0:NC9],
            k.small[:, bias0:bias0 + tiles].rearrange("p (g c) -> p g c", g=4)
            .unsqueeze(3).to_broadcast([P, 4, 4, NC9]), ALU.add).then_inc(self.out, 1)

    def fold(self, dve, scales):
        k = self.k
        for layer, chunk, gain in scales:
            s = k.mod_tiles(layer, chunk)
            g = k.col(gain, layer * KT, KT).unsqueeze(2).to_broadcast([P, KT, NC9])
            k.nc.vector.scalar_tensor_tensor(out=s, in0=s, scalar=1.0, in1=g, op0=ALU.add, op1=ALU.mult)\
             .then_inc(self.folded, 1)
        dve.wait_ge(self.folded, len(scales))


def phase_ada(k, ada):
    nc = k.nc
    with ExitStack() as ctx:
        ps = k.ps("ada_ps", [P, 512], ctx)
        with nc.Block() as block:
            @block.tensor
            def _(pe):
                for j in range(KT):
                    pe.wait_ge(ada.ready[j], 16)
                    ada.products(ps, 0, j)
                pe.wait_ge(ada.copied, 1)
                ada.turn(ps[:, :])

            @block.vector
            def _(dve):
                dve.wait_ge(ada.turned, 1)
                ada.store(ps[:, :], 0)
                dve.wait_ge(ada.out, 1)
                ada.fold(dve, [(0, 1, "ln_mix")])

            @block.scalar
            def _(act):
                act.wait_ge(ada.used, KT)
                nc.scalar.activation(ada.rows[:, :], ps[:, :], ACT.Copy).then_inc(ada.copied, 1)


def phase_norm(k, name, layer, chunk, h_hi=None, slots=None):
    nc = k.nc
    squared, summed, root, scaled = (k.sem(f"{name}_{s}") for s in ("squared", "summed", "root", "scaled"))
    root_in, own_d, own_a = (k.sem(f"{name}_{s}") for s in ("root_in", "own_d", "own_a"))
    sample_done, high, low, added = (k.sem(f"{name}_{s}") for s in ("sample", "high", "low", "added"))
    with ExitStack() as ctx:
        sq = k.sb(f"{name}_sq", [P, 2, T], ctx=ctx)
        acc = k.sb(f"{name}_acc", [P, T], ctx=ctx)
        rstd = k.sb(f"{name}_rstd", [P, T], ctx=ctx)
        ps = k.ps(f"{name}_ps", [P, 2, 512], ctx)
        with nc.Block() as block:
            @block.scalar
            def _(act):
                nc.scalar.activation(acc[:, :], k.xT[:, 0, :], ACT.Square).then_inc(squared, 1)
                for j in range(1, KT):
                    if j >= 3:
                        act.wait_ge(added, j - 2)
                    nc.scalar.activation(sq[:, j % 2, :], k.xT[:, j, :], ACT.Square).then_inc(squared, 1)
                act.wait_ge(root_in, 1)
                nc.scalar.activation(rstd[:, :], rstd[:, :], ACT.Sqrt).then_inc(root, 1)
                for j in range(KT):
                    act.wait_ge(scaled, j + 1)
                    if layer is not None:
                        nc.scalar.activation(k.hT[:, j, 0:TP], k.hT[:, j, 0:TP], ACT.Identity,
                                             bias=k.mod[:, layer * 48 + chunk * KT + j, 0:1],
                                             scale=k.mod[:, layer * 48 + (chunk + 1) * KT + j, 0:1]).then_inc(own_a, 1)
                if layer is not None:
                    act.wait_ge(own_a, KT)
                if h_hi is not None:
                    act.wait_ge(sample_done, 1)
                    for j in range(KT):
                        nc.scalar.activation(h_hi[:, j, :], k.hT[:, j, :], ACT.Copy).then_inc(high, 1)

            @block.tensor
            def _(pe):
                pe.wait_ge(added, KT - 1)
                for h in range(2):
                    last = nc.tensor.matmul(ps[:, h, 0:HALF], k.ones[:, :], acc[:, h * HALF:(h + 1) * HALF],
                                            start=True, stop=True)
                last.then_inc(summed, 1)

            @block.vector
            def _(dve):
                own = Chain(dve, own_d)
                for j in range(1, KT):
                    dve.wait_ge(squared, j + 1)
                    if j >= 2:
                        dve.wait_ge(added, j - 1)
                    nc.vector.tensor_tensor(acc[:, :], acc[:, :], sq[:, j % 2, :], ALU.add).then_inc(added, 1)
                dve.wait_ge(summed, 1)
                nc.vector.tensor_scalar(by_half(rstd[:, :]), ps[:, :, 0:HALF], 1.0 / D, EPS, ALU.mult, ALU.add)\
                  .then_inc(root_in, 1)
                dve.wait_ge(root, 1)
                own.step(nc.vector.reciprocal(rstd[:, :], rstd[:, :]))
                for j in range(KT):
                    if layer is None:
                        nc.vector.scalar_tensor_tensor(out=k.hT[:, j, :], in0=k.xT[:, j, :],
                                                       scalar=k.col("final_g", j), in1=rstd[:, :],
                                                       op0=ALU.mult, op1=ALU.mult).then_inc(scaled, 1)
                    else:
                        nc.vector.tensor_tensor(k.hT[:, j, :], k.xT[:, j, :], rstd[:, :], ALU.mult).then_inc(scaled, 1)
                dve.wait_ge(scaled, KT)
                if layer is not None:
                    hs = k.hT[:, :, TP:T].rearrange("p k (b q) -> p k b q", q=NQ)
                    a = k.mod_tiles(layer, chunk + 1)[:, :, 1:NC9].unsqueeze(3).to_broadcast([P, KT, NB, NQ])
                    s = k.mod_tiles(layer, chunk)[:, :, 1:NC9].unsqueeze(3).to_broadcast([P, KT, NB, NQ])
                    own.step(nc.vector.tensor_tensor(hs, hs, a, ALU.mult))
                    nc.vector.tensor_tensor(hs, hs, s, ALU.add).then_inc(sample_done, 1)
                    dve.wait_ge(sample_done, 1)
                if h_hi is not None:
                    for j in range(KT):
                        dve.wait_ge(high, j + 1)
                        nc.vector.tensor_tensor(k.hT_r[:, j, :], k.hT[:, j, :], h_hi[:, j, :], ALU.subtract)\
                          .then_inc(low, 1)
                    dve.wait_ge(low, KT)

            if slots:
                @block.sync
                def _(sp):
                    slots.load(sp)

                @block.gpsimd
                def _(pool):
                    slots.split_first(pool)

            if layer is None:
                stored = k.sem("y_stored")

                @block.sync
                def _(sp):
                    y = k.io["yT"].rearrange("(k p) t -> p k t", p=P)
                    for j in range(KT):
                        sp.wait_ge(scaled, j + 1)
                        sp.dma_start(y[:, j, :], k.hT[:, j, :]).then_inc(stored, 16)
                    sp.wait_ge(stored, 16 * KT)


def phase_qkv(k, vtok, h_hi, slots):
    nc = k.nc

    def scaled(first, scale):
        at = lambda tile: by_half(k.qk[:, bass.ds(tile + first, 1), :].rearrange("p a t -> p (a t)"))
        return (lambda tile, ps: nc.vector.tensor_scalar(at(tile), ps[:, :, 0:HALF], scale, None, ALU.mult),
                lambda tile, ps: nc.scalar.activation(at(tile), ps[:, :, 0:HALF], ACT.Copy, scale=scale))

    def value_products(hi, lo, t, ps):
        for i, bank, c in ((0, 0, 0), (1, 1, 0)) if t == 0 else ((2, 0, 0), (3, 1, 0), (4, 1, 256)):
            a, m = TOK[i]
            for j in range(KT):
                for n, (x, w) in enumerate(((h_hi, hi), (k.hT_r, hi), (h_hi, lo))):
                    last = nc.tensor.matmul(ps[0:m, bank, c:c + 256], x[:, j, a:a + m], w[:, j, :],
                                            start=(j == 0 and n == 0), stop=(j == KT - 1 and n == 2))
        return last

    def take_first(tile, ps):
        return nc.vector.tensor_copy(vtok[:, 0:2, bass.ds(tile * P, 256)], ps[:, :, 0:256])

    def take_second(tile, ps):
        nc.scalar.activation(vtok[0:TS, 4, bass.ds(tile * P - P, 256)], ps[0:TS, 1, 256:512], ACT.Copy)
        return nc.scalar.activation(vtok[:, 2:4, bass.ds(tile * P - P, 256)], ps[:, :, 0:256], ACT.Copy)

    w = k.io["mix_w_in"]
    feature = feature_products(nc, lambda j: h_hi[:, j, :], lambda j: k.hT_r[:, j, :], KT)
    phase_project(k, "qkv", KT, [Part(w[:, 2576:3600], 4, feature, scaled(0, HD ** -0.5)),
                                 Part(w[:, 3600:4624], 4, feature, scaled(KT, 1.0)),
                                 Part(w[:, 4624:5648], 4, value_products, (take_first, take_second))], slots)


def phase_attention_prompt(k, vtok, mixT, qn, kn, ada):
    nc = k.nc
    units = [(h, j) for h in range(H) for j in (3, 2, 1, 0)]
    NZ, NSP, NW, LAG = 6, 8, 4, 3
    AT = [1 + 5 * j // 4 for j in range(KT)]
    SPAN = AT[-1] + 3
    parts = range(len(ada.parts))
    ada_at = {SPAN * part + AT[j]: (part, j) for part in parts for j in range(KT)}
    copy_at, turn_at, store_at = ({SPAN * part + AT[-1] + d: part for part in parts} for d in (1, 2, 3))
    assert max(store_at) < len(units)
    names = ("z_done", "zb_done", "e_done", "l_done", "sp_done", "spm_done", "cum_done", "w_done", "wm_done",
             "pv_done", "o_done", "hi_done", "lo_done", "signs")
    s = {n: k.sem("ap_" + n) for n in names}
    kept, stored = k.sem("qk_kept"), k.sem("kv_stored")
    with ExitStack() as ctx:
        zb = k.sb("ap_zb", [P, 3, 512], ctx=ctx)
        sp_t = k.sb("ap_sp", [P, NSP, 512], ctx=ctx)
        sp_lo = k.split_view("ap_sp", [P, NSP, 512])
        sp_hi = k.sb("ap_sp_hi", [P, NSP, 512], F32R, ctx=ctx)
        neg_tri_r, neg_ones_r = k.sb("neg_tri_r", [P, P], F32R, ctx=ctx), k.sb("neg_ones_r", [P, P], F32R, ctx=ctx)
        w_t = k.sb("ap_w", [P, NW, 512], ctx=ctx)
        z_ps = [k.ps(f"ap_z{i}", [P, 512], ctx) for i in range(NZ)]
        o_ps = k.ps("ap_o", [P, 512], ctx)
        ada_ps = k.ps("ap_ada", [P, 512], ctx)
        n_units = len(units)

        with nc.Block() as block:
            @block.sync
            def _(sp):
                stores = [(k.io["kT"], k.kT)] + [(k.io["v"][a:a + m, :], vtok[0:m, i, :])
                                                 for i, (a, m) in enumerate(TOK)]
                for m in range(len(ada.parts) * KT):
                    if m >= ada.slots:
                        sp.wait_ge(ada.used, m - ada.slots + 1)
                        if stores:
                            sp.dma_start(*stores.pop()).then_inc(stored, 16)
                    ada.load(sp, m // KT, m % KT)
                sp.wait_ge(stored, 16 * (1 + TT))

            @block.tensor
            def _(pe):
                def scores(u):
                    h, j = units[u]
                    r = slice(64 * (h % 2), 64 * (h % 2) + 64)
                    if u >= NZ:
                        pe.wait_ge(s["w_done"], u - NZ + 1)
                    nc.tensor.matmul(z_ps[u % NZ][:, j * P:512], k.kT[r, h // 2, j * P:(j + 1) * P],
                                     k.qT[r, h // 2, j * P:TP], start=True, stop=False, skip_group_check=True)\
                      .then_inc(s["z_done"], 1)

                def cumulate(u):
                    h, j = units[u]
                    pe.wait_ge(s["lo_done"], u + 1)
                    if u == 0:
                        pe.wait_ge(s["signs"], 2)
                    z = z_ps[u % NZ]
                    for part in (sp_lo, sp_hi):
                        last = nc.tensor.matmul(z[:, j * P:512], neg_tri_r[:, :], part[:, u % NSP, j * P:512],
                                                start=False, stop=(j == 3 and part is sp_hi), skip_group_check=True)
                    for back in range(1, 4 - j):
                        jj = j + back
                        for part in (sp_lo, sp_hi):
                            last = nc.tensor.matmul(z[:, jj * P:512], neg_ones_r[:, :],
                                                    part[:, (u - back) % NSP, jj * P:512], start=False,
                                                    stop=(jj == 3 and part is sp_hi), skip_group_check=True)
                    last.then_inc(s["cum_done"], 1)

                def values(u):
                    h, j = units[u]
                    r = slice(64 * (h % 2), 64 * (h % 2) + 64)
                    pe.wait_ge(s["wm_done"], u + 1)
                    if j == 3 and h % 2 == 0 and h >= 2:
                        pe.wait_ge(s["o_done"], h // 2)
                    nc.tensor.matmul(o_ps[r, j * P:512], vtok[:, j, h * HD:(h + 1) * HD],
                                     w_t[:, u % NW, j * P:512], start=(j == 3), stop=(j == 0), skip_group_check=True)\
                      .then_inc(s["pv_done"], 1)

                for u in range(n_units + LAG + 2):
                    if u < n_units:
                        scores(u)
                    if u in ada_at:
                        part, j = ada_at[u]
                        if j == 0 and part:
                            pe.wait_ge(ada.out, part)
                        m = part * KT + j
                        pe.wait_ge(ada.ready[m % ada.slots], 16 * (m // ada.slots + 1))
                        ada.products(ada_ps, part, j)
                    if u in turn_at:
                        pe.wait_ge(ada.copied, turn_at[u] + 1)
                        ada.turn(ada_ps[:, :])
                    if LAG <= u < n_units + LAG:
                        cumulate(u - LAG)
                    if u >= LAG + 2:
                        values(u - LAG - 2)

            @block.vector
            def _(dve):
                def bounded(u):
                    h, j = units[u]
                    dve.wait_ge(s["z_done"], u + 1)
                    if u >= 3:
                        dve.wait_ge(s["e_done"], u - 2)
                    nc.vector.tensor_scalar(zb[:, u % 3, j * P:512], z_ps[u % NZ][:, j * P:512],
                                            k.col("sb_bias", h), 40.0, ALU.add, ALU.min).then_inc(s["zb_done"], 1)

                def softplus(u):
                    h, j = units[u]
                    dve.wait_ge(s["l_done"], u + 1)
                    nc.vector.scalar_tensor_tensor(out=sp_t[:, u % NSP, j * P:512], in0=z_ps[u % NZ][:, j * P:512],
                                                   scalar=k.col("sb_bias", h), in1=sp_t[:, u % NSP, j * P:512],
                                                   op0=ALU.add, op1=ALU.max).then_inc(s["sp_done"], 1)

                def low(u):
                    h, j = units[u]
                    dve.wait_ge(s["hi_done"], u + 1)
                    nc.vector.tensor_tensor(sp_lo[:, u % NSP, j * P:512], sp_t[:, u % NSP, j * P:512],
                                            sp_hi[:, u % NSP, j * P:512], ALU.subtract).then_inc(s["lo_done"], 1)

                def output(pair):
                    dve.wait_ge(s["pv_done"], 8 * (pair + 1))
                    nc.vector.tensor_copy(mixT[:, KT + pair, 0:TP], o_ps[:, :]).then_inc(s["o_done"], 1)

                for u in range(n_units + 2):
                    if u < n_units:
                        bounded(u)
                    if 1 <= u <= n_units:
                        softplus(u - 1)
                    if u >= 2:
                        low(u - 2)
                    if u >= 13 and (u - 13) % 8 == 0:
                        output((u - 13) // 8)
                    if u in copy_at:
                        dve.wait_ge(ada.used, KT * (copy_at[u] + 1))
                        nc.vector.tensor_copy(ada.rows[:, :], ada_ps[:, :]).then_inc(ada.copied, 1)
                    if u in store_at:
                        dve.wait_ge(ada.turned, store_at[u] + 1)
                        ada.store(ada_ps[:, :], store_at[u])
                for pair in range((n_units + 1 - 13) // 8 + 1, H // 2):
                    output(pair)
                dve.wait_ge(ada.out, len(ada.parts))
                ada.fold(dve, [(0, 4, "ln_ffn"), (1, 1, "ln_mix"), (1, 4, "ln_ffn")])
                dve.wait_ge(s["o_done"], H // 2)

            @block.scalar
            def _(act):
                nc.scalar.preload_act_table_set("natural_log_exp_and_others")

                def exponential(u):
                    h, j = units[u]
                    act.wait_ge(s["zb_done"], u + 1)
                    if u >= NSP:
                        act.wait_ge(s["cum_done"], (u - NSP) // 4 * 4 + 4)
                    nc.scalar.activation(sp_t[:, u % NSP, j * P:512], zb[:, u % 3, j * P:512], ACT.Exp)\
                      .then_inc(s["e_done"], 1)
                    act.wait_ge(s["e_done"], u + 1)
                    nc.scalar.activation(sp_t[:, u % NSP, j * P:512], sp_t[:, u % NSP, j * P:512], ACT.Ln, bias=1.0)\
                      .then_inc(s["l_done"], 1)

                def weights(u):
                    h, j = units[u]
                    act.wait_ge(s["cum_done"], u + 1)
                    if u >= NW:
                        act.wait_ge(s["pv_done"], u - NW + 1)
                    nc.scalar.activation(w_t[:, u % NW, j * P:512], z_ps[u % NZ][:, j * P:512], ACT.Exp,
                                         bias=k.col("sb_bias", h)).then_inc(s["w_done"], 1)

                def high(u):
                    h, j = units[u]
                    act.wait_ge(s["spm_done"], u + 1)
                    nc.scalar.activation(sp_hi[:, u % NSP, j * P:512], sp_t[:, u % NSP, j * P:512], ACT.Copy)\
                      .then_inc(s["hi_done"], 1)

                nc.scalar.activation(neg_tri_r[:, :], k.neg_tri[:, :], ACT.Copy).then_inc(s["signs"], 1)
                nc.scalar.activation(neg_ones_r[:, :], k.neg_ones[:, :], ACT.Copy).then_inc(s["signs"], 1)
                for u in range(n_units + LAG):
                    if u < n_units:
                        exponential(u)
                    if u >= LAG:
                        weights(u - LAG)
                    if 1 <= u <= n_units:
                        high(u - 1)

                for dst, src in ((qn, k.qT), (kn, k.kT)):
                    nc.scalar.activation(dst[:, :, :, :], src[:, :, TP:T].rearrange("p k (b q) -> p k b q", q=NQ),
                                         ACT.Copy).then_inc(kept, 1)
                act.wait_ge(kept, 2)

            @block.gpsimd
            def _(pool):
                def mask(tile, buf, ready, done, u):
                    h, j = units[u]
                    pool.wait_ge(ready, u + 1)
                    d = tile[:, buf, j * P:(j + 1) * P]
                    nc.gpsimd.affine_select(out=d, in_=d, pattern=[[1, P]], base=0, channel_multiplier=-1,
                                            compare_op=ALU.is_gt, fill=0.0).then_inc(done, 1)

                for u in range(n_units + LAG):
                    if u < n_units:
                        mask(sp_t, u % NSP, s["sp_done"], s["spm_done"], u)
                    if u >= LAG:
                        mask(w_t, (u - LAG) % NW, s["w_done"], s["wm_done"], u - LAG)


def phase_attention_sample(k, mixT, qn, kn):
    nc = k.nc
    RING, ROUNDS = 4, NB // 2
    KEYS = PAGES * PAGE
    names = ("table", "zn", "zb", "ln", "sp", "z", "arg", "w", "tr", "wt", "pv", "masked", "oc", "turn",
             "out", "own_d", "cleared", "padded", "nb", "ne", "narg", "nw", "ntr", "nwt", "e_own")
    s = {n: k.sem("as_" + n) for n in names}
    arrived = [k.sem(f"as_slot{r}") for r in range(RING)]
    vn_ready = [k.sem(f"as_vn{r}") for r in range(2)]
    order = [("k", 0), ("k", 1)]
    for t in range(ROUNDS):
        order.append(("v", t))
        if t + 2 < ROUNDS:
            order.append(("k", t + 2))
    place = {what: n for n, what in enumerate(order)}
    with ExitStack() as ctx:
        pages = k.sb("as_pages", [P, RING, PAGES, D], ctx=ctx)
        vn = k.sb("as_vn", [NQ, 2, 2, D], ctx=ctx)
        qz = k.sb("qz", [P, KT, NB, 32], ctx=ctx)
        table = k.sb("as_table", [1, NB * PAGES], I32, ctx=ctx)
        zb = k.sb("as_zb", [P, 2, KEYS], ctx=ctx)
        sp_t = k.sb("as_sp", [P, 2, 1 + KEYS], ctx=ctx)
        cum = k.sb("as_cum", [P, 2, 1 + KEYS], ctx=ctx)
        w_t = k.sb("as_w", [P, 2, KEYS], ctx=ctx)
        wT = k.sb("as_wT", [P, 2, PAGES, P], ctx=ctx)
        om = k.sb("as_om", [P, 8, HD], ctx=ctx)
        oc = k.sb("as_oc", [P, 2, HD], ctx=ctx)
        z_n = k.sb("as_zn_sb", [P, ROUNDS, NQ], ctx=ctx)
        sp_n = k.sb("as_sp_n", [P, ROUNDS, NQ], ctx=ctx)
        w_n = k.sb("as_w_n", [P, ROUNDS, NQ], ctx=ctx)
        wT_n = k.sb("as_wT_n", [NQ, ROUNDS, P], ctx=ctx)
        z_ps = [k.ps(f"as_z{i}", [P, KEYS], ctx) for i in range(2)]
        zn_ps = k.ps("as_znps", [P, 512], ctx)
        tr_ps = k.ps("as_tr", [P, PAGES, P], ctx)
        o_ps = [k.ps(f"as_o{i}", [P, 512], ctx) for i in range(2)]
        turn_ps = k.ps("as_turn", [P, 2, 8, 2, NQ], ctx)
        bias = k.col("sb_rows", 0)

        def groups():
            return [(slice(32 * (2 * bb + o), 32 * (2 * bb + o) + 32), bb, 4 * o) for bb in range(2) for o in range(2)]

        with nc.Block() as block:
            @block.sync
            def _(sp):
                sp.dma_start(table[:, :], k.io["page_table"]).then_inc(s["table"], 16)
                sp.wait_ge(s["table"], 16)
                for n, (kind, t) in enumerate(order):
                    if n >= 2:
                        was, wt = order[n - 2]
                        sp.wait_ge(s["z"] if was == "k" else s["pv"], wt + 1)
                    for bb in range(2):
                        b, r = 2 * t + bb, 2 * (n % 2) + bb
                        for p in range(PAGES):
                            page = sp.value_load(table[0:1, b * PAGES + p:b * PAGES + p + 1], min_val=0,
                                                 max_val=POOL_PAGES - 1)
                            src = k.io["cache_kT"] if kind == "k" else k.io["cache_v"]
                            sp.dma_start(pages[:, r, PAGES - 1 - p, :],
                                         src[bass.ds(page, 1), :, :].rearrange("a p n -> p (a n)"))\
                              .then_inc(arrived[r], 16)
                        if kind == "v":
                            if t >= 2:
                                sp.wait_ge(s["pv"], t - 1)
                            sp.dma_start(vn[:, t % 2, bb, :], k.io["v"][TP + NQ * b:TP + NQ * (b + 1), :])\
                              .then_inc(vn_ready[t % 2], 16)

            @block.tensor
            def _(pe):
                def arrive(what):
                    n = place[what]
                    for bb in range(2):
                        pe.wait_ge(arrived[2 * (n % 2) + bb], 16 * PAGES * (n // 2 + 1))
                    return 2 * (n % 2)

                pe.wait_ge(s["padded"], 2 * KT)
                for t in range(ROUNDS):
                    for j in range(4):
                        for r, bb, j0 in groups():
                            last = nc.tensor.matmul(zn_ps[r, t * NQ:(t + 1) * NQ], qz[:, j0 + j, 2 * t + bb, :],
                                                    kn[:, j0 + j, 2 * t + bb, :], start=(j == 0), stop=(j == 3),
                                                    skip_group_check=True)
                last.then_inc(s["zn"], 1)

                def scores(t):
                    if t >= 2:
                        pe.wait_ge(s["arg"], t - 1)
                    slot = arrive(("k", t))
                    for j in range(4):
                        for r, bb, j0 in groups():
                            last = nc.tensor.matmul(z_ps[t % 2][r, :], qz[:, j0 + j, 2 * t + bb, :],
                                                    pages[:, slot + bb, :, (j0 + j) * P:(j0 + j + 1) * P],
                                                    start=(j == 0), stop=(j == 3), skip_group_check=True)
                    last.then_inc(s["z"], 1)

                def turned_weights(t):
                    pe.wait_ge(s["w"], t + 1)
                    if t >= 1:
                        pe.wait_ge(s["wt"], t)
                    for p in range(PAGES):
                        last = nc.tensor.transpose(tr_ps[:, p, :], w_t[:, t % 2, p * P:(p + 1) * P], k.ident[:, :])
                    last.then_inc(s["tr"], 1)

                def sums(t):
                    pe.wait_ge(s["wt"], t + 1)
                    slot = arrive(("v", t))
                    pe.wait_ge(vn_ready[t % 2], 32 * (t // 2 + 1))
                    if t >= 2:
                        pe.wait_ge(s["masked"], t - 1)
                    for p in range(PAGES):
                        for r, bb, j0 in groups():
                            nc.tensor.matmul(o_ps[t % 2][r, :], wT[:, t % 2, p, r], pages[:, slot + bb, p, j0 * P:(j0 + 4) * P],
                                             start=(p == 0), stop=False, skip_group_check=True)
                    for r, bb, j0 in groups():
                        last = nc.tensor.matmul(o_ps[t % 2][r, :], wT_n[:, t, r], vn[:, t % 2, bb, j0 * P:(j0 + 4) * P],
                                                start=False, stop=True, skip_group_check=True)
                    last.then_inc(s["pv"], 1)

                def turned_sums(t):
                    pe.wait_ge(s["oc"], t + 1)
                    if t >= 1:
                        pe.wait_ge(s["out"], 2 * t)
                    nc.tensor.transpose(turn_ps[:, :, :, :, :].rearrange("p b j g q -> p (b j g q)"),
                                        oc[:, :, :].rearrange("p d e -> p (d e)"), k.ident[:, :]).then_inc(s["turn"], 1)

                scores(0)
                pe.wait_ge(s["nw"], 2)
                for t in range(ROUNDS):
                    last = nc.tensor.transpose(zn_ps[0:NQ, t * P:(t + 1) * P], w_n[:, t, :], k.ident[:, :])
                last.then_inc(s["ntr"], 1)
                pe.wait_ge(s["nwt"], 1)
                for t in range(ROUNDS):
                    if t + 1 < ROUNDS:
                        scores(t + 1)
                    turned_weights(t)
                    sums(t)
                    if t >= 1:
                        turned_sums(t - 1)
                turned_sums(ROUNDS - 1)

            @block.vector
            def _(dve):
                own = Chain(dve, s["own_d"])
                V = nc.vector
                before = k.col("before", 0, NQ).unsqueeze(1).to_broadcast([P, ROUNDS, NQ])
                V.memset(qz[:, :, :, :], 0.0).then_inc(s["cleared"], 1)
                dve.wait_ge(s["cleared"], 1)
                for j in range(KT):
                    for g in range(2):
                        r = slice(64 * g, 64 * g + 64)
                        c = (2 * (j % 4) + g) * NQ
                        V.tensor_copy(qz[r, j, :, c:c + NQ], qn[r, j, :, :]).then_inc(s["padded"], 1)
                dve.wait_ge(s["zn"], 1)
                own.step(V.tensor_scalar(z_n[:, :, :], zn_ps[:, 0:ROUNDS * NQ].rearrange("p (t n) -> p t n", n=NQ),
                                         bias, None, ALU.add))
                V.tensor_scalar(sp_n[:, :, :], z_n[:, :, :], 40.0, None, ALU.min).then_inc(s["nb"], 1)
                dve.wait_ge(s["ne"], 1)
                own.step(V.tensor_tensor(sp_n[:, :, :], sp_n[:, :, :], z_n[:, :, :], ALU.max))
                own.step(V.tensor_tensor(sp_n[:, :, :], sp_n[:, :, :], before, ALU.mult))
                for n in (2, 1, 0):
                    own.step(V.tensor_tensor(sp_n[:, :, n], sp_n[:, :, n], sp_n[:, :, n + 1], ALU.add))
                own.step(V.tensor_tensor(z_n[:, :, :], z_n[:, :, :], sp_n[:, :, :], ALU.subtract))
                V.tensor_scalar(w_n[:, :, :], z_n[:, :, :], 40.0, None, ALU.min).then_inc(s["narg"], 1)
                dve.wait_ge(s["nw"], 1)
                V.tensor_tensor(w_n[:, :, :], w_n[:, :, :], before, ALU.mult).then_inc(s["nw"], 1)

                def bounded(t):
                    dve.wait_ge(s["z"], t + 1)
                    if t >= 2:
                        dve.wait_ge(s["ln"], t - 1)
                    V.tensor_scalar(zb[:, t % 2, :], z_ps[t % 2][:, :], bias, 40.0, ALU.add, ALU.min)\
                     .then_inc(s["zb"], 1)

                def running(t):
                    own.did(V.tensor_copy(sp_t[:, t % 2, 0:1], sp_n[:, t, 0:1]))
                    dve.wait_ge(s["ln"], t + 1)
                    own.did(V.scalar_tensor_tensor(out=sp_t[:, t % 2, 1:1 + KEYS], in0=z_ps[t % 2][:, :], scalar=bias,
                                                   in1=sp_t[:, t % 2, 1:1 + KEYS], op0=ALU.add, op1=ALU.max))
                    own.settle()
                    own.step(V.tensor_tensor_scan(cum[:, t % 2, :], sp_t[:, t % 2, :], sp_t[:, t % 2, :], 0.0, ALU.add,
                                                  ALU.bypass))
                    if t >= 2:
                        dve.wait_ge(s["tr"], t - 1)
                    V.scalar_tensor_tensor(out=w_t[:, t % 2, :], in0=z_ps[t % 2][:, :], scalar=bias,
                                           in1=cum[:, t % 2, 1:1 + KEYS], op0=ALU.add, op1=ALU.subtract)\
                     .then_inc(s["arg"], 1)

                def result(t):
                    dve.wait_ge(s["pv"], t + 1)
                    V.tensor_tensor(om[:, :, :], o_ps[t % 2][:, :].rearrange("p (h e) -> p h e", e=HD),
                                    k.col("own_head", 0, 8).unsqueeze(2).to_broadcast([P, 8, HD]), ALU.mult)\
                     .then_inc(s["masked"], 1)
                    dve.wait_ge(s["masked"], t + 1)
                    if t >= 1:
                        dve.wait_ge(s["turn"], t)
                    own.step(V.tensor_reduce(oc[:, 0, :].unsqueeze(2), om[:, :, :].rearrange("p h e -> p e h"), AX_X,
                                             ALU.add))
                    V.tensor_copy(oc[:, 1, :], oc[:, 0, :]).then_inc(s["oc"], 1)
                    dve.wait_ge(s["turn"], t + 1)
                    for g in range(2):
                        r = slice(64 * g, 64 * g + 64)
                        for bb in range(2):
                            a = TP + NQ * (2 * t + bb)
                            ins = V.tensor_copy(mixT[r, KT:2 * KT, a:a + NQ], turn_ps[r, bb, :, g, :])
                        ins.then_inc(s["out"], 1)

                bounded(0)
                for t in range(ROUNDS):
                    running(t)
                    if t + 1 < ROUNDS:
                        bounded(t + 1)
                    if t >= 1:
                        result(t - 1)
                result(ROUNDS - 1)
                dve.wait_ge(s["out"], 2 * ROUNDS)

            @block.scalar
            def _(act):
                nc.scalar.preload_act_table_set("natural_log_exp_and_others")
                own = Chain(act, s["e_own"])
                act.wait_ge(s["nb"], 1)
                own.step(nc.scalar.activation(sp_n[:, :, :], sp_n[:, :, :], ACT.Exp))
                nc.scalar.activation(sp_n[:, :, :], sp_n[:, :, :], ACT.Ln, bias=1.0).then_inc(s["ne"], 1)
                act.wait_ge(s["narg"], 1)
                nc.scalar.activation(w_n[:, :, :], w_n[:, :, :], ACT.Exp).then_inc(s["nw"], 1)
                act.wait_ge(s["ntr"], 1)
                nc.scalar.activation(wT_n[:, :, :].rearrange("n t r -> n (t r)"), zn_ps[0:NQ, :], ACT.Copy)\
                  .then_inc(s["nwt"], 1)

                def softplus(t):
                    act.wait_ge(s["zb"], t + 1)
                    if t >= 2:
                        act.wait_ge(s["arg"], t - 1)
                    own.step(nc.scalar.activation(sp_t[:, t % 2, 1:1 + KEYS], zb[:, t % 2, :], ACT.Exp))
                    nc.scalar.activation(sp_t[:, t % 2, 1:1 + KEYS], sp_t[:, t % 2, 1:1 + KEYS], ACT.Ln, bias=1.0)\
                      .then_inc(s["ln"], 1)

                softplus(0)
                for t in range(ROUNDS):
                    act.wait_ge(s["arg"], t + 1)
                    nc.scalar.activation(w_t[:, t % 2, :], w_t[:, t % 2, :], ACT.Exp).then_inc(s["w"], 1)
                    if t + 1 < ROUNDS:
                        softplus(t + 1)
                    act.wait_ge(s["tr"], t + 1)
                    if t >= 2:
                        act.wait_ge(s["pv"], t - 1)
                    nc.scalar.activation(wT[:, t % 2, :, :], tr_ps[:, :, :], ACT.Copy).then_inc(s["wt"], 1)


def phase_ssd_project(k, xc, zs, dt_tok, h_hi):
    nc, io = k.nc, k.io
    loaded, kept_done, stored, own_d, own_a, mult, conv, sample = (
        k.sem("cv_" + n) for n in ("loaded", "kept", "stored", "own_d", "own_a", "mult", "conv", "sample"))
    split, dt_mm, u_done, l_done, pads, act_done = (k.sem("cv_" + n) for n in ("split", "dtmm", "u", "l", "pads", "act"))
    with ExitStack() as ctx:
        raw = k.sb("cv_raw", [P, XT, 3 + T], ctx=ctx)
        raw_s = k.sb("cv_raws", [P, XT, NB, 3 + NQ], ctx=ctx)
        tmp = k.sb("cv_tmp", [P, XT, NB, NQ], ctx=ctx)
        kept = k.sb("cv_kept", [P, XT, 3 + TS], ctx=ctx)
        w_dt = k.sb("cv_wdt", [P, KT, H], ctx=ctx)
        w_dt_hi = k.sb("cv_wdt_hi", [P, KT, H], F32R, ctx=ctx)
        w_dt_lo = k.sb("cv_wdt_lo", [P, KT, H], F32R, ctx=ctx)
        xs = xc[:, :, TP:T].rearrange("p k (b q) -> p k b q", q=NQ)

        with nc.Block() as block:
            @block.sync
            def _(sp):
                sp.dma_start(kept[:, :, :].rearrange("p k t -> p (k t)")[:, 0:XT * NB * 3],
                             io["conv_state"].rearrange("p k b t -> p (k b t)")).then_inc(loaded, 16)
                sp.dma_start(w_dt[:, :, :], io["mix_w_in"][:, 2560:2576].rearrange("(k p) n -> p k n", p=P))\
                  .then_inc(loaded, 16)
                sp.wait_ge(loaded, 32)

            @block.vector
            def _(dve):
                nc.vector.memset(raw[:, :, 0:3], 0.0).then_inc(pads, 1)
                dve.wait_ge(loaded, 32)
                nc.vector.tensor_copy(raw_s[:, :, :, 0:3], kept[:, :, :].rearrange("p k t -> p (k t)")
                                      [:, 0:XT * NB * 3].rearrange("p (k b t) -> p k b t", b=NB, t=3)).then_inc(pads, 1)
                nc.vector.tensor_copy(w_dt_hi[:, :, :], w_dt[:, :, :]).then_inc(split, 1)
                dve.wait_ge(split, 1)
                nc.vector.tensor_tensor(w_dt_lo[:, :, :], w_dt[:, :, :], w_dt_hi[:, :, :], ALU.subtract)\
                  .then_inc(split, 1)
                dve.wait_ge(split, 2)
                dve.wait_ge(pads, 2)

        x_rounds, z_steps = 3, 4
        z_base = k.rounds + x_rounds
        PER = XT // z_steps
        dve_own = {}

        def x_there(eng):
            for b in range(2):
                for t in range(2):
                    eng.wait_ge(k.ps_free[b][t], z_base + 1)

        def conv_vector(dve, step):
            if step == 0:
                dve_own["c"] = Chain(dve, own_d)
            own = dve_own["c"]
            if step == 0:
                x_there(dve)
                own.did(nc.vector.tensor_copy(raw_s[:, :, :, 3:3 + NQ],
                                              raw[:, :, 3 + TP:3 + T].rearrange("p k (b q) -> p k b q", q=NQ)))
                nc.vector.tensor_copy(kept[:, :, 0:3], raw[:, :, TP:TP + 3]).then_inc(kept_done, 1)
                nc.vector.tensor_copy(kept[:, :, 3:3 + TS], raw[:, :, 3 + TP:3 + T]).then_inc(kept_done, 1)
                own.settle()
                w = COLS["conv_w"][0]
                for t in range(4):
                    wide = k.small[:, w + t * XT:w + (t + 1) * XT].unsqueeze(2).unsqueeze(3).to_broadcast([P, XT, NB, NQ])
                    own.step(nc.vector.tensor_tensor(xs if t == 0 else tmp[:, :, :, :], raw_s[:, :, :, t:t + NQ], wide,
                                                     ALU.mult))
                    if t:
                        ins = nc.vector.tensor_tensor(xs, xs, tmp[:, :, :, :], ALU.add)
                        if t < 3:
                            own.step(ins)
                        else:
                            ins.then_inc(sample, 1)
            tiles = range(PER * step, PER * (step + 1))
            for t in range(1, 4):
                for i in tiles:
                    if t == 1:
                        dve.wait_ge(mult, i + 1)
                    else:
                        dve.wait_ge(conv, 3 * PER * step + (t - 2) * PER + i - PER * step + 1)
                    nc.vector.scalar_tensor_tensor(out=xc[:, i, 0:TP], in0=raw[:, i, t:t + TP],
                                                   scalar=k.col("conv_w", t * XT + i), in1=xc[:, i, 0:TP],
                                                   op0=ALU.mult, op1=ALU.add).then_inc(conv, 1)

        def silu(act, step):
            act.wait_ge(sample, 1)
            act.wait_ge(conv, 3 * PER * (step + 1))
            for i in range(PER * step, PER * (step + 1)):
                nc.scalar.activation(xc[:, i, :], xc[:, i, :], ACT.Silu, bias=k.col("conv_b", i)).then_inc(act_done, 1)

        def conv_scalar(act, step):
            if step == 0:
                x_there(act)
            for i in range(PER * step, PER * (step + 1)):
                nc.scalar.activation(xc[:, i, 0:TP], raw[:, i, 0:TP], ACT.Copy, scale=k.col("conv_w", i))\
                  .then_inc(mult, 1)
            if step:
                silu(act, step - 1)

        def z_take(tile, ps):
            return nc.scalar.activation(by_half(zs[:, bass.ds(tile, 1), :].rearrange("p a t -> p (a t)")),
                                        ps[:, :, 0:HALF], ACT.Silu)

        feature = feature_products(nc, lambda j: h_hi[:, j, :], lambda j: k.hT_r[:, j, :], KT)
        phase_project(k, "xbcz", KT, [
            Part(io["mix_w_in"][:, 1024:2560], 2 * x_rounds, feature, copies_to(nc, raw, 0, 3)),
            Part(io["mix_w_in"][:, 0:1024], z_steps, feature, (z_take, z_take), True, (conv_vector, conv_scalar))])

        u = k.sb("cv_u", [P, TT, H], ctx=ctx)
        w1 = k.sb("cv_w1", [P, TT, H], ctx=ctx)
        dt_ln = k.sb("cv_ln", [P, TT, H], ctx=ctx)
        dt_ps = k.ps("cv_dtps", [P, TT, H], ctx)
        with nc.Block() as block:
            @block.sync
            def _(sp):
                sp.dma_start(io["conv_out"], kept[:, :, :]).then_inc(stored, 16)
                sp.wait_ge(stored, 16)

            @block.tensor
            def _(pe):
                for i, (a, m) in enumerate(TOK):
                    for j in range(KT):
                        for n, (x, w) in enumerate(((h_hi, w_dt_hi), (k.hT_r, w_dt_hi), (h_hi, w_dt_lo))):
                            last = nc.tensor.matmul(dt_ps[0:m, i, :], x[:, j, a:a + m], w[:, j, :],
                                                    start=(j == 0 and n == 0), stop=(j == KT - 1 and n == 2))
                last.then_inc(dt_mm, 1)

            @block.vector
            def _(dve):
                own = dve_own["c"]
                own.eng = dve
                own.step(nc.vector.memset(u[:, :, :], 0.0))
                dve.wait_ge(dt_mm, 1)
                bias = k.small[:, COLS["dt_bias"][0]:COLS["dt_bias"][1]]
                own.step(nc.vector.tensor_tensor(u[:, 0:4, :], dt_ps[:, 0:4, :],
                                                 bias.unsqueeze(1).to_broadcast([P, 4, H]), ALU.add))
                own.step(nc.vector.tensor_tensor(u[0:TS, 4, :], dt_ps[0:TS, 4, :], bias[0:TS, :], ALU.add))
                own.step(nc.vector.tensor_scalar(dt_tok[:, :, :], u[:, :, :], 0.0, None, ALU.max))
                own.step(nc.vector.tensor_scalar(w1[:, :, :], u[:, :, :], -1.0, None, ALU.mult))
                nc.vector.tensor_tensor(u[:, :, :], u[:, :, :], w1[:, :, :], ALU.min).then_inc(u_done, 1)
                dve.wait_ge(l_done, 1)
                nc.vector.tensor_scalar(w1[:, :, :], u[:, :, :], 1.0, None, ALU.add).then_inc(u_done, 1)
                dve.wait_ge(l_done, 2)
                lnw = dt_ln
                own.step(nc.vector.tensor_scalar(w1[:, :, :], w1[:, :, :], 1.0, 1.0e-30, ALU.subtract, ALU.max))
                own.step(nc.vector.reciprocal(w1[:, :, :], w1[:, :, :]))
                own.step(nc.vector.tensor_tensor(w1[:, :, :], w1[:, :, :], u[:, :, :], ALU.mult))
                own.step(nc.vector.tensor_tensor(w1[:, :, :], w1[:, :, :], lnw[:, :, :], ALU.mult))
                own.step(nc.vector.tensor_scalar(lnw[:, :, :], u[:, :, :], -0.5, 1.0, ALU.mult, ALU.add))
                own.step(nc.vector.tensor_tensor(u[:, :, :], u[:, :, :], lnw[:, :, :], ALU.mult))
                own.step(nc.vector.tensor_tensor(w1[:, :, :], w1[:, :, :], u[:, :, :], ALU.max))
                own.step(nc.vector.tensor_tensor(dt_tok[:, :, :], dt_tok[:, :, :], w1[:, :, :], ALU.add))

            @block.scalar
            def _(act):
                silu(act, z_steps - 1)
                nc.scalar.preload_act_table_set("natural_log_exp_and_others")
                act.wait_ge(u_done, 1)
                nc.scalar.activation(u[:, :, :], u[:, :, :], ACT.Exp).then_inc(l_done, 1)
                act.wait_ge(u_done, 2)
                nc.scalar.activation(dt_ln[:, :, :], w1[:, :, :], ACT.Ln).then_inc(l_done, 1)
                act.wait_ge(act_done, XT)


def phase_ssd(k, xc, mixT, dt_tok):
    nc, io = k.nc, k.io
    names = ("tr", "trc", "dA", "ac_mm", "ac_ev", "aexp", "own_d", "xdt", "xw", "bm", "cb", "cbc", "bc", "seg",
             "kept", "decx", "e", "m", "cs", "y", "yo", "st_mm", "st", "sload", "sst", "own_p", "decayed", "sst_done",
             "st_own", "zeroed", "cleared")
    s = {n: k.sem("ss_" + n) for n in names}
    UNITS = 4 * TT
    zero_rows = k.hT[:, :, :].rearrange("p k t -> p (k t)")[:, 0:D]
    with ExitStack() as ctx:
        x_tok = k.sb("x_tok", [P, 2, D], ctx=ctx)
        b_tok = k.sb("b_tok", [P, 2, 2 * NS], ctx=ctx)
        xdt = k.sb("xdt", [P, 2, D], ctx=ctx)
        dA = k.sb("dA", [P, TT, H], ctx=ctx)
        neg_a = k.sb("neg_a", [P, H], ctx=ctx)
        nacum = k.sb("nacum", [P, TT, H], ctx=ctx)
        to_end = k.sb("to_end", [P, TT, H], ctx=ctx)
        cd = k.sb("cd", [P, 4, H], ctx=ctx)
        cds = k.sb("cds", [P, NB, H], ctx=ctx)
        dAm = k.sb("dAm", [TS, NB, H], ctx=ctx)
        bm = k.sb("bm", [TS, NB, 2 * NS], ctx=ctx)
        cbs = k.sb("cbs", [P, 2, 2, P], ctx=ctx)
        dec = k.sb("dec", [P, 3, 4, P], ctx=ctx)
        e_t = k.sb("e_t", [P, 3, 4, P], ctx=ctx)
        st = k.sb("st", [P, 2, D], ctx=ctx)
        sst = k.sb("sst", [P, NB, D], ctx=ctx)
        ac_ps = k.ps("ss_acps", [P, 512], ctx)
        tr_ps = k.ps("ss_trps", [P, 512], ctx)
        bc_ps = [k.ps(f"ss_bc{i}", [P, 4, P], ctx) for i in range(2)]
        y_ps = [k.ps(f"ss_y{i}", [P, 2, P], ctx) for i in range(2)]
        st_ps = [k.ps(f"ss_st{i}", [P, 512], ctx) for i in range(2)]
        GROUPS = ((0, 4), (4, 8), (8, 10))

        def tri(c):
            return k.tri_le[:, :] if c < 4 else k.tri_same[:, :]

        with nc.Block() as block:
            @block.sync
            def _(sp):
                sp.dma_start(sst[:, :, :], io["ssm_state"]).then_inc(s["sload"], 16)
                sp.wait_ge(s["zeroed"], 1)
                for i in range(NE * CAP, NBLK * CAP, P):
                    sp.dma_start(k.y_rows[i:i + P, :], zero_rows).then_inc(s["cleared"], 16)
                sp.wait_ge(s["st"], 4)
                sp.dma_start(io["ssm_p"], st[:, 1, :]).then_inc(s["sst"], 16)
                for b in range(NB):
                    sp.wait_ge(s["sst_done"], b + 1)
                    sp.dma_start(io["ssm_s"][:, b, :], sst[:, b, :]).then_inc(s["sst"], 16)
                sp.wait_ge(s["sst"], 16 * (1 + NB))
                sp.wait_ge(s["cleared"], 16 * (OVB * CAP // P))

            @block.tensor
            def _(pe):
                pe.wait_ge(s["dA"], 2)
                for c, (a, n) in enumerate(TOK):
                    nc.tensor.matmul(ac_ps[0:n, c * H:(c + 1) * H], tri(c), dA[0:n, c, :], start=True, stop=True)
                for c in range(4):
                    nc.tensor.matmul(ac_ps[:, 80 + c * H:80 + (c + 1) * H], k.ones[:, :], dA[:, c, :],
                                     start=True, stop=True)
                nc.tensor.matmul(ac_ps[0:TS, 144:160], k.same[:, :], dA[0:TS, 4, :], start=True, stop=True)
                nc.tensor.matmul(ac_ps[:, 160:288], k.ones[0:TS, :], dAm[:, :, :], start=True, stop=True)\
                  .then_inc(s["ac_mm"], 1)

                def turn(c, part):
                    a, n = TOK[c]
                    if part < 3:
                        if 3 * c + part:
                            pe.wait_ge(s["trc"], 3 * c + part)
                        g0, g1 = GROUPS[part]
                        for i in range(g0, g1):
                            last = nc.tensor.transpose(tr_ps[0:n, (i - g0) * P:(i - g0 + 1) * P], xc[:, i, a:a + n],
                                                       k.ident[:, :])
                        last.then_inc(s["tr"], 1)
                    if part == 2:
                        if c == 0:
                            pe.wait_ge(s["ac_ev"], 1)
                        else:
                            pe.wait_ge(s["cbc"], c)
                        for g in range(2):
                            last = nc.tensor.matmul(ac_ps[0:n, 256 + g * P:256 + g * P + n], xc[:, 8 + g, a:a + n],
                                                    xc[:, 10 + g, a:a + n], start=True, stop=True)
                        last.then_inc(s["cb"], 1)

                def broadcast_sums(u):
                    c, n = u // 4, TOK[u // 4][1]
                    if u >= 2:
                        pe.wait_ge(s["seg"], u - 1)
                        pe.wait_ge(s["e"], u - 1)
                    for h in range(4):
                        last = nc.tensor.matmul(bc_ps[u % 2][:, h, 0:n],
                                                dA[0:n, c, 4 * (u % 4) + h:4 * (u % 4) + h + 1].to_broadcast([n, P]),
                                                tri(c), start=True, stop=True)
                    last.then_inc(s["bc"], 1)

                def outputs(u):
                    c, q = u // 4, u % 4
                    n = TOK[c][1]
                    pe.wait_ge(s["m"], u + 1)
                    pe.wait_ge(s["cs"], u + 1)
                    if u >= 2:
                        pe.wait_ge(s["yo"], u - 1)
                    if 1 <= c < 4:
                        pe.wait_ge(s["st"], c)
                    if u == 16:
                        pe.wait_ge(s["sload"], 16)
                    for h in (0, 2, 1, 3):
                        r = slice(64 * (h % 2), 64 * (h % 2) + 64)
                        hh = 4 * q + h
                        f = slice(hh * HD, (hh + 1) * HD)
                        last = nc.tensor.matmul(y_ps[u % 2][r, h // 2, 0:n], xdt[0:n, c % 2, f],
                                                dec[0:n, u % 3, h, 0:n], start=True, stop=(c == 0),
                                                skip_group_check=True)
                        if 1 <= c < 4:
                            last = nc.tensor.matmul(y_ps[u % 2][r, h // 2, 0:n], st[:, (c - 1) % 2, f],
                                                    e_t[:, u % 3, h, 0:n], start=False, stop=True,
                                                    skip_group_check=True)
                        if c == 4:
                            for b in range(NB):
                                last = nc.tensor.matmul(y_ps[u % 2][r, h // 2, NQ * b:NQ * (b + 1)],
                                                        sst[:, b, f], e_t[:, u % 3, h, NQ * b:NQ * (b + 1)],
                                                        start=False, stop=(b == NB - 1), skip_group_check=True)
                    last.then_inc(s["y"], 1)

                def state_product(c):
                    pe.wait_ge(s["xw"], c + 1)
                    if c >= 1:
                        pe.wait_ge(s["st"], c)
                    for g in range(2):
                        last = nc.tensor.matmul(st_ps[g][:, :], b_tok[:, c % 2, g * NS:(g + 1) * NS],
                                                x_tok[:, c % 2, g * 512:(g + 1) * 512], start=True, stop=True)
                    last.then_inc(s["st_mm"], 1)

                for part in range(3):
                    turn(0, part)
                for i in range(UNITS + 2):
                    if i < UNITS:
                        broadcast_sums(i)
                    if i < UNITS - 4:
                        turn(i // 4 + 1, i % 4)
                    if i >= 2:
                        outputs(i - 2)
                    if i % 4 == 3 and i // 4 < 4:
                        state_product(i // 4)
                pe.wait_ge(s["bm"], NB)
                pe.wait_ge(s["xw"], TT)
                for b in range(NB):
                    for g in range(2):
                        if b == 0:
                            pe.wait_ge(s["st"], 4)
                        else:
                            pe.wait_ge(s["st_own"], 2 * b + g - 1)
                        nc.tensor.matmul(st_ps[g][:, :], bm[:, b, g * NS:(g + 1) * NS],
                                         x_tok[0:TS, 0, g * 512:(g + 1) * 512], start=True, stop=True)\
                          .then_inc(s["st_mm"], 1)

            @block.vector
            def _(dve):
                own = Chain(dve, s["own_d"])
                dve.wait_ge(s["aexp"], 1)
                own.step(nc.vector.tensor_scalar(neg_a[:, :], neg_a[:, :], -1.0, None, ALU.mult))
                nc.vector.tensor_tensor(dA[:, :, :], dt_tok[:, :, :], neg_a[:, :].unsqueeze(1).to_broadcast([P, TT, H]),
                                        ALU.mult).then_inc(s["dA"], 1)
                dve.wait_ge(s["dA"], 1)
                nc.vector.tensor_tensor(dAm[:, :, :], dA[0:TS, 4, :].unsqueeze(1).to_broadcast([TS, NB, H]),
                                        k.member[:, :].unsqueeze(2).to_broadcast([TS, NB, H]), ALU.mult)\
                  .then_inc(s["dA"], 1)
                dve.wait_ge(s["ac_mm"], 1)
                own.did(nc.vector.memset(nacum[:, :, :], 0.0))
                own.did(nc.vector.memset(to_end[:, :, :], 0.0))
                own.settle()
                ac = ac_ps[:, 0:80].rearrange("p (c h) -> p c h", h=H)
                en = ac_ps[:, 80:144].rearrange("p (c h) -> p c h", h=H)
                own.did(nc.vector.tensor_scalar(nacum[:, 0:4, :], ac[:, 0:4, :], -1.0, None, ALU.mult))
                own.did(nc.vector.tensor_scalar(nacum[0:TS, 4, :], ac[0:TS, 4, :], -1.0, None, ALU.mult))
                own.settle()
                own.did(nc.vector.tensor_tensor(to_end[:, 0:4, :], en, nacum[:, 0:4, :], ALU.add))
                own.did(nc.vector.tensor_tensor(to_end[0:TS, 4, :], ac_ps[0:TS, 144:160], nacum[0:TS, 4, :], ALU.add))
                own.did(nc.vector.tensor_copy(cd[:, :, :], en))
                own.did(nc.vector.tensor_copy(cds[:, :, :], ac_ps[:, 160:288].rearrange("p (b h) -> p b h", h=H)))
                own.settle()
                dve.sem_inc(s["ac_ev"], 1)

                def prepare(c, part):
                    a, n = TOK[c]
                    xt = x_tok[0:n, c % 2, :].rearrange("p (h e) -> p h e", e=HD)
                    xd = xdt[0:n, c % 2, :].rearrange("p (h e) -> p h e", e=HD)
                    if part == 2:
                        dve.wait_ge(s["trc"], 3 * c + 2)
                        if c >= 2:
                            dve.wait_ge(s["y"], 4 * (c - 1))
                        nc.vector.tensor_tensor(xd, xt, dt_tok[0:n, c, :].unsqueeze(2).to_broadcast([n, H, HD]),
                                                ALU.mult).then_inc(s["xdt"], 1)
                    if part == 3:
                        dve.wait_ge(s["xdt"], c + 1)
                        if c == 0:
                            dve.wait_ge(s["aexp"], 4)
                        nc.vector.tensor_tensor(xt, xd, to_end[0:n, c, :].unsqueeze(2).to_broadcast([n, H, HD]),
                                                ALU.mult).then_inc(s["xw"], 1)
                        dve.wait_ge(s["cb"], c + 1)
                        if c >= 2:
                            dve.wait_ge(s["m"], 4 * (c - 1))
                        nc.vector.tensor_copy(cbs[0:n, c % 2, :, 0:n],
                                              ac_ps[0:n, 256:512].rearrange("p (g l) -> p g l", g=2)[:, :, 0:n])\
                          .then_inc(s["cbc"], 1)

                def segment(u):
                    c, q, n = u // 4, u % 4, TOK[u // 4][1]
                    dve.wait_ge(s["e"], u + 1)
                    if u >= 3:
                        dve.wait_ge(s["y"], u - 2)
                    nc.vector.tensor_tensor(dec[0:n, u % 3, :, 0:n], bc_ps[u % 2][0:n, :, 0:n],
                                            nacum[0:n, c, 4 * q:4 * q + 4].unsqueeze(2).to_broadcast([n, 4, n]),
                                            ALU.add).then_inc(s["seg"], 1)

                def weigh(u):
                    c, q, n = u // 4, u % 4, TOK[u // 4][1]
                    dve.wait_ge(s["decx"], u + 1)
                    dve.wait_ge(s["cbc"], c + 1)
                    nc.vector.tensor_tensor(dec[0:n, u % 3, :, 0:n], dec[0:n, u % 3, :, 0:n],
                                            cbs[0:n, c % 2, q // 2, 0:n].unsqueeze(1).to_broadcast([n, 4, n]),
                                            ALU.mult).then_inc(s["m"], 1)

                def skip(u):
                    c, q = u // 4, u % 4
                    a, n = TOK[c]
                    dve.wait_ge(s["y"], u + 1)
                    for i in range(2):
                        j = 2 * q + i
                        ins = nc.vector.scalar_tensor_tensor(out=mixT[:, j, a:a + n], in0=xc[:, j, a:a + n],
                                                             scalar=k.col("d_skip", j), in1=y_ps[u % 2][:, i, 0:n],
                                                             op0=ALU.mult, op1=ALU.add)
                        if i == 0:
                            own.did(ins)
                        else:
                            ins.then_inc(s["yo"], 1)

                def state(c):
                    dve.wait_ge(s["st_mm"], c + 1)
                    if c >= 1:
                        if c >= 2:
                            dve.wait_ge(s["y"], 4 * c)
                        own.step(nc.vector.tensor_tensor(
                            st[:, c % 2, :].rearrange("p (h e) -> p h e", e=HD),
                            st[:, (c - 1) % 2, :].rearrange("p (h e) -> p h e", e=HD),
                            cd[:, c, :].unsqueeze(2).to_broadcast([P, H, HD]), ALU.mult))
                    for g in range(2):
                        f = slice(g * 512, (g + 1) * 512)
                        if c == 0:
                            ins = nc.vector.tensor_copy(st[:, 0, f], st_ps[g][:, :])
                        else:
                            ins = nc.vector.tensor_tensor(st[:, c % 2, f], st[:, c % 2, f], st_ps[g][:, :], ALU.add)
                        own.did(ins)
                    own.settle()
                    dve.sem_inc(s["st"], 1)

                prepare(0, 2)
                prepare(0, 3)
                for i in range(UNITS + 3):
                    if i < UNITS:
                        segment(i)
                    if 1 <= i < UNITS + 1:
                        weigh(i - 1)
                    if i >= 3:
                        skip(i - 3)
                    if i < UNITS - 4:
                        prepare(i // 4 + 1, i % 4)
                    if i % 4 == 0 and 4 <= i <= 16:
                        state(i // 4 - 1)
                    if i == 16:
                        for b in range(NB):
                            nc.vector.tensor_scalar(bm[:, b, :], b_tok[0:TS, 0, :], k.member[:, b:b + 1], None,
                                                    ALU.mult).then_inc(s["bm"], 1)
                for b in range(NB):
                    dve.wait_ge(s["decayed"], b + 1)
                    for g in range(2):
                        f = slice(g * 512, (g + 1) * 512)
                        dve.wait_ge(s["st_mm"], 4 + 2 * b + g + 1)
                        nc.vector.tensor_tensor(sst[:, b, f], sst[:, b, f], st_ps[g][:, :], ALU.add)\
                          .then_inc(s["st_own"], 1)
                    dve.wait_ge(s["st_own"], 2 * b + 2)
                    dve.sem_inc(s["sst_done"], 1)
                own.settle()
                dve.wait_ge(s["yo"], UNITS)

            @block.scalar
            def _(act):
                nc.scalar.activation(neg_a[:, :], k.small[:, COLS["a_log"][0]:COLS["a_log"][1]], ACT.Exp)\
                  .then_inc(s["aexp"], 1)

                def keep(c, part):
                    n = TOK[c][1]
                    if c >= 2 and part == 0:
                        act.wait_ge(s["st_mm"], c - 1)
                    g0, g1 = GROUPS[part]
                    act.wait_ge(s["tr"], 3 * c + part + 1)
                    dst = x_tok[0:n, c % 2, g0 * P:g1 * P] if part < 2 else b_tok[0:n, c % 2, :]
                    nc.scalar.activation(dst, tr_ps[0:n, 0:(g1 - g0) * P], ACT.Copy).then_inc(s["trc"], 1)

                for part in range(2):
                    keep(0, part)
                act.wait_ge(s["ac_ev"], 1)
                nc.scalar.activation(to_end[:, :, :], to_end[:, :, :], ACT.Exp).then_inc(s["aexp"], 1)
                nc.scalar.activation(cd[:, :, :], cd[:, :, :], ACT.Exp).then_inc(s["aexp"], 1)
                nc.scalar.activation(cds[:, :, :], cds[:, :, :], ACT.Exp).then_inc(s["aexp"], 1)
                keep(0, 2)
                for i in range(UNITS + 1):
                    if i < UNITS:
                        n = TOK[i // 4][1]
                        act.wait_ge(s["bc"], i + 1)
                        if i >= 3:
                            act.wait_ge(s["y"], i - 2)
                        nc.scalar.activation(e_t[:, i % 3, :, 0:n], bc_ps[i % 2][:, :, 0:n], ACT.Exp)\
                          .then_inc(s["e"], 1)
                    if i < UNITS - 4 and i % 4 < 3:
                        keep(i // 4 + 1, i % 4)
                    if i >= 1:
                        u = i - 1
                        n = TOK[u // 4][1]
                        act.wait_ge(s["kept"], u + 1)
                        d = dec[0:n, u % 3, :, 0:n]
                        nc.scalar.activation(d, d, ACT.Exp).then_inc(s["decx"], 1)
                act.wait_ge(s["decx"], UNITS)

            @block.gpsimd
            def _(pool):
                nc.gpsimd.memset(zero_rows, 0.0).then_inc(s["zeroed"], 1)
                own = Chain(pool, s["own_p"])
                for i in range(UNITS + 1):
                    if i < UNITS:
                        n = TOK[i // 4][1]
                        pool.wait_ge(s["seg"], i + 1)
                        d = dec[0:n, i % 3, :, 0:n]
                        ins = nc.gpsimd.affine_select(out=d, in_=d, pattern=[[0, 4], [1, n]], base=0,
                                                      channel_multiplier=-1, compare_op=ALU.is_ge, fill=NO_DECAY)
                        if i >= 16:
                            own.step(ins)
                            d = d.rearrange("p h (b q) -> p h b q", q=NQ)
                            ins = nc.gpsimd.affine_select(out=d, in_=d, pattern=[[0, 4], [-NQ, NB], [0, NQ]], base=0,
                                                          channel_multiplier=1, compare_op=ALU.is_ge, fill=NO_DECAY)
                        ins.then_inc(s["kept"], 1)
                        pool.wait_ge(s["kept"], i + 1)
                    if i >= 1:
                        u = i - 1
                        q, (a, n) = u % 4, TOK[u // 4]
                        pool.wait_ge(s["e"], u + 1)
                        nc.gpsimd.tensor_tensor(e_t[:, u % 3, :, 0:n], e_t[:, u % 3, :, 0:n],
                                                xc[:, 10 + q // 2, a:a + n].unsqueeze(1).to_broadcast([P, 4, n]),
                                                ALU.mult).then_inc(s["cs"], 1)
                        pool.wait_ge(s["cs"], u + 1)
                pool.wait_ge(s["y"], UNITS)
                for b in range(NB):
                    sv = sst[:, b, :].rearrange("p (h e) -> p h e", e=HD)
                    nc.gpsimd.tensor_tensor(sv, sv, cds[:, b, :].unsqueeze(2).to_broadcast([P, H, HD]), ALU.mult)\
                      .then_inc(s["decayed"], 1)
                    pool.wait_ge(s["decayed"], b + 1)


def phase_gated_norm(k, zs, mixT, mix_r, mix_hi, slots):
    nc = k.nc
    gated, squared, summed, root_in, root, done, own_d, high, low = (
        k.sem("gn_" + n) for n in ("gated", "sq", "sum", "ri", "root", "done", "own", "high", "low"))

    def lower(j):
        return nc.vector.tensor_tensor(mix_r[:, j, :], mixT[:, j, :], mix_hi(j), ALU.subtract).then_inc(low, 1)

    def upper(j):
        return nc.scalar.activation(mix_hi(j), mixT[:, j, :], ACT.Copy).then_inc(high, 1)

    with ExitStack() as ctx:
        sq = k.sb("gn_sq", [P, 2, T], ctx=ctx)
        rstd = k.sb("gn_rstd", [P, 2, T], ctx=ctx)
        ps = k.ps("gn_ps", [P, 4, 512], ctx)
        with nc.Block() as block:
            @block.vector
            def _(dve):
                own = Chain(dve, own_d)
                for j in range(KT):
                    nc.vector.tensor_tensor(mixT[:, j, :], mixT[:, j, :], zs[:, j, :], ALU.mult).then_inc(gated, 1)
                for j in range(KT, 2 * KT):
                    dve.wait_ge(high, j - KT + 1)
                    lower(j)
                for g in range(2):
                    dve.wait_ge(summed, 4 * (g + 1))
                    nc.vector.tensor_scalar(by_half(rstd[:, g, :]), ps[:, 2 * g:2 * g + 2, 0:HALF], 2.0 / D, EPS,
                                            ALU.mult, ALU.add).then_inc(root_in, 1)
                for g in range(2):
                    dve.wait_ge(root, g + 1)
                    own.step(nc.vector.reciprocal(rstd[:, g, :], rstd[:, g, :]))
                dve.wait_ge(gated, KT)
                dve.wait_ge(squared, KT)
                for j in range(KT):
                    nc.vector.scalar_tensor_tensor(out=mixT[:, j, :], in0=mixT[:, j, :], scalar=k.col("norm_g", j),
                                                   in1=rstd[:, j // 4, :], op0=ALU.mult, op1=ALU.mult).then_inc(done, 1)
                for j in range(KT):
                    dve.wait_ge(high, KT + j + 1)
                    lower(j)
                dve.wait_ge(low, 2 * KT)

            @block.scalar
            def _(act):
                for j in range(KT):
                    act.wait_ge(gated, j + 1)
                    if j >= 2:
                        act.wait_ge(summed, j - 1)
                    nc.scalar.activation(sq[:, j % 2, :], mixT[:, j, :], ACT.Square).then_inc(squared, 1)
                    upper(KT + j)
                for g in range(2):
                    act.wait_ge(root_in, g + 1)
                    nc.scalar.activation(rstd[:, g, :], rstd[:, g, :], ACT.Sqrt).then_inc(root, 1)
                for j in range(KT):
                    act.wait_ge(done, j + 1)
                    upper(j)

            @block.sync
            def _(sp):
                slots.load(sp)

            @block.gpsimd
            def _(pool):
                slots.split_first(pool)

            @block.tensor
            def _(pe):
                for j in range(KT):
                    pe.wait_ge(squared, j + 1)
                    for h in range(2):
                        last = nc.tensor.matmul(ps[:, 2 * (j // 4) + h, 0:HALF], k.ones[:, :],
                                                sq[:, j % 2, h * HALF:(h + 1) * HALF],
                                                start=(j % 4 == 0), stop=(j % 4 == 3))
                    last.then_inc(summed, 1)


def phase_out_project(k, name, w, kt, x_hi, x_lo, layer, chunk, slots):
    with ExitStack() as ctx:
        res = k.sb(f"{name}_res", [P, KT, T], ctx=ctx)
        phase_project(k, name, kt, [Part(w, 4, feature_products(k.nc, x_hi, x_lo, kt), copies_to(k.nc, res))],
                      slots)
        phase_residual(k, name, res, layer * 48 + chunk * KT)


def phase_residual(k, name, res, m0):
    nc = k.nc
    done, scaled = k.sem(f"{name}_added"), k.sem(f"{name}_scaled")
    with nc.Block() as block:
        @block.vector
        def _(dve):
            for j in range(KT):
                nc.vector.scalar_tensor_tensor(out=k.xT[:, j, 0:TP], in0=res[:, j, 0:TP], scalar=k.mod[:, m0 + j, 0:1],
                                               in1=k.xT[:, j, 0:TP], op0=ALU.mult, op1=ALU.add).then_inc(done, 1)
            rs = res[:, :, TP:T].rearrange("p k (b q) -> p k b q", q=NQ)
            g = k.mod[:, m0:m0 + KT, 1:NC9].unsqueeze(3).to_broadcast([P, KT, NB, NQ])
            nc.vector.tensor_tensor(rs, rs, g, ALU.mult).then_inc(scaled, 1)
            dve.wait_ge(scaled, 1)
            nc.vector.tensor_tensor(k.xT[:, :, TP:T], k.xT[:, :, TP:T], res[:, :, TP:T], ALU.add).then_inc(done, 1)
            dve.wait_ge(done, KT + 1)


def phase_short_conv(k, gT, g_lo, h_hi, slots, next_w):
    nc, io = k.nc, k.io
    loaded, own_d, kept_done, stored, mult, conv, high, low, prod, cu = (
        k.sem("sc_" + n) for n in ("loaded", "own", "kept", "stored", "mult", "conv", "high", "low", "prod", "cu"))
    with ExitStack() as ctx:
        proj = k.sb("sc_proj", [P, 3 * KT, T], ctx=ctx)
        cur = k.sb("sc_cu", [P, KT, 2 + T], ctx=ctx)
        buf = k.sb("sc_buf", [P, KT, NB, 2], ctx=ctx)
        kept = k.sb("sc_kept", [P, KT, 2 + TS], ctx=ctx)
        raw_s = k.sb("sc_raws", [P, KT, NB, 2 + NQ], ctx=ctx)
        tmp = k.sb("sc_tmp", [P, KT, NB, NQ], ctx=ctx)
        gs = gT[:, :, TP:T].rearrange("p k (b q) -> p k b q", q=NQ)
        STEPS = 4
        PER = KT // STEPS
        b_base = k.rounds + 4
        own_of = {}

        with nc.Block() as block:
            @block.sync
            def _(sp):
                sp.dma_start(buf[:, :, :, :], io["sc_state"]).then_inc(loaded, 16)
                sp.wait_ge(loaded, 16)

        def conv_vector(dve, step):
            if step == 0:
                own = own_of["c"] = Chain(dve, own_d)
                own.did(nc.vector.memset(cur[:, :, 0:2], 0.0))
                for b in range(2):
                    for t in range(2):
                        dve.wait_ge(k.ps_free[b][t], b_base + 1)
                for j in range(KT):
                    nc.vector.tensor_tensor(cur[:, j, 2:2 + T], proj[:, j, :], proj[:, KT + j, :], ALU.mult)\
                      .then_inc(cu, 1)
                own.settle()
                dve.wait_ge(cu, KT)
                dve.sem_inc(cu, 1)
                new = cur[:, :, 2 + TP:2 + T]
                own.did(nc.vector.tensor_copy(raw_s[:, :, :, 2:2 + NQ], new.rearrange("p k (b q) -> p k b q", q=NQ)))
                own.did(nc.vector.tensor_copy(raw_s[:, :, :, 0:2], buf[:, :, :, :]))
                nc.vector.tensor_copy(kept[:, :, 0:2], cur[:, :, TP:TP + 2]).then_inc(kept_done, 1)
                nc.vector.tensor_copy(kept[:, :, 2:2 + TS], new).then_inc(kept_done, 1)
                own.settle()
                w = COLS["sc_w"][0]
                for t in range(3):
                    wide = k.small[:, w + t * KT:w + (t + 1) * KT].unsqueeze(2).unsqueeze(3).to_broadcast([P, KT, NB, NQ])
                    own.step(nc.vector.tensor_tensor(gs if t == 0 else tmp[:, :, :, :], raw_s[:, :, :, t:t + NQ], wide,
                                                     ALU.mult))
                    if t:
                        own.step(nc.vector.tensor_tensor(gs, gs, tmp[:, :, :, :], ALU.add))
            for t in range(1, 3):
                for j in range(PER * step, PER * (step + 1)):
                    if t == 1:
                        dve.wait_ge(mult, j + 1)
                    else:
                        dve.wait_ge(conv, 2 * PER * step + j - PER * step + 1)
                    nc.vector.scalar_tensor_tensor(out=gT[:, j, 0:TP], in0=cur[:, j, t:t + TP],
                                                   scalar=k.col("sc_w", t * KT + j), in1=gT[:, j, 0:TP],
                                                   op0=ALU.mult, op1=ALU.add).then_inc(conv, 1)

        def conv_scalar(act, step):
            if step == 0:
                act.wait_ge(cu, KT + 1)
            for j in range(PER * step, PER * (step + 1)):
                nc.scalar.activation(gT[:, j, 0:TP], cur[:, j, 0:TP], ACT.Copy, scale=k.col("sc_w", j)).then_inc(mult, 1)

        def take_b(tile, ps):
            return nc.scalar.activation(by_half(proj[:, bass.ds(tile + 2 * KT, 1), :].rearrange("p a t -> p (a t)")),
                                        ps[:, :, 0:HALF], ACT.Copy)

        feature = feature_products(nc, lambda j: h_hi[:, j, :], lambda j: k.hT_r[:, j, :], KT)
        phase_project(k, "sc", KT, [Part(io["sc_w_in"][:, D:3 * D], 8, feature, copies_to(nc, proj)),
                                    Part(io["sc_w_in"][:, 0:D], STEPS, feature, (take_b, take_b), True,
                                         (conv_vector, conv_scalar))], slots)

        slots.aim(next_w)
        with nc.Block() as block:
            @block.sync
            def _(sp):
                slots.load(sp)
                sp.dma_start(io["sc_out"], kept[:, :, :]).then_inc(stored, 16)
                sp.wait_ge(stored, 16)

            @block.gpsimd
            def _(pool):
                slots.split_first(pool)

            @block.vector
            def _(dve):
                for j in range(KT):
                    nc.vector.tensor_tensor(gT[:, j, :], gT[:, j, :], proj[:, 2 * KT + j, :], ALU.mult).then_inc(prod, 1)
                for j in range(KT):
                    dve.wait_ge(high, j + 1)
                    nc.vector.tensor_tensor(g_lo[:, j, :], gT[:, j, :], k.hT_r[:, j, :], ALU.subtract).then_inc(low, 1)
                dve.wait_ge(low, KT)

            @block.scalar
            def _(act):
                for j in range(KT):
                    act.wait_ge(prod, j + 1)
                    nc.scalar.activation(k.hT_r[:, j, :], gT[:, j, :], ACT.Copy).then_inc(high, 1)


class Routing:

    def __init__(self, k, ctx, layer):
        self.tok = k.sb(f"route{layer}_tok", [CAP, NBLK], I32, ctx=ctx)
        self.slot = k.sb(f"route{layer}_slot", [P, 2, TT], I32, ctx=ctx)
        self.weight = k.sb(f"route{layer}_weight", [P, 2, TT], ctx=ctx)
        self.more = k.sb(f"route{layer}_more", [1, 1 + OVB], I32, ctx=ctx)


def phase_route(k, layer, r, ex):
    nc, io = k.nc, k.io
    nm = f"rt{layer}_"
    names = ("w", "iota", "tr", "trc", "rows", "lt", "ltc", "lg", "e_in", "e_out", "mask", "rank", "pair", "slots",
             "own_d", "own_p", "done", "mats")
    s = {n: k.sem(nm + n) for n in names}
    with ExitStack() as ctx:
        sb = lambda n, shape, dt=F32: k.sb(nm + n, shape, dt, ctx=ctx)
        w_r = sb("wr", [P, KT, 36])
        rows = sb("rowbuf", [P, 4, D])
        lgT = sb("lgT", [36, T])
        tri_r, ones_r = sb("tri_r", [P, P], F32R), sb("ones_r", [P, P], F32R)
        lg = sb("lg", [P, TT, 36])
        desc = sb("desc", [P, 8])
        expert = sb("expert", [P, NE])
        block_id = sb("block_id", [P, NBLK])
        row_id = sb("row_id", [P, CAP])
        tok_id = sb("tok_id", [P, TT])
        full = sb("full", [P, MAXQ])
        valid = sb("valid", [P, TT])
        t1, t2, t3, t4 = (sb(f"t{i}", [P, TT, 1]) for i in range(4))
        g4, oh_g = sb("g4", [P, TT, 4]), sb("oh_g", [P, TT, 4])
        e8, sc8 = sb("e8", [P, TT, 8]), sb("sc8", [P, TT, 8])
        oh8 = [sb(f"oh8{i}", [P, TT, 8]) for i in range(2)]
        top = [sb(f"top{i}", [P, TT, 1]) for i in range(2)]
        oh, x64 = sb("oh", [P, 2, TT, NE]), sb("x64", [P, 2, TT, NE])
        x32, mask, rank = sb("x32", [P, TT, NE]), sb("mask", [P, TT + 1, NE], F32R), sb("rank", [P, TT, NE])
        cnt, nov, ovb = sb("cnt", [P, NE]), sb("nov", [P, NE]), sb("ovb", [P, NE])
        cmp_n = sb("cmp_n", [P, NE, MAXQ])
        cmp_q = sb("cmp_q", [P, 2, TT, MAXQ])
        cmp_o = sb("cmp_o", [1, OVB, NE])
        more_f = sb("more_f", [1, 1 + OVB])
        blk, row, rk, q_, ov = (sb(n, [P, 2, TT]) for n in ("blk", "row", "rk", "q", "ov"))
        row_hot = sb("row_hot", [P, 2, CAP])
        blk_hot = sb("blk_hot", [P, 2, NBLK])
        slot_f = sb("slot_f", [CAP, NBLK])
        none = sb("none", [CAP, NBLK])
        tr_ps = [k.ps(f"{nm}tr{i}", [P, 512], ctx) for i in range(2)]
        lt_ps = k.ps(nm + "ltps", [36, 2, 512], ctx)
        lg_ps = k.ps(nm + "lgps", [P, TT, 36], ctx)
        rk_ps = k.ps(nm + "rkps", [P, TT + 1, NE], ctx)
        sl_ps = k.ps(nm + "slps", [CAP, NBLK], ctx)

        with nc.Block() as block:
            @block.sync
            def _(sp):
                sp.dma_start(w_r[:, :, :], io["w_route"][layer].rearrange("(k p) n -> p k n", p=P)).then_inc(s["w"], 16)
                for b in range(2):
                    ex.load(k, sp, b, b, ex.w[b])
                for i, (a, m) in enumerate(TOK):
                    sp.wait_ge(s["trc"], 2 * (i + 1))
                    sp.dma_start(k.h_rows[a:a + m, :], rows[0:m, i % 4, :]).then_inc(s["rows"], 16)
                    if i == 0:
                        sp.wait_ge(s["rows"], 16)
                for b in range(2, ex.SLOTS):
                    ex.load(k, sp, b, b, ex.w[b])
                sp.wait_ge(s["rows"], 16 * TT)

            @block.gpsimd
            def _(pool):
                own = Chain(pool, s["own_p"])
                kw = dict(allow_small_or_imprecise_dtypes=True)
                own.did(nc.gpsimd.iota(desc[:, :], [[-1, 8]], base=8, channel_multiplier=0, **kw))
                own.did(nc.gpsimd.iota(expert[:, :], [[1, NE]], base=0, channel_multiplier=0, **kw))
                own.did(nc.gpsimd.iota(block_id[:, :], [[1, NBLK]], base=0, channel_multiplier=0, **kw))
                own.did(nc.gpsimd.iota(row_id[:, :], [[1, CAP]], base=0, channel_multiplier=0, **kw))
                own.did(nc.gpsimd.iota(tok_id[:, :], [[P, TT]], base=1, channel_multiplier=1, **kw))
                own.did(nc.gpsimd.iota(full[:, :], [[CAP, MAXQ]], base=CAP, channel_multiplier=0, **kw))
                own.step(nc.gpsimd.memset(valid[:, :], 1.0))
                own.step(nc.gpsimd.affine_select(out=valid[:, :], in_=valid[:, :], pattern=[[-P, TT]], base=T - 1,
                                                 channel_multiplier=-1, compare_op=ALU.is_ge, fill=0.0))
                pool.sem_inc(s["iota"], 1)

            @block.tensor
            def _(pe):
                pe.wait_ge(s["w"], 16)
                for h in range(2):
                    for j in range(KT):
                        last = nc.tensor.matmul(lt_ps[:, h, 0:HALF], w_r[:, j, :], k.hT[:, j, h * HALF:(h + 1) * HALF],
                                                start=(j == 0), stop=(j == KT - 1))
                last.then_inc(s["lt"], 1)

                def turn_rows(i):
                    a, m = TOK[i]
                    for n in range(2):
                        u = 2 * i + n
                        if u >= 2:
                            pe.wait_ge(s["trc"], u - 1)
                        for j in range(4):
                            last = nc.tensor.transpose(tr_ps[n][0:m, j * P:(j + 1) * P], k.hT[:, 4 * n + j, a:a + m],
                                                       k.ident[:, :])
                        last.then_inc(s["tr"], 1)

                turn_rows(0)
                pe.wait_ge(s["ltc"], 1)
                for i, (a, m) in enumerate(TOK):
                    last = nc.tensor.transpose(lg_ps[0:m, i, :], lgT[:, a:a + m], k.ident[0:36, 0:36])
                last.then_inc(s["lg"], 1)
                for i in range(1, TT):
                    turn_rows(i)
                pe.wait_ge(s["mask"], 2)
                pe.wait_ge(s["mats"], 2)
                nc.tensor.matmul(rk_ps[:, :, :], tri_r[:, :], mask[:, :, :], start=True, stop=False,
                                 skip_group_check=True)
                for d in range(1, TT + 1):
                    last = nc.tensor.matmul(rk_ps[:, d:TT + 1, :], ones_r[:, :], mask[:, 0:TT + 1 - d, :], start=False,
                                            stop=(d == TT), skip_group_check=True)
                last.then_inc(s["rank"], 1)
                for n in range(2 * TT):
                    m = TOK[n // 2][1]
                    pe.wait_ge(s["pair"], n + 1)
                    last = nc.tensor.matmul(sl_ps[:, :], row_hot[0:m, n % 2, :], blk_hot[0:m, n % 2, :],
                                            start=(n == 0), stop=(n == 2 * TT - 1))
                    last.then_inc(s["slots"], 1)

            @block.scalar
            def _(act):
                nc.scalar.activation(tri_r[:, :], k.tri_lt[:, :], ACT.Copy).then_inc(s["mats"], 1)
                nc.scalar.activation(ones_r[:, :], k.ones[:, :], ACT.Copy).then_inc(s["mats"], 1)
                nc.scalar.preload_act_table_set("exp_and_others")

                def keep_rows(i):
                    m = TOK[i][1]
                    for n in range(2):
                        act.wait_ge(s["tr"], 2 * i + n + 1)
                        if i == 4 and n == 0:
                            act.wait_ge(s["rows"], 16)
                        nc.scalar.activation(rows[0:m, i % 4, n * 512:(n + 1) * 512], tr_ps[n][0:m, :], ACT.Copy)\
                          .then_inc(s["trc"], 1)

                act.wait_ge(s["lt"], 1)
                nc.scalar.activation(by_half(lgT[:, :]), lt_ps[:, :, 0:HALF], ACT.Copy).then_inc(s["ltc"], 1)
                keep_rows(0)
                keep_rows(1)
                act.wait_ge(s["e_in"], 1)
                nc.scalar.activation(g4[:, :, :], g4[:, :, :], ACT.Exp).then_inc(s["e_out"], 1)
                for i in (2, 3):
                    keep_rows(i)
                act.wait_ge(s["e_in"], 2)
                nc.scalar.activation(e8[:, :, :], e8[:, :, :], ACT.Exp).then_inc(s["e_out"], 1)
                keep_rows(4)

            @block.vector
            def _(dve):
                own = Chain(dve, s["own_d"])
                V = nc.vector
                step = own.step
                wide = lambda t, n: t[:, :, :].to_broadcast([P, TT, n])
                own.did(V.memset(lg[:, :, :], 0.0))
                own.step(V.memset(x32[:, 0, :], 0.0))
                V.tensor_copy(mask[:, TT, :], x32[:, 0, :]).then_inc(s["mask"], 1)
                dve.wait_ge(s["lg"], 1)
                bias = k.small[:, COLS["router_b"][0] + 36 * layer:COLS["router_b"][0] + 36 * (layer + 1)]
                step(V.tensor_tensor(lg[:, 0:4, :], lg_ps[:, 0:4, :], bias.unsqueeze(1).to_broadcast([P, 4, 36]), ALU.add))
                step(V.tensor_tensor(lg[0:TS, 4, :], lg_ps[0:TS, 4, :], bias[0:TS, :], ALU.add))
                step(V.tensor_reduce(t1[:, :, :], lg[:, :, 0:4], AX_X, ALU.max))
                V.tensor_tensor(g4[:, :, :], lg[:, :, 0:4], wide(t1, 4), ALU.subtract).then_inc(s["e_in"], 1)
                dve.wait_ge(s["iota"], 1)
                dve.wait_ge(s["e_out"], 1)
                g_top = t4
                step(V.tensor_reduce(t1[:, :, :], g4[:, :, :], AX_X, ALU.max))
                step(V.tensor_reduce(t2[:, :, :], g4[:, :, :], AX_X, ALU.add))
                step(V.reciprocal(t3[:, :, :], t2[:, :, :]))
                step(V.tensor_tensor(g_top[:, :, :], t1[:, :, :], t3[:, :, :], ALU.mult))

                def first_largest(out, values, largest, n, scratch):
                    step(V.tensor_tensor(out, values, wide(largest, n), ALU.is_equal))
                    step(V.tensor_tensor(out, out, desc[:, 0:n].unsqueeze(1).to_broadcast([P, TT, n]), ALU.mult))
                    step(V.tensor_reduce(scratch[:, :, :], out, AX_X, ALU.max))
                    step(V.tensor_tensor(out, out, wide(scratch, n), ALU.is_equal))

                first_largest(oh_g[:, :, :], g4[:, :, :], t1, 4, t2)
                by_group = lambda t: t[:, :, :].rearrange("p t (g e) -> p t g e", e=8)
                for i in range(TT):
                    own.did(V.tensor_tensor(x32[:, i, :].rearrange("p (g e) -> p g e", e=8),
                                            lg[:, i, 4:36].rearrange("p (g e) -> p g e", e=8),
                                            oh_g[:, i, :].unsqueeze(2).to_broadcast([P, 4, 8]), ALU.mult))
                own.settle()
                step(V.tensor_reduce(sc8[:, :, :].unsqueeze(3), x32[:, :, :].rearrange("p t (g e) -> p t e g", e=8),
                                     AX_X, ALU.add))
                step(V.tensor_reduce(t1[:, :, :], sc8[:, :, :], AX_X, ALU.max))
                V.tensor_tensor(e8[:, :, :], sc8[:, :, :], wide(t1, 8), ALU.subtract).then_inc(s["e_in"], 1)
                dve.wait_ge(s["e_out"], 2)
                for i in range(2):
                    step(V.tensor_reduce(top[i][:, :, :], e8[:, :, :], AX_X, ALU.max))
                    first_largest(oh8[i][:, :, :], e8[:, :, :], top[i], 8, t2)
                    if i == 0:
                        step(V.scalar_tensor_tensor(out=e8[:, :, :], in0=oh8[0][:, :, :], scalar=-2.0, in1=e8[:, :, :],
                                                    op0=ALU.mult, op1=ALU.add))
                step(V.tensor_tensor(t1[:, :, :], top[0][:, :, :], top[1][:, :, :], ALU.add))
                step(V.reciprocal(t2[:, :, :], t1[:, :, :]))
                step(V.tensor_tensor(t2[:, :, :], t2[:, :, :], g_top[:, :, :], ALU.mult))
                for i in range(2):
                    step(V.tensor_tensor(r.weight[:, i, :], top[i][:, :, 0], t2[:, :, 0], ALU.mult))
                    for t in range(TT):
                        own.did(V.tensor_tensor(oh[:, i, t, :].rearrange("p (g e) -> p g e", e=8),
                                                oh_g[:, t, :].unsqueeze(2).to_broadcast([P, 4, 8]),
                                                oh8[i][:, t, :].unsqueeze(1).to_broadcast([P, 4, 8]), ALU.mult))
                own.settle()
                step(V.tensor_tensor(x32[:, :, :], oh[:, 0, :, :], oh[:, 1, :, :], ALU.add))
                V.tensor_tensor(mask[:, 0:TT, :], x32[:, :, :], valid[:, :].unsqueeze(2).to_broadcast([P, TT, NE]), ALU.mult)\
                 .then_inc(s["mask"], 1)
                dve.wait_ge(s["rank"], 1)
                step(V.tensor_copy(rank[:, :, :], rk_ps[:, 0:TT, :]))
                step(V.tensor_copy(cnt[:, :], rk_ps[:, TT, :]))
                step(V.tensor_tensor(cmp_n[:, :, :], cnt[:, :].unsqueeze(2).to_broadcast([P, NE, MAXQ]),
                                     full[:, :].unsqueeze(1).to_broadcast([P, NE, MAXQ]), ALU.is_gt))
                step(V.tensor_reduce(nov[:, :].unsqueeze(2), cmp_n[:, :, :], AX_X, ALU.add))
                step(V.tensor_tensor_scan(ovb[:, :], nov[:, :], nov[:, :], 0.0, ALU.add, ALU.bypass))
                step(V.tensor_tensor(cmp_o[:, :, :], block_id[0:1, 0:OVB].unsqueeze(2).to_broadcast([1, OVB, NE]),
                                     ovb[0:1, :].unsqueeze(1).to_broadcast([1, OVB, NE]), ALU.is_ge))
                step(V.tensor_reduce(more_f[:, 1:1 + OVB].unsqueeze(2), cmp_o[:, :, :], AX_X, ALU.add))
                step(V.tensor_scalar(more_f[:, 1:1 + OVB], more_f[:, 1:1 + OVB], float(NE - 1), None, ALU.min))
                step(V.tensor_copy(more_f[:, 0:1], ovb[0:1, NE - 1:NE]))
                step(V.tensor_copy(r.more[:, :], more_f[:, :]))
                step(V.tensor_tensor(ovb[:, :], ovb[:, :], nov[:, :], ALU.subtract))
                def pick(dst, table):
                    step(V.tensor_tensor(x64[:, :, :, :], oh[:, :, :, :], table, ALU.mult))
                    step(V.tensor_reduce(dst[:, :, :].unsqueeze(3), x64[:, :, :, :], AX_X, ALU.add))

                both = lambda t: t.unsqueeze(1).to_broadcast([P, 2, TT, NE])
                pick(rk, both(rank[:, :, :]))
                pick(blk, expert[:, :].unsqueeze(1).unsqueeze(1).to_broadcast([P, 2, TT, NE]))
                pick(ov, ovb[:, :].unsqueeze(1).unsqueeze(1).to_broadcast([P, 2, TT, NE]))
                step(V.tensor_tensor(cmp_q[:, :, :, :], rk[:, :, :].unsqueeze(3).to_broadcast([P, 2, TT, MAXQ]),
                                     full[:, :].unsqueeze(1).unsqueeze(1).to_broadcast([P, 2, TT, MAXQ]), ALU.is_ge))
                step(V.tensor_reduce(q_[:, :, :].unsqueeze(3), cmp_q[:, :, :, :], AX_X, ALU.add))
                step(V.scalar_tensor_tensor(out=row[:, :, :], in0=q_[:, :, :], scalar=-float(CAP), in1=rk[:, :, :],
                                            op0=ALU.mult, op1=ALU.add))
                step(V.tensor_tensor(ov[:, :, :], ov[:, :, :], q_[:, :, :], ALU.add))
                step(V.scalar_tensor_tensor(out=ov[:, :, :], in0=ov[:, :, :], scalar=float(NE - 1), in1=blk[:, :, :],
                                            op0=ALU.add, op1=ALU.subtract))
                step(V.tensor_scalar(q_[:, :, :], q_[:, :, :], 1.0, None, ALU.min))
                step(V.tensor_tensor(ov[:, :, :], ov[:, :, :], q_[:, :, :], ALU.mult))
                step(V.tensor_tensor(blk[:, :, :], blk[:, :, :], ov[:, :, :], ALU.add))
                step(V.scalar_tensor_tensor(out=rk[:, :, :], in0=blk[:, :, :], scalar=float(CAP), in1=row[:, :, :],
                                            op0=ALU.mult, op1=ALU.add))
                step(V.tensor_copy(r.slot[:, :, :], rk[:, :, :]))
                for n in range(2 * TT):
                    t, i = n // 2, n % 2
                    if n >= 2:
                        dve.wait_ge(s["slots"], n - 1)
                    own.did(V.tensor_scalar(row_hot[:, i, :], row_id[:, :], row[:, i, t:t + 1], None, ALU.is_equal))
                    own.settle()
                    V.tensor_scalar(blk_hot[:, i, :], block_id[:, :], blk[:, i, t:t + 1], tok_id[:, t:t + 1],
                                    ALU.is_equal, ALU.mult).then_inc(s["pair"], 1)
                dve.wait_ge(s["slots"], 2 * TT)
                step(V.tensor_scalar(none[:, :], sl_ps[:, :], 0.0, BIG, ALU.is_equal, ALU.mult))
                step(V.scalar_tensor_tensor(out=slot_f[:, :], in0=sl_ps[:, :], scalar=-1.0, in1=none[:, :],
                                            op0=ALU.add, op1=ALU.add))
                step(V.tensor_copy(r.tok[:, :], slot_f[:, :]))


class Experts:

    SLOTS = 4

    def __init__(self, k, layer, ctx):
        self.layer = layer
        self.gu = [k.sb(f"ex{layer}_gu{b}", [P, 2, KT, DE], ctx=ctx) for b in range(self.SLOTS)]
        self.dn = [k.sb(f"ex{layer}_dn{b}", [P, 2, D], ctx=ctx) for b in range(self.SLOTS)]
        self.w = [k.sem(f"ex{layer}_w{b}") for b in range(self.SLOTS)]

    def load(self, k, sp, b, e, ready):
        one = lambda w: w[self.layer][bass.ds(e, 1), :, :]
        sp.dma_start(self.gu[b][:, 0, :, :], one(k.io["moe_w_gate"]).rearrange("a (p j) f -> p (a j f)", p=P))\
          .then_inc(ready, 16)
        sp.dma_start(self.gu[b][:, 1, :, :], one(k.io["moe_w_up"]).rearrange("a (p j) f -> p (a j f)", p=P))\
          .then_inc(ready, 16)
        sp.dma_start(self.dn[b][:, :, :], one(k.io["moe_w_down"]).rearrange("a (m p) d -> p (a m) d", p=P))\
          .then_inc(ready, 16)


def phase_experts(k, layer, r, ex):
    nc, io = k.nc, k.io
    nm = f"ex{layer}_"
    S = ex.SLOTS
    with ExitStack() as ctx:
        sb = lambda n, shape, dt=F32: k.sb(nm + n, shape, dt, ctx=ctx)
        hg = [sb(f"hg{b}", [CAP, D]) for b in range(2)]
        he = [sb(f"he{b}", [P, KT, CAP]) for b in range(2)]
        sg = sb("sg", [P, P])
        hid = sb("hid", [P, P])
        hid_t = sb("hid_t", [P, P])
        yo = [sb(f"yo{b}", [P, 512]) for b in range(2)]
        tr_ps = [k.ps(f"{nm}trps{b}", [P, KT, CAP], ctx) for b in range(2)]
        gu_ps = k.ps(f"{nm}gups", [P, 2, P], ctx)
        ht_ps = k.ps(f"{nm}htps", [P, P], ctx)
        y_ps = [k.ps(f"{nm}yps{b}", [P, 512], ctx) for b in range(2)]

        def block_programs(pass_name, rounds, first, load_slot, preloaded, w_ready):
            sems = {n: k.sem(f"{nm}{pass_name}{n}") for n in ("tr", "he", "gu", "sg", "hid", "htp", "ht", "y", "yo")}
            g = [k.sem(f"{nm}{pass_name}g{b}") for b in range(2)]
            st = [k.sem(f"{nm}{pass_name}st{b}") for b in range(2)]

            def sync_program(sp):
                if not preloaded:
                    for b in range(S):
                        load_slot(sp, b, b)
                if rounds > 1:
                    with sp.Fori(0, rounds - 1) as i:
                        for b in range(S):
                            sp.wait_ge(sems["y"], i * S + (b + 1))
                            load_slot(sp, b, i * S + (S + b))

            def pool_program(pool):
                for n in range(S * rounds):
                    if n >= 2:
                        pool.wait_ge(sems["tr"], n - 1)
                        pool.wait_ge(g[n % 2], 16 * (n // 2))
                    nc.gpsimd.indirect_dma_start(out=hg[n % 2][:, :], out_offset=None, in_=k.h_rows,
                                                 in_offset=bass.IndirectOffsetOnAxis(
                                                     ap=r.tok[:, first + n:first + n + 1], axis=0),
                                                 bounds_check=T - 1, oob_is_err=False).then_inc(g[n % 2], 16)

            def tensor_program(pe):
                with pe.Fori(0, rounds) as i:
                    for b in range(S):
                        p = b % 2
                        pe.wait_ge(g[p], i * (8 * S) + 16 * (b // 2 + 1))
                        nc.tensor.matmul(tr_ps[p][:, 0, :], hg[p][:, 0::KT], k.ident[0:CAP, 0:CAP], start=True, stop=True)
                        for j in range(1, KT):
                            last = nc.tensor.transpose(tr_ps[p][:, j, :], hg[p][:, j::KT], k.ident[0:CAP, 0:CAP])
                        last.then_inc(sems["tr"], 1)
                        pe.wait_ge(w_ready[b], i * 48 + 48)
                        pe.wait_ge(sems["he"], i * S + (b + 1))
                        for j in range(KT):
                            for q in range(2):
                                last = nc.tensor.matmul(gu_ps[64 * q:64 * q + 64, :, :], he[p][:, j, :],
                                                        ex.gu[b][:, :, j, q * P:(q + 1) * P],
                                                        start=(j == 0), stop=(j == KT - 1), skip_group_check=True)
                        last.then_inc(sems["gu"], 1)
                        pe.wait_ge(sems["hid"], i * S + (b + 1))
                        nc.tensor.transpose(ht_ps[:, :], hid[:, :], k.ident[:, :]).then_inc(sems["htp"], 1)
                        pe.wait_ge(sems["yo"], i * S + (b + 1))
                        pe.wait_ge(sems["ht"], i * S + (b + 1))
                        for m in range(2):
                            for n in range(2):
                                last = nc.tensor.matmul(y_ps[p][64 * n:64 * n + 64, :], hid_t[:, m * CAP:(m + 1) * CAP],
                                                        ex.dn[b][:, m, n * 512:(n + 1) * 512],
                                                        start=(m == 0), stop=(m == 1), skip_group_check=True)
                        last.then_inc(sems["y"], 1)

            def vector_program(dve):
                with dve.Fori(0, rounds) as i:
                    for b in range(S):
                        dve.wait_ge(sems["tr"], i * S + (b + 1))
                        nc.vector.tensor_copy(he[b % 2][:, :, :], tr_ps[b % 2][:, :, :]).then_inc(sems["he"], 1)
                        dve.wait_ge(sems["sg"], i * S + (b + 1))
                        nc.vector.tensor_tensor(hid[:, :], sg[:, :], gu_ps[:, 1, :], ALU.mult).then_inc(sems["hid"], 1)
                        dve.wait_ge(sems["htp"], i * S + (b + 1))
                        nc.vector.tensor_copy(hid_t[:, :], ht_ps[:, :]).then_inc(sems["ht"], 1)

            def scalar_program(act):
                act.sem_inc(sems["yo"], 1)
                for b in range(2):
                    act.sem_inc(st[b], 32)
                with act.Fori(0, rounds) as i:
                    for b in range(S):
                        p = b % 2
                        act.wait_ge(sems["gu"], i * S + (b + 1))
                        nc.scalar.activation(sg[:, :], gu_ps[:, 0, :], ACT.Silu).then_inc(sems["sg"], 1)
                        act.wait_ge(sems["y"], i * S + (b + 1))
                        act.wait_ge(st[p], i * (16 * S) + 32 * (b // 2 + 1))
                        nc.scalar.activation(yo[p][:, :], y_ps[p][:, :], ACT.Copy).then_inc(sems["yo"], 1)
                        act.wait_ge(sems["yo"], i * S + (b + 2))
                        for n in range(2):
                            act.dma_start(k.y_rows[bass.ds(i * (S * CAP) + (first + b) * CAP, CAP), n * 512:(n + 1) * 512],
                                          yo[p][64 * n:64 * n + 64, :]).then_inc(st[p], 16)
                for b in range(2):
                    act.wait_ge(st[b], 16 * S * rounds + 32)

            return sync_program, tensor_program, vector_program, scalar_program, pool_program

        main = block_programs("a", NE // S, 0, lambda sp, b, n: ex.load(k, sp, b, n, ex.w[b]), True, ex.w)
        rows_clear = k.sem(nm + "rows_clear")
        with nc.Block() as block:
            @block.vector
            def _(dve):
                for b in range(2):
                    nc.vector.memset(hg[b][:, :], 0.0).then_inc(rows_clear, 1)
                main[2](dve)

            @block.sync
            def _(sp):
                main[0](sp)

            @block.tensor
            def _(pe):
                main[1](pe)

            @block.scalar
            def _(act):
                main[3](act)

            @block.gpsimd
            def _(pool):
                pool.wait_ge(rows_clear, 2)
                main[4](pool)

        w_more = [k.sem(f"{nm}w_more{b}") for b in range(S)]

        def load_more(sp, b, n):
            e = sp.value_load(r.more[0:1, bass.ds(n + 1, 1)], min_val=0, max_val=NE - 1)
            ex.load(k, sp, b, e, w_more[b])

        more = block_programs("b", OVB // S, NE, load_more, False, w_more)

        def when_more(eng, program):
            n = eng.value_load(r.more[0:1, 0:1], min_val=0, max_val=OVB)
            with eng.If(n > 0):
                program(eng)

        with nc.Block() as block:
            @block.sync
            def _(sp):
                when_more(sp, more[0])

            @block.tensor
            def _(pe):
                when_more(pe, more[1])

            @block.vector
            def _(dve):
                when_more(dve, more[2])

            @block.scalar
            def _(act):
                when_more(act, more[3])

            @block.gpsimd
            def _(pool):
                when_more(pool, more[4])


def phase_combine(k, layer, r):
    nc = k.nc
    nm = f"co{layer}_"
    sc, sm, tr, ev = (k.sem(nm + n) for n in ("sc", "sm", "tr", "ev"))
    gathered = [k.sem(f"{nm}gathered{t}") for t in range(TT)]
    with ExitStack() as ctx:
        y = k.sb(nm + "y", [P, TT, 2, D], ctx=ctx)
        res = k.sb(nm + "res", [P, KT, T], ctx=ctx)
        ps = k.ps(nm + "ps", [P, KT, P], ctx)
        with nc.Block() as block:
            @block.gpsimd
            def _(pool):
                for t, (a, m) in enumerate(TOK):
                    for i in range(2):
                        nc.gpsimd.indirect_dma_start(out=y[0:m, t, i, :], out_offset=None, in_=k.y_rows,
                                                     in_offset=bass.IndirectOffsetOnAxis(ap=r.slot[0:m, i, t:t + 1],
                                                                                         axis=0),
                                                     bounds_check=NBLK * CAP - 1, oob_is_err=False).then_inc(gathered[t], 16)
                for t in range(TT):
                    pool.wait_ge(gathered[t], 32)

            @block.scalar
            def _(act):
                for t, (a, m) in enumerate(TOK):
                    act.wait_ge(gathered[t], 32)
                    nc.scalar.activation(y[0:m, t, 0, :], y[0:m, t, 0, :], ACT.Copy,
                                         scale=r.weight[0:m, 0, t:t + 1]).then_inc(sc, 1)

            @block.vector
            def _(dve):
                for t, (a, m) in enumerate(TOK):
                    dve.wait_ge(gathered[t], 32)
                    dve.wait_ge(sc, t + 1)
                    nc.vector.scalar_tensor_tensor(out=y[0:m, t, 0, :], in0=y[0:m, t, 1, :],
                                                   scalar=r.weight[0:m, 1, t:t + 1], in1=y[0:m, t, 0, :],
                                                   op0=ALU.mult, op1=ALU.add).then_inc(sm, 1)
                    dve.wait_ge(tr, t + 1)
                    nc.vector.tensor_copy(res[:, :, a:a + m], ps[:, :, 0:m]).then_inc(ev, 1)
                dve.wait_ge(ev, TT)

            @block.tensor
            def _(pe):
                for t, (a, m) in enumerate(TOK):
                    pe.wait_ge(sm, t + 1)
                    if t:
                        pe.wait_ge(ev, t)
                    for j in range(KT):
                        last = nc.tensor.transpose(ps[:, j, 0:m], y[0:m, t, 0, j * P:(j + 1) * P],
                                                   k.ident[0:m, 0:m])
                    last.then_inc(tr, 1)
        phase_residual(k, nm, res, layer * 48 + 5 * KT)


def moe(k, layer):
    with ExitStack() as ctx:
        r = Routing(k, ctx, layer)
        with ExitStack() as c:
            ex = Experts(k, layer, c)
            phase_route(k, layer, r, ex)
            phase_experts(k, layer, r, ex)
        phase_combine(k, layer, r)


def build(nc, io):
    with ExitStack() as ctx:
        k = Trunk(nc, ctx, io)
        k.h_rows = nc.dram_tensor("h_rows", (T, D), F32).ap()
        k.y_rows = nc.dram_tensor("y_rows", (NBLK * CAP, D), F32).ap()
        k.cT = k.sb("cT_sb", [P, KT, 32])
        with ExitStack() as c:
            ada = AdaWeights(k, "ada", [(0, 0)], KT, c)
            phase_constants(k, ada)
            phase_ada(k, ada)
        with ExitStack() as c0:
            mixT = k.sb("mixT", [P, 2 * KT, T], ctx=c0)
            mix_r = k.split_view("mixT", [P, 2 * KT, T])
            h_hi = mix_r
            ca = ExitStack()
            qn = k.sb("qn", [P, KT, NB, NQ], ctx=ca)
            kn = k.sb("kn", [P, KT, NB, NQ], ctx=ca)
            with ExitStack() as c:
                k.qk = k.sb("qk", [P, 2 * KT, T], ctx=c)
                k.qT, k.kT = k.qk[:, 0:KT, :], k.qk[:, KT:2 * KT, :]
                vtok = k.sb("vtok", [P, TT, D], ctx=c)
                with ExitStack() as cw:
                    slots = Slots(k, "qkv", KT, io["mix_w_in"][:, 2576:3600], cw)
                    phase_norm(k, "n0", 0, 0, h_hi, slots)
                    phase_qkv(k, vtok, h_hi, slots)
                with ExitStack() as cw:
                    rest = [(0, 1), (0, 2), (1, 0), (1, 1), (1, 2)]
                    phase_attention_prompt(k, vtok, mixT, qn, kn, AdaWeights(k, "ada_rest", rest, 3, cw))
            with ca:
                phase_attention_sample(k, mixT, qn, kn)
            k.recycle()
            with ExitStack() as c:
                xc = k.sb("xc", [P, XT, T], ctx=c)
                hi_attention = k.split_view("xc", [P, KT, T])
                with ExitStack() as cs:
                    zs = k.sb("zs", [P, KT, T], ctx=cs)
                    dt_tok = k.sb("dt_tok", [P, TT, H], ctx=cs)
                    phase_ssd_project(k, xc, zs, dt_tok, h_hi)
                    phase_ssd(k, xc, mixT, dt_tok)
                    mix_hi = lambda j: k.hT_r[:, j, :] if j < KT else hi_attention[:, j - KT, :]
                    slots = Slots(k, "out0", 2 * KT, io["mix_w_out"], cs)
                    phase_gated_norm(k, zs, mixT, mix_r, mix_hi, slots)
                    phase_out_project(k, "out0", io["mix_w_out"], 2 * KT, mix_hi, lambda j: mix_r[:, j, :], 0, 2, slots)
        k.recycle()
        phase_norm(k, "n1", 0, 3)
        moe(k, 0)
        k.recycle()
        with ExitStack() as c:
            gT = k.sb("gT", [P, KT, T], ctx=c)
            g_lo = k.split_view("gT", [P, KT, T])
            slots = Slots(k, "sc", KT, io["sc_w_in"][:, D:3 * D], c)
            with ExitStack() as c1:
                h_hi = k.sb("h_hi", [P, KT, T], F32R, ctx=c1)
                phase_norm(k, "n2", 1, 0, h_hi, slots)
                phase_short_conv(k, gT, g_lo, h_hi, slots, io["sc_w_out"])
            phase_out_project(k, "out1", io["sc_w_out"], KT, lambda j: k.hT_r[:, j, :], lambda j: g_lo[:, j, :], 1, 2,
                              slots)
        k.recycle()
        phase_norm(k, "n3", 1, 3)
        moe(k, 1)
        phase_norm(k, "n4", None, 0)


def kernel(x_prompt, x_sample, c_prompt, c_sample, state_ssm, state_ssd_conv, cache_k, cache_v, page_table,
           state_short_conv, ada_w, ada_b, ln_mix_g, ln_ffn_g, mix_w_in, mix_w_out, ssd_conv_w, ssd_conv_b,
           ssd_dt_bias, ssd_a_log, ssd_d, ssd_norm_g, sb_bias, sc_w_in, sc_conv_w, sc_w_out, moe_w_group,
           moe_b_group, moe_w_router, moe_b_router, moe_w_gate, moe_w_up, moe_w_down, final_g):
    import numpy as np
    import concourse.bacc as bacc
    from concourse.bass_utils import run_bass_kernel_spmd as run

    def arr(a):
        return np.asarray(a)

    def feature(a):
        a = arr(a)
        a = a.reshape(-1, a.shape[-1] // P, P)
        return a.transpose(2, 0, 1).reshape(P, -1)

    def row(a):
        return np.broadcast_to(arr(a).reshape(1, -1), (P, arr(a).size))

    p = np.arange(P)[:, None]
    before = (np.arange(NQ)[None] < p % NQ).astype(np.float32)
    own_head = (np.arange(8)[None] == p // NQ % 8).astype(np.float32)
    small = np.concatenate([
        feature(ada_b), feature(ln_mix_g), feature(ln_ffn_g), feature(final_g[None]), feature(ssd_conv_w[0]),
        feature(ssd_conv_b), np.repeat(arr(ssd_d)[0], HD).reshape(KT, P).T, feature(ssd_norm_g),
        feature(sc_conv_w[0]), row(ssd_dt_bias), row(ssd_a_log), row(sb_bias),
        row(np.concatenate([arr(moe_b_group), arr(moe_b_router)], axis=1)),
        np.tile(np.repeat(arr(sb_bias).reshape(-1), NQ), 2).reshape(P, 1), before, own_head], axis=1)
    assert small.shape == (P, N_SMALL)
    inputs = {
        "xT": np.concatenate([arr(x_prompt)[0], arr(x_sample).reshape(TS, D)], axis=0).T,
        "cT": np.concatenate([arr(c_prompt), arr(c_sample)], axis=0).T,
        "small": small,
        "ssm_state": arr(state_ssm)[0].transpose(3, 0, 1, 2).reshape(NS, NB, D),
        "conv_state": arr(state_ssd_conv)[0].reshape(NB, 3, XT, P).transpose(3, 2, 0, 1),
        "sc_state": arr(state_short_conv)[0].reshape(NB, 2, KT, P).transpose(3, 2, 0, 1),
        "cache_kT": arr(cache_k)[0].reshape(POOL_PAGES, PAGE, KT, P).transpose(0, 3, 2, 1)[:, :, :, ::-1]
        .reshape(POOL_PAGES, P, D),
        "cache_v": arr(cache_v)[0].reshape(POOL_PAGES, PAGE, D)[:, ::-1],
        "page_table": arr(page_table).reshape(1, NB * PAGES),
        "ada_w": arr(ada_w), "mix_w_in": arr(mix_w_in)[0], "mix_w_out": arr(mix_w_out)[0],
        "sc_w_in": arr(sc_w_in)[0], "sc_w_out": arr(sc_w_out)[0],
        "w_route": np.concatenate([arr(moe_w_group), arr(moe_w_router)], axis=2),
        "moe_w_gate": arr(moe_w_gate), "moe_w_up": arr(moe_w_up), "moe_w_down": arr(moe_w_down),
    }
    inputs = {n: np.ascontiguousarray(a) for n, a in inputs.items()}
    outputs = {"yT": (D, T), "ssm_p": (NS, D), "ssm_s": (NS, NB, D), "conv_out": (P, XT, 3 + TS),
               "kT": (P, KT, T), "v": (T, D), "sc_out": (P, KT, 2 + TS)}
    nc = bacc.Bacc("TRN2", target_bir_lowering=False, num_devices=1)
    io = {n: nc.dram_tensor("in_" + n, a.shape, mybir.dt.from_np(a.dtype), kind="ExternalInput").ap()
          for n, a in inputs.items()}
    io.update({n: nc.dram_tensor("out_" + n, shape, F32, kind="ExternalOutput").ap() for n, shape in outputs.items()})
    build(nc, io)
    r = run(nc, [{"in_" + n: a for n, a in inputs.items()}], core_ids=[0]).results[0]
    r = {n: r["out_" + n] for n in outputs}

    y = r["yT"].T
    conv = r["conv_out"].transpose(2, 1, 0).reshape(3 + TS, XT * P)
    kk = r["kT"].transpose(2, 1, 0).reshape(T, D)
    sc = r["sc_out"].transpose(2, 1, 0).reshape(2 + TS, D)
    c = np.ascontiguousarray
    return (c(y[:TP]).reshape(1, TP, D), c(y[TP:]).reshape(NB, NQ, D),
            c(r["ssm_p"].reshape(NS, H, HD).transpose(1, 2, 0))[None, None],
            c(r["ssm_s"].reshape(NS, NB, H, HD).transpose(1, 2, 3, 0))[None],
            c(conv[:3])[None, None], c(conv[3:].reshape(NB, NQ, XT * P)[:, 1:])[None],
            c(kk[:TP]).reshape(1, 1, TP, H, HD), c(kk[TP:]).reshape(1, NB, NQ, H, HD),
            c(r["v"][:TP]).reshape(1, 1, TP, H, HD), c(r["v"][TP:]).reshape(1, NB, NQ, H, HD),
            c(sc[:2])[None, None], c(sc[2:].reshape(NB, NQ, D)[:, 2:])[None])
```
